# Optimizing a Trainium2 kernel written in Bass

```python
import math
import jax, jax.numpy as jnp
from jax import lax
import numpy as np

D_MODEL = 1024
BATCH = 1
SEQ = 512
DEPTH = 2

GRID_W = 64
CTX_LEN = 256
EPS = 1e-6

N_Q_HEADS = 8
N_KV_HEADS = 2
HEAD_DIM = 64
ATTN_WIDTH = N_Q_HEADS * HEAD_DIM
KV_WIDTH = N_KV_HEADS * HEAD_DIM
WINDOW = 128
BLOCK = 128
ROPE_BASE = 10000.0
ROPE_FREQS = HEAD_DIM // 4

N_SG_GROUPS = 8
SG_GROUP_DIM = 64
SG_WIDTH = N_SG_GROUPS * SG_GROUP_DIM
CHUNK = 128

IN_AB = ATTN_WIDTH + 2 * KV_WIDTH + 2 * SG_WIDTH
SPLITS_AB = [ATTN_WIDTH, ATTN_WIDTH + KV_WIDTH, ATTN_WIDTH + 2 * KV_WIDTH,
             ATTN_WIDTH + 2 * KV_WIDTH + SG_WIDTH]
MIX_AB = ATTN_WIDTH + SG_WIDTH

HYENA_WIDTH = 1024
HYENA_ORDER = 2
SHORT_CONV = 3
FILT_BANDS = 16
FILT_EMB = 1 + 2 * FILT_BANDS
FILT_HIDDEN = 64
FILT_OUT = HYENA_ORDER * 2 * HYENA_WIDTH
DECAY_SHIFT = 0.05

N_EXPERTS = 64
TOP_K = 8
N_GROUPS = 8
TOPK_GROUPS = 4
D_EXPERT = 256
D_SHARED = 256
ROUTED_SCALE = 2.5
MOE_BLOCK = 128

N_EVEN = (DEPTH + 1) // 2
N_ODD = DEPTH // 2

kernel_name = "hybrid_swa_gmlp_hyena_moe_dit"

def rmsnorm(x, g):
    xf = x.astype(jnp.float32)
    y = xf * lax.rsqrt(jnp.mean(jnp.square(xf), axis=-1, keepdims=True) + EPS)
    return (y * g.astype(jnp.float32)).astype(x.dtype)

def axial_rope_tables(rows):
    row = jnp.repeat(jnp.arange(rows, dtype=jnp.float32), GRID_W)
    col = jnp.tile(jnp.arange(GRID_W, dtype=jnp.float32), rows)
    inv = jnp.power(ROPE_BASE, -jnp.arange(ROPE_FREQS, dtype=jnp.float32) / ROPE_FREQS)
    ang = jnp.stack([row[:, None] * inv, col[:, None] * inv], axis=1)
    return jnp.cos(ang), jnp.sin(ang)

def axial_rope(x, cos, sin):
    B, N, H, Dh = x.shape
    xs = x.astype(jnp.float32).reshape(B, N, H, 2, 2, ROPE_FREQS)
    x1, x2 = xs[..., 0, :], xs[..., 1, :]
    cb, sb = cos[None, :, None], sin[None, :, None]
    out = jnp.stack([x1 * cb - x2 * sb, x2 * cb + x1 * sb], axis=-2)
    return out.reshape(B, N, H, Dh).astype(x.dtype)

def window_attention(q, k, v, k_ctx, v_ctx, sink):
    B, L = q.shape[:2]
    C = k_ctx.shape[1]
    nb = L // BLOCK
    G = N_Q_HEADS // N_KV_HEADS
    scale = HEAD_DIM ** -0.5
    qb = q.reshape(B, nb, BLOCK, N_KV_HEADS, G, HEAD_DIM)

    def band(t):
        tp = jnp.pad(t, ((0, 0), (BLOCK, BLOCK), (0, 0), (0, 0)))
        tp = tp.reshape(B, nb + 2, BLOCK, N_KV_HEADS, HEAD_DIM)
        return jnp.concatenate([tp[:, :-2], tp[:, 1:-1], tp[:, 2:]], axis=2)

    kb, vb = band(k), band(v)
    s_loc = jnp.einsum('bnqhgd,bnkhd->bnhgqk', qb, kb).astype(jnp.float32) * scale
    s_ctx = jnp.einsum('bnqhgd,bchd->bnhgqc', qb, k_ctx).astype(jnp.float32) * scale
    blk = jnp.arange(nb)[:, None, None]
    qpos = blk * BLOCK + jnp.arange(BLOCK)[None, :, None]
    kpos = (blk - 1) * BLOCK + jnp.arange(3 * BLOCK)[None, None, :]
    mask = (jnp.abs(qpos - kpos) <= WINDOW) & (kpos >= 0) & (kpos < L)
    s_loc = jnp.where(mask[None, :, None, None], s_loc, -jnp.inf)
    s_sink = jnp.broadcast_to(sink.astype(jnp.float32).reshape(1, 1, N_KV_HEADS, G, 1, 1),
                              s_ctx.shape[:-1] + (1,))
    p = jax.nn.softmax(jnp.concatenate([s_loc, s_ctx, s_sink], axis=-1), axis=-1)
    p_loc = p[..., :3 * BLOCK].astype(v.dtype)
    p_ctx = p[..., 3 * BLOCK:3 * BLOCK + C].astype(v.dtype)
    o = (jnp.einsum('bnhgqk,bnkhd->bnqhgd', p_loc, vb)
         + jnp.einsum('bnhgqc,bchd->bnqhgd', p_ctx, v_ctx))
    return o.reshape(B, L, ATTN_WIDTH)

def context_attention(q, k, v, sink):
    B, C = q.shape[:2]
    G = N_Q_HEADS // N_KV_HEADS
    qg = q.reshape(B, C, N_KV_HEADS, G, HEAD_DIM)
    s = jnp.einsum('bqhgd,bkhd->bhgqk', qg, k).astype(jnp.float32) * HEAD_DIM ** -0.5
    s_sink = jnp.broadcast_to(sink.astype(jnp.float32).reshape(1, N_KV_HEADS, G, 1, 1),
                              s.shape[:-1] + (1,))
    p = jax.nn.softmax(jnp.concatenate([s, s_sink], axis=-1), axis=-1)[..., :C].astype(v.dtype)
    return jnp.einsum('bhgqk,bkhd->bqhgd', p, v).reshape(B, C, ATTN_WIDTH)

def spatial_gating(u, v, w_s, b_s):
    B, N, _ = u.shape
    nc = N // CHUNK
    ug = jax.nn.gelu(u).reshape(B, nc, CHUNK, N_SG_GROUPS, SG_GROUP_DIM)
    vf = jax.nn.gelu(v).astype(jnp.float32).reshape(B, nc, CHUNK, N_SG_GROUPS, SG_GROUP_DIM)
    vc = vf - jnp.mean(vf, axis=-1, keepdims=True)
    vn = (vc * lax.rsqrt(jnp.mean(jnp.square(vc), axis=-1, keepdims=True) + EPS)).astype(u.dtype)
    s = jnp.einsum('gij,bcjgd->bcigd', w_s, vn) + b_s.T[None, None, :, :, None]
    return (ug * s).reshape(B, N, SG_WIDTH)

def mixer_ab(h, hc, cos, sin, w_in, sink, w_s, b_s, w_out, ctx_out):
    B, L, _ = h.shape
    C = hc.shape[1]
    q, k, v, u, g = jnp.split(h @ w_in, SPLITS_AB, axis=-1)
    q = axial_rope(q.reshape(B, L, N_Q_HEADS, HEAD_DIM), cos, sin)
    k = axial_rope(k.reshape(B, L, N_KV_HEADS, HEAD_DIM), cos, sin)
    v = v.reshape(B, L, N_KV_HEADS, HEAD_DIM)
    if ctx_out:
        qc, kc, vc, uc, gc = jnp.split(hc @ w_in, SPLITS_AB, axis=-1)
        qc = qc.reshape(B, C, N_Q_HEADS, HEAD_DIM)
    else:
        kc, vc = jnp.split(hc @ w_in[:, ATTN_WIDTH:ATTN_WIDTH + 2 * KV_WIDTH], 2, axis=-1)
    kc = kc.reshape(B, C, N_KV_HEADS, HEAD_DIM)
    vc = vc.reshape(B, C, N_KV_HEADS, HEAD_DIM)
    y = jnp.concatenate([window_attention(q, k, v, kc, vc, sink),
                         spatial_gating(u, g, w_s, b_s)], axis=-1) @ w_out
    yc = None
    if ctx_out:
        yc = jnp.concatenate([context_attention(qc, kc, vc, sink),
                              spatial_gating(uc, gc, w_s, b_s)], axis=-1) @ w_out
    return y, yc

def short_conv(z, w, b):
    N = z.shape[1]
    pad = SHORT_CONV // 2
    zp = jnp.pad(z, ((0, 0), (pad, pad), (0, 0)))
    return sum(zp[:, j:j + N] * w[j] for j in range(SHORT_CONV)) + b

def hyena_filters(N, w1, b1, w2, b2, w3, freq, delta):
    f32 = jnp.float32
    t = jnp.arange(N, dtype=f32)
    t01 = t / max(N - 1, 1)
    bands = jnp.linspace(1e-4, FILT_BANDS - 1, FILT_BANDS, dtype=f32)
    ang = (2.0 * math.pi / N) * t[:, None] * bands[None, :]
    feats = jnp.concatenate([t01[:, None], jnp.cos(ang), jnp.sin(ang)], axis=-1)
    fr = freq.astype(f32)
    a = jnp.sin(fr * (feats @ w1.astype(f32) + b1.astype(f32)))
    a = jnp.sin(fr * (a @ w2.astype(f32) + b2.astype(f32)))
    hf = a @ w3.astype(f32)
    window = jnp.exp(-t01[:, None] * jnp.abs(delta.astype(f32))[None, :]) + DECAY_SHIFT
    hf = (hf * window).reshape(N, HYENA_ORDER, 2, HYENA_WIDTH)
    h_fwd, h_bwd = hf[:, :, 0], hf[:, :, 1]
    l1 = jnp.sum(jnp.abs(h_fwd), axis=0) + jnp.sum(jnp.abs(h_bwd[1:]), axis=0)
    k_circ = jnp.concatenate([h_fwd, jnp.zeros((1, HYENA_ORDER, HYENA_WIDTH), f32),
                              h_bwd[:0:-1]], axis=0) / l1
    return jnp.fft.rfft(k_circ, axis=0)

def hyena(h, w_in, conv_w, conv_b, w1, b1, w2, b2, w3, freq, delta, f_bias, w_out):
    N = h.shape[1]
    z = short_conv(h @ w_in, conv_w, conv_b)
    v, x1, x2 = jnp.split(z, 3, axis=-1)
    K = hyena_filters(N, w1, b1, w2, b2, w3, freq, delta)
    y = v
    for o, gate in enumerate((x1, x2)):
        Y = jnp.fft.rfft(y.astype(jnp.float32), n=2 * N, axis=1)
        conv = jnp.fft.irfft(Y * K[None, :, o], n=2 * N, axis=1)[:, :N]
        y = gate * (conv.astype(y.dtype) + f_bias[o] * y)
    return y @ w_out

def moe(h, w_router, e_bias, w_gate, w_up, w_down, ws_gate, ws_up, ws_down):
    T, D = h.shape
    scores = jax.nn.sigmoid((h @ w_router).astype(jnp.float32))
    biased = scores + e_bias.astype(jnp.float32)
    grp = biased.reshape(T, N_GROUPS, N_EXPERTS // N_GROUPS)
    grp_score = jnp.sum(lax.top_k(grp, 2)[0], axis=-1)
    _, gidx = lax.top_k(grp_score, TOPK_GROUPS)
    gmask = jnp.sum(jax.nn.one_hot(gidx, N_GROUPS), axis=1) > 0
    emask = jnp.repeat(gmask, N_EXPERTS // N_GROUPS, axis=1)
    _, eidx = lax.top_k(jnp.where(emask, biased, -jnp.inf), TOP_K)
    wts = jnp.take_along_axis(scores, eidx, axis=1)
    wts = wts / jnp.sum(wts, axis=-1, keepdims=True) * ROUTED_SCALE

    n_pairs = T * TOP_K
    e_flat = eidx.reshape(-1)
    tok_flat = jnp.arange(n_pairs, dtype=jnp.int32) // TOP_K
    order = jnp.argsort(e_flat)
    e_s, tok_s, w_s = e_flat[order], tok_flat[order], wts.reshape(-1)[order]
    counts = jnp.bincount(e_flat, length=N_EXPERTS)
    starts = jnp.cumsum(counts) - counts
    pcounts = (counts + MOE_BLOCK - 1) // MOE_BLOCK * MOE_BLOCK
    pends = jnp.cumsum(pcounts)
    pstarts = pends - pcounts
    dest = pstarts[e_s] + jnp.arange(n_pairs) - starts[e_s]
    n_blocks = -(-n_pairs // MOE_BLOCK) + N_EXPERTS
    n_slots = n_blocks * MOE_BLOCK
    slot_tok = jnp.zeros((n_slots,), jnp.int32).at[dest].set(tok_s)
    slot_w = jnp.zeros((n_slots,), jnp.float32).at[dest].set(w_s)
    blk_e = jnp.minimum(jnp.searchsorted(pends, jnp.arange(n_blocks) * MOE_BLOCK, side='right'),
                        N_EXPERTS - 1)

    def expert_block(args):
        tok, wt, e = args
        xb = h[tok]
        a = jax.nn.silu(xb @ w_gate[e]) * (xb @ w_up[e])
        return (a @ w_down[e]) * wt[:, None].astype(h.dtype)

    out = lax.map(expert_block, (slot_tok.reshape(n_blocks, MOE_BLOCK),
                                 slot_w.reshape(n_blocks, MOE_BLOCK), blk_e))
    routed = jax.ops.segment_sum(out.reshape(n_slots, D), slot_tok, num_segments=T)
    shared = (jax.nn.silu(h @ ws_gate) * (h @ ws_up)) @ ws_down
    return shared + routed

def setup_inputs(seed: int = 0) -> dict:
    key = jax.random.key(seed)
    ks = iter(jax.random.split(key, 40))
    f32 = jnp.float32

    def nrm(shape, scale):
        return jax.random.normal(next(ks), shape, f32) * scale

    D = D_MODEL
    decay = jnp.tile(jnp.linspace(math.log(1e-2) / 1.5, math.log(1e-2) / 0.3, HYENA_WIDTH,
                                  dtype=f32), HYENA_ORDER * 2)
    return {
        "x": nrm((BATCH, SEQ, D), 1.0),
        "c": nrm((BATCH, D), 1.0),
        "ctx": nrm((BATCH, CTX_LEN, D), 1.0),
        "c_ctx": nrm((D,), 1.0),
        "w_mod": nrm((DEPTH, D, 6 * D), 0.5 * D ** -0.5),
        "b_mod": nrm((DEPTH, 6 * D), 0.02),
        "norm_g": 1.0 + nrm((DEPTH, 2, D), 0.05),
        "w_in_ab": nrm((N_EVEN, D, IN_AB), D ** -0.5),
        "sink": nrm((N_EVEN, N_Q_HEADS), 0.5),
        "w_spatial": nrm((N_EVEN, N_SG_GROUPS, CHUNK, CHUNK), CHUNK ** -0.5),
        "b_spatial": 1.0 + nrm((N_EVEN, N_SG_GROUPS, CHUNK), 0.05),
        "w_out_ab": nrm((N_EVEN, MIX_AB, D), MIX_AB ** -0.5),
        "w_in_c": nrm((N_ODD, D, 3 * HYENA_WIDTH), D ** -0.5),
        "conv_w": nrm((N_ODD, SHORT_CONV, 3 * HYENA_WIDTH), SHORT_CONV ** -0.5),
        "conv_b": nrm((N_ODD, 3 * HYENA_WIDTH), 0.02),
        "filt_w1": nrm((N_ODD, FILT_EMB, FILT_HIDDEN), 1.0),
        "filt_b1": nrm((N_ODD, FILT_HIDDEN), 0.1),
        "filt_w2": nrm((N_ODD, FILT_HIDDEN, FILT_HIDDEN), FILT_HIDDEN ** -0.5),
        "filt_b2": nrm((N_ODD, FILT_HIDDEN), 0.1),
        "filt_w3": nrm((N_ODD, FILT_HIDDEN, FILT_OUT), FILT_HIDDEN ** -0.5),
        "filt_freq": 1.0 + nrm((N_ODD, FILT_HIDDEN), 0.1),
        "filt_delta": decay[None, :] * (1.0 + nrm((N_ODD, FILT_OUT), 0.05)),
        "filt_bias": nrm((N_ODD, HYENA_ORDER, HYENA_WIDTH), 0.5),
        "w_out_c": nrm((N_ODD, HYENA_WIDTH, D), HYENA_WIDTH ** -0.5),
        "w_router": nrm((DEPTH, D, N_EXPERTS), D ** -0.5),
        "e_bias": nrm((DEPTH, N_EXPERTS), 0.01),
        "w_gate": nrm((DEPTH, N_EXPERTS, D, D_EXPERT), D ** -0.5),
        "w_up": nrm((DEPTH, N_EXPERTS, D, D_EXPERT), D ** -0.5),
        "w_down": nrm((DEPTH, N_EXPERTS, D_EXPERT, D), D_EXPERT ** -0.5),
        "ws_gate": nrm((DEPTH, D, D_SHARED), D ** -0.5),
        "ws_up": nrm((DEPTH, D, D_SHARED), D ** -0.5),
        "ws_down": nrm((DEPTH, D_SHARED, D), D_SHARED ** -0.5),
        "final_g": 1.0 + nrm((D,), 0.05),
    }

def reference(x, c, ctx, c_ctx, w_mod, b_mod, norm_g, w_in_ab, sink, w_spatial, b_spatial,
              w_out_ab, w_in_c, conv_w, conv_b, filt_w1, filt_b1, filt_w2, filt_b2, filt_w3,
              filt_freq, filt_delta, filt_bias, w_out_c, w_router, e_bias, w_gate, w_up, w_down,
              ws_gate, ws_up, ws_down, final_g):
    B, L, D = x.shape
    C = ctx.shape[1]
    rows = L // GRID_W
    cos, sin = axial_rope_tables(rows)
    x_ctx = ctx
    for i in range(DEPTH):
        j = i // 2
        ctx_read = (i % 2 == 0)
        ctx_next = any(l % 2 == 0 for l in range(i + 1, DEPTH))
        m = jax.nn.silu(c) @ w_mod[i] + b_mod[i]
        sh1, sc1, g1, sh2, sc2, g2 = [t[:, None, :] for t in jnp.split(m, 6, axis=-1)]
        h = rmsnorm(x, norm_g[i, 0]) * (1.0 + sc1) + sh1
        hc = None
        if ctx_read or ctx_next:
            mc = jax.nn.silu(c_ctx) @ w_mod[i] + b_mod[i]
            csh1, csc1, cg1, csh2, csc2, cg2 = jnp.split(mc, 6)
            hc = rmsnorm(x_ctx, norm_g[i, 0]) * (1.0 + csc1) + csh1
        if i % 2 == 0:
            y, yc = mixer_ab(h, hc, cos, sin, w_in_ab[j], sink[j], w_spatial[j], b_spatial[j],
                             w_out_ab[j], ctx_next)
        else:
            hy = (w_in_c[j], conv_w[j], conv_b[j], filt_w1[j], filt_b1[j], filt_w2[j], filt_b2[j],
                  filt_w3[j], filt_freq[j], filt_delta[j], filt_bias[j], w_out_c[j])
            y = hyena(h, *hy)
            yc = hyena(hc, *hy) if ctx_next else None
        x = x + g1 * y
        h2 = rmsnorm(x, norm_g[i, 1]) * (1.0 + sc2) + sh2
        moe_p = (w_router[i], e_bias[i], w_gate[i], w_up[i], w_down[i],
                 ws_gate[i], ws_up[i], ws_down[i])
        if ctx_next:
            x_ctx = x_ctx + cg1 * yc
            hc2 = rmsnorm(x_ctx, norm_g[i, 1]) * (1.0 + csc2) + csh2
            out = moe(jnp.concatenate([h2.reshape(B * L, D), hc2.reshape(B * C, D)], axis=0), *moe_p)
            x = x + g2 * out[:B * L].reshape(B, L, D)
            x_ctx = x_ctx + cg2 * out[B * L:].reshape(B, C, D)
        else:
            x = x + g2 * moe(h2.reshape(B * L, D), *moe_p).reshape(B, L, D)
    return rmsnorm(x, final_g)


_drawn_inputs = setup_inputs


def setup_inputs(seed=0):
    import zlib

    import numpy as np

    out = dict(_drawn_inputs(seed))
    spreads = {}
    factors = {'sink': 51.113,
     'conv_b': 6.095,
     'filt_b1': 6.672,
     'filt_b2': 3.955,
     'filt_freq': 3.333,
     'filt_delta': 21.106}
    for name, (base, spread) in spreads.items():
        noise = np.random.default_rng([zlib.crc32(name.encode()), seed]).standard_normal(out[name].shape)
        drawn = base * np.exp(spread * noise) if base else spread * noise
        out[name] = __import__('jax').numpy.asarray(drawn.astype(out[name].dtype))
    for name, factor in factors.items():
        out[name] = (out[name] * factor).astype(out[name].dtype)
    return out
```

```python
import math
from contextlib import ExitStack

import numpy as np

import concourse.bass as bass
from concourse import mybir

F32 = mybir.dt.float32
BF16 = mybir.dt.bfloat16
I32 = mybir.dt.int32
ALU = mybir.AluOpType
ACT = mybir.ActivationFunctionType
AX = mybir.AxisListType.X

P = 128
D = 1024
T = 512
CTX = 256
GRID_W = 64
KD = D // P
NT = T // P
NC = CTX // P
BANK = 512
EPS = 1e-6

N_Q, N_KV, HD = 8, 2, 64
ROPE_F = HD // 4
WINDOW = 128
ATT_W = N_Q * HD
SG_G, SG_D = 8, 64
BIG = 1.0e30

HY_Q = 4
CH = D // HY_Q
FILT_EMB, FILT_HID, BANDS = 33, 64, 16
DECAY_SHIFT = 0.05

E = 64
TOP_K = 8
GROUPS = 8
TOPK_GROUPS = 4
FE = 256
ROUTED_SCALE = 2.5
OVER = T * TOP_K // P
NBLK = E + OVER
FEW = 8
CG = 6

C_ID, C_IOTA, C_TRI, C_LT, C_E128, C_T01, C_TID, C_END = 0, 128, 256, 384, 448, 512, 516, 524
R_MASK, R_COS, R_SIN, R_END = 0, 384, 640, 896


def constants():
    small = np.zeros((P, C_END), np.float32)
    p = np.arange(P)
    small[:, C_ID:C_ID + P] = np.eye(P)
    small[:, C_IOTA:C_IOTA + P] = p[None, :]
    small[:, C_TRI:C_TRI + P] = p[:, None] < p[None, :]
    g = np.arange(GROUPS)
    small[:, C_LT:C_LT + 64] = (g[None, :] < g[:, None]).reshape(1, 64)
    small[:, C_E128:C_E128 + E] = 128.0 * np.arange(E)[None, :]
    t = np.arange(T, dtype=np.float32).reshape(NT, P).T
    small[:, C_T01:C_T01 + NT] = -(t / np.float32(T - 1))
    small[:, C_TID:C_TID + 8:2] = p[:, None]
    small[:, C_TID + 1:C_TID + 8:2] = 128.0 * np.arange(NT)[None, :]

    rope = np.zeros((P, R_END), np.float32)
    q, j = np.arange(P)[:, None], np.arange(3 * P)[None, :] - P
    rope[:, R_MASK:R_MASK + 3 * P] = np.where(np.abs(q - j) <= WINDOW, 0.0, -BIG)
    inv = np.power(10000.0, -np.arange(ROPE_F, dtype=np.float32) / ROPE_F).astype(np.float32)
    tok = np.arange(T)
    for axis, pos in enumerate((tok // GRID_W, tok % GRID_W)):
        ang = (pos.astype(np.float32)[:, None] * inv).astype(np.float32)
        cos, sin = np.cos(ang).astype(np.float32), np.sin(ang).astype(np.float32)
        for m in range(NT):
            rows = slice(m * P, (m + 1) * P)
            c0, s0 = R_COS + m * HD + axis * 32, R_SIN + m * HD + axis * 32
            rope[:, c0:c0 + 16], rope[:, c0 + 16:c0 + 32] = cos[rows], cos[rows]
            rope[:, s0:s0 + 16], rope[:, s0 + 16:s0 + 32] = -sin[rows], sin[rows]

    n = np.arange(T, dtype=np.float32)
    bands = np.linspace(1e-4, BANDS - 1, BANDS, dtype=np.float32)
    ang = np.float32(2.0 * math.pi / T) * n[:, None] * bands[None, :]
    feats = np.concatenate([(n / np.float32(T - 1))[:, None], np.cos(ang), np.sin(ang)], 1).T
    th = np.outer(np.arange(T), np.arange(T) + 0.5) * (math.pi / T)
    c, s = np.cos(th), np.sin(th)
    dft = np.stack([c, s, c.T / T, s.T / T]).astype(np.float32).reshape(4, NT, P, T)
    return {"c_small": small, "c_rope": rope, "c_feats": np.ascontiguousarray(feats, np.float32),
            "c_dft": np.ascontiguousarray(dft.transpose(2, 0, 1, 3))}


class Chain:

    def __init__(self, eng, sem):
        self.eng, self.sem, self.n, self.off = eng, sem, 0, 0

    def __call__(self, ins):
        ins.then_inc(self.sem, 1)
        self.n += 1

    def sync(self):
        self.eng.wait_ge(self.sem, self.off + self.n)

    def enter(self, i, stride):
        self.start, self.off, self.stride = self.n, i * stride, stride

    def leave(self, count):
        assert self.n - self.start == self.stride, self.n - self.start
        self.n, self.off = self.start + count * self.stride, 0


def hybrid_backbone(nc, x, c, ctx, c_ctx, w_mod, b_mod, norm_g, w_in_ab, sink, w_spatial, b_spatial,
                    w_out_ab, w_in_c, conv_w, conv_b, filt_w1, filt_b1, filt_w2, filt_b2, filt_w3,
                    filt_freq, filt_delta, filt_bias, w_out_c, w_router, e_bias, w_gate, w_up, w_down,
                    ws_gate, ws_up, ws_down, final_g, c_small, c_rope, c_feats, c_dft, out):
    h2_dram = [nc.dram_tensor(f"h2_rows_{l}", [T, D], F32, kind="Internal").ap() for l in range(2)]
    mod_dram = nc.dram_tensor("modulation_1", [1, 6 * D], F32, kind="Internal").ap()
    y_dram = nc.dram_tensor("expert_rows", [NBLK * P, D], F32, kind="Internal").ap()

    ctxs = ExitStack()
    with ctxs:
        def sb(name, shape, dt=F32):
            return ctxs.enter_context(nc.sbuf_tensor(name, shape, dt))

        sems = {}

        def sem(name):
            return sems[name]

        def wait(eng, name, value):
            if not (isinstance(value, int) and value <= 0):
                eng.wait_ge(sem(name), value)

        def make(*names):
            for n in names:
                sems[n] = ctxs.enter_context(nc.semaphore(n))

        X = sb("residual", [P, NT, D])
        MODR = sb("modulation_rows", [P, 6 * D])
        HT = sb("features_major", [P, KD, T])
        H = sb("token_major", [P, NT, D])
        arena = sb("arena", [P, 128 * 256])
        K = sb("constants", [P, C_END])
        ones = sb("ones", [P, P])
        tid = sb("token_ids", [P, 8], BF16)
        ss = sb("square_sums", [P, 16])
        sm = sb("small_columns", [P, 640])
        ps = ctxs.enter_context(nc.psum_tensor("ps", [P, 8, BANK], F32))

        def A(kb, n, parts=P):
            return arena[0:parts, int(kb * 256):int(kb * 256) + n]

        def A3(kb, a, b, parts=P):
            return A(kb, a * b, parts).rearrange("p (a b) -> p a b", a=a)

        ident = K[:, C_ID:C_ID + P]

        SLOTS = 3
        dense = []

        def rows8(w, lo, n):
            return w.rearrange("(p k) n -> p k n", k=KD)[:, :, lo:lo + n]

        def add(*parts):
            dense.append(parts)
            return len(dense) - 1

        def slot(n, k, w, at=0):
            base = (n % SLOTS) * 16
            return A3(base, k, w) if at == 0 else None

        W_MOD = [[], []]
        for n in range(12):
            W_MOD[0].append(add((0, KD, 512, rows8(w_mod[0], n * 512, 512), 0, 512)))
        W_KV = add((0, KD, 512, rows8(w_in_ab[0], 512, 256), 0, 256))
        W_Q = add((0, KD, 512, rows8(w_in_ab[0], 0, 512), 0, 512))
        W_G = add((0, KD, 512, rows8(w_in_ab[0], 1280, 512), 0, 512))
        W_U = add((0, KD, 512, rows8(w_in_ab[0], 768, 512), 0, 512))
        W_OUT = [[], []]
        W_SH = [None, None]
        for n in range(12):
            W_MOD[1].append(add((0, KD, 512, rows8(w_mod[1], n * 512, 512), 0, 512)))
        for n in range(2):
            W_OUT[0].append(add((0, KD, 512, rows8(w_out_ab[0], n * 512, 512), 0, 512)))

        def add_shared(l):
            a = add((0, KD, 512, rows8(ws_gate[l], 0, FE), 0, FE), (0, KD, 512, rows8(ws_up[l], 0, FE), FE, 2 * FE))
            b = add((0, 2, D, ws_down[l].rearrange("(p k) n -> p k n", k=2), 0, D))
            W_SH[l] = (a, b)

        add_shared(0)
        for n in range(2):
            W_OUT[1].append(add((0, KD, 512, w_out_c[0].rearrange("(k p) n -> p k n", p=P)[:, :, n * 512:(n + 1) * 512], 0, 512)))
        add_shared(1)
        landed = []
        total = [0] * SLOTS
        for n, parts in enumerate(dense):
            total[n % SLOTS] += 16 * len(parts)
            landed.append(total[n % SLOTS])

        make("x_in", "consts_in", "bmod_in", "norm_row_in", "consts_made", "dense_used",
             "silu_c", "cond_cols", "dve_chain", "act_chain", "h2_stored", "layer_start")
        for s in range(SLOTS):
            make(f"dense_landed_{s}")
        make("mod_mm", "mod_add", "mod_stored")
        NORMS = ["n1_0", "nc_0", "n2_0", "n1_1", "n2_1", "fin"]
        make("sq", "ms", "rt", "h", "tp", "turned")
        tiles_of = dict(zip(NORMS, (NT, NC, NT, NT, NT, NT)))
        before = {n: sum(tiles_of[m] for m in NORMS[:i]) for i, n in enumerate(NORMS)}
        make("row_used", "tables_in", "ws_in", "kv_mm", "kv_act", "kv_dve", "q_mm", "q_dve",
             "gu_mm", "gu_act", "qk_tp", "qk_ev", "ws_tp", "ws_ev", "sg_ln", "sg_sq", "sg_ms", "sg_rt", "sg_mm", "sg_done",
             "s_mm", "s_dve", "s_act", "s_max", "p_act", "pt_mm", "pt_out", "o_mm", "o_dve",
             "mt_tp", "mt_turned", "yo_mm", "yo_dve")
        for l in range(2):
            make(*[f"{n}_{l}" for n in (
                "wgu0", "wgu1", "wd0", "wd1", "oh", "tok_mm", "tok", "xg0", "xg1", "xt_mm", "xt_out", "gu_m",
                "silu", "a", "at_mm", "at", "y_mm", "y_out", "yst0", "yst1", "next_range")])
        make("lg_mm", "score", "eb_in", "sel", "pos_mm", "slots", "tables", "shgu_mm", "shsilu", "sha", "shat_mm", "shat",
             "shy_mm", "shy_act", "shy_dve", "cadd", "moe_done")
        make(*[f"cg{b}" for b in range(CG)])
        make("out_stored", "rows_asked", "over_stored_0", "over_stored_1", "zero_ready", "zeroed")
        for n in ("hy_in", "cols_tp", "cols_ev", "f_mm", "f_arg", "f_sin", "wz_in", "wf_in", "dft_in",
                  "z_mm", "z_act", "z_dve", "yt_mm", "yt_act", "yt_dup", "win", "hf_mm", "hfw", "l1sum", "l1_mm", "rl1", "sd",
                  "ky_mm", "ky_act", "pp", "iv_mm", "iv_act", "yn"):
            make(n)

        block = ctxs.enter_context(nc.Block())

        cbc = A3(48, KD, P)
        ccbc = A3(52, KD, P)
        MODC = A(56, 2 * D)
        CX = A3(64, NC, D)
        HC = A3(72, NC, D)
        HCT = A3(80, KD, CTX)
        GROW = A(88, D)
        tmpn = [A(92, D), A(96, D)]
        RP = A(100, R_END)
        Q = A3(104, NT, ATT_W)
        VG = A3(112, NT, 512)
        UG = A3(120, NT, 512)
        V = A3(48, NT, P)
        VC = A3(50, NC, P)
        KDUP = A3(52, NT, 2 * P)
        KCDUP = A3(62, NC, 2 * P)
        QT = A3(64, 4, T)
        KT = A3(72, 2, T)
        KCT = A3(76, 2, CTX)
        SS = [A(80, 640), A(82.5, 640)]
        PB = [A(85, 640), A(87.5, 640)]
        PT = [A(56, 640), A(58.5, 640)]
        WST = A3(92, SG_G, P)
        WSR = A3(96, SG_G, P)
        SGT = MODR[:, 0:2048]
        MIX = H
        ZERO = HT[:, 0:2, :].rearrange("p k t -> p (k t)")
        BROW = A(104, 6 * D, 1)
        ccol = sm[:, 0:16]
        sinkb = sm[:, 16:24]
        bsr = sm[0:SG_G, 24:152]
        bsc = sm[:, 152:160]
        acol = sm[:, 160:192]
        mxc = sm[:, 192:224]
        nmc = sm[:, 224:256]
        rsc = sm[:, 256:288]
        esc = sm[:, 288:320]
        dnc = sm[:, 320:352]
        rcc = sm[:, 352:384]
        sgm = sm[:, 384:416]
        sgv = sm[:, 416:448]

        def sp_setup(sp):
            sp.dma_start(ccol[:, 0:8], c.rearrange("a (p k) -> p (a k)", k=KD)).then_inc(sem("consts_in"), 16)
            sp.dma_start(ccol[:, 8:16], c_ctx.rearrange("(p k) -> p k", k=KD)).then_inc(sem("consts_in"), 16)
            sp.dma_start(K[:, :], c_small).then_inc(sem("consts_in"), 16)
            for n in range(3):
                sp_dense(sp, n)
            sp.dma_start(MODR[:, :], b_mod[0:1, :].to_broadcast([P, 6 * D])).then_inc(sem("bmod_in"), 16)
            sp.dma_start(MODC, b_mod[0:1, 0:2 * D].to_broadcast([P, 2 * D])).then_inc(sem("bmod_in"), 16)

        def sp_layer0(sp):
            sp.dma_start(X[:, :, :], x[0].rearrange("(m p) d -> p m d", p=P)).then_inc(sem("x_in"), 16)
            sp.dma_start(CX, ctx[0].rearrange("(m p) d -> p m d", p=P)).then_inc(sem("x_in"), 16)
            sp.dma_start(GROW, norm_g[0, 0:1, :].to_broadcast([P, D])).then_inc(sem("norm_row_in"), 16)
            sp.dma_start(RP, c_rope).then_inc(sem("tables_in"), 16)
            sp.dma_start(sinkb, sink.to_broadcast([P, N_Q])).then_inc(sem("tables_in"), 16)
            sp.dma_start(bsr, b_spatial[0]).then_inc(sem("tables_in"), 16)

        def sp_zero_rows(sp):
            sp.wait_ge(sem("zero_ready"), 1)
            sp.dma_start(y_dram[E * P:NBLK * P, :].rearrange("(b s) d -> s b d", s=P),
                         ZERO.unsqueeze(1).to_broadcast([P, OVER, D])).then_inc(sem("zeroed"), 16)

        def sp_dense(sp, n):
            if n >= SLOTS:
                sp.wait_ge(sem("dense_used"), n - SLOTS + 1)
            for (_, k, w, src, lo, hi) in dense[n]:
                base = (n % SLOTS) * 16
                if hi <= 1:
                    dst = A3(base, k, w, FILT_HID)[:, lo, :]
                else:
                    dst = A3(base, k, w)[:, :, lo:hi]
                sp.dma_start(dst, src).then_inc(sem(f"dense_landed_{n % SLOTS}"), 16)

        def W(n, k, w, parts=P):
            return A3((n % SLOTS) * 16, k, w, parts)

        def w_wait(pe, n):
            pe.wait_ge(sem(f"dense_landed_{n % SLOTS}"), landed[n])

        def act_setup(act, a):
            act.wait_ge(sem("consts_in"), 48)
            act.activation(sm[:, 0:16], sm[:, 0:16], ACT.Silu).then_inc(sem("silu_c"), 1)

        def dve_setup(dve, v):
            dve.memset(ones[:, :], 1.0).then_inc(sem("consts_made"), 1)
            dve.wait_ge(sem("consts_in"), 48)
            dve.tensor_copy(tid[:, :], K[:, C_TID:C_TID + 8]).then_inc(sem("consts_made"), 1)

        def dve_cond(dve, v):
            dve.wait_ge(sem("silu_c"), 1)
            for i, dst in enumerate((cbc, ccbc)):
                dve.tensor_copy(dst, ccol[:, 8 * i:8 * i + 8].unsqueeze(2).to_broadcast([P, KD, P])) \
                    .then_inc(sem("cond_cols"), 1)

        def pe_mod(pe):
            pe.wait_ge(sem("cond_cols"), 2)
            t = 0
            for n in range(12):
                w_wait(pe, W_MOD[0][n])
                w = W(W_MOD[0][n], KD, 512)
                for s in [cbc, ccbc] if n < 4 else [cbc]:
                    if t >= 8:
                        pe.wait_ge(sem("mod_add"), t - 7)
                    for k in range(KD):
                        mm = pe.matmul(ps[:, t % 8, :], s[:, k, :], w[:, k, :], start=k == 0, stop=k == KD - 1)
                    mm.then_inc(sem("mod_mm"), 1)
                    t += 1
                used(pe, "mod_mm", t)

        def pe_mod_1(pe, step):
            n, k = step // KD, step % KD
            if k == 0:
                w_wait(pe, W_MOD[1][n])
                pe.wait_ge(sem("mod_add"), 16 + n)
            mm = pe.matmul(ps[0:1, 7, :], ccol[:, k:k + 1], W(W_MOD[1][n], KD, 512)[:, k, :],
                           start=k == 0, stop=k == KD - 1)
            if k == KD - 1:
                mm.then_inc(sem("mod_mm"), 1)
                used(pe, "mod_mm", 16 + n + 1)

        def dve_mod_1(dve, n):
            if n == 0:
                dve.wait_ge(sem("bmod_in"), 48)
            dve.wait_ge(sem("mod_mm"), 16 + n + 1)
            d = BROW[:, n * 512:(n + 1) * 512]
            dve.tensor_tensor(d, ps[0:1, 7, :], d, ALU.add).then_inc(sem("mod_add"), 1)

        def used(pe, name, value):
            pe.wait_ge(sem(name), value)
            pe.sem_inc(sem("dense_used"), 1)

        def dve_mod(dve, v):
            dve.wait_ge(sem("bmod_in"), 32)
            t = 0
            for n in range(12):
                for dst in ([MODR, MODC] if n < 4 else [MODR]):
                    dve.wait_ge(sem("mod_mm"), t + 1)
                    d = dst[:, n * 512:(n + 1) * 512]
                    dve.tensor_tensor(d, ps[:, t % 8, :], d, ALU.add).then_inc(sem("mod_add"), 1)
                    t += 1
            dve.wait_ge(sem("mod_add"), t)

        def act_norm_sq(act, a, n, src, nt, junk):
            for m in range(nt):
                if m >= 2 or n == "nc_0":
                    act.wait_ge(sem("sq"), before[n] + m - 1)
                if n in ("n1_1", "fin"):
                    act.wait_ge(sem("layer_start"), NT * (1 + (n == "fin")) - NT + m + 1)
                act.activation(junk[m % 2], src[:, m, :], ACT.Square, accum_out=ss[:, m:m + 1]) \
                    .then_inc(sem("sq"), 1)
            act.wait_ge(sem("ms"), NORMS.index(n) + 1)
            act.activation(ss[:, 8:8 + nt], ss[:, 4:4 + nt], ACT.Sqrt).then_inc(sem("rt"), 1)

        def dve_norm(dve, v, n, src, nt, rowA, rowB, dst, grow, tmp, final=None):
            dve.wait_ge(sem("sq"), before[n] + nt)
            dve.tensor_scalar(ss[:, 4:4 + nt], ss[:, 0:nt], 1.0 / D, EPS, ALU.mult, ALU.add).then_inc(sem("ms"), 1)
            if rowA is not None:
                dve.scalar_tensor_tensor(rowA, rowA, 1.0, grow, ALU.add, ALU.mult).then_inc(sem("row_used"), 1)
            dve.wait_ge(sem("rt"), NORMS.index(n) + 1)
            v(dve.reciprocal(ss[:, 12:12 + nt], ss[:, 8:8 + nt]))
            v.sync()
            if rowA is not None:
                dve.wait_ge(sem("row_used"), NORMS.index(n) + 1)
            for m in range(nt):
                r = ss[:, 12 + m:13 + m]
                if rowA is None:
                    dve.scalar_tensor_tensor(dst[:, m, :], src[:, m, :], r, grow, ALU.mult, ALU.mult) \
                        .then_inc(sem("h"), 1)
                    continue
                v(dve.scalar_tensor_tensor(tmp[m % 2], src[:, m, :], r, rowA, ALU.mult, ALU.mult))
                v.sync()
                dve.tensor_tensor(dst[:, m, :].rearrange("p (k j) -> p j k", k=KD),
                                  tmp[m % 2].rearrange("p (j k) -> p j k", k=KD),
                                  rowB.rearrange("p (j k) -> p j k", k=KD), ALU.add).then_inc(sem("h"), 1)

        def pe_turn(pe, src, dst_sem, nt, strided=False, norm=None):
            for m in range(nt):
                if norm is not None:
                    pe.wait_ge(sem("h"), before[norm] + m + 1)
                for kk in range(2):
                    for j in range(4):
                        k = 4 * kk + j
                        s = src[:, m, k:k + 8 * (P - 1) + 1:8] if strided else src[:, m, k * P:(k + 1) * P]
                        mm = pe.transpose(ps[:, 2 * m + kk, j * P:(j + 1) * P], s, ident)
                    mm.then_inc(sem(dst_sem), 1)

        def turned(eng, copy, dst, dst_sem, done, nt, kk, norm=None):
            for m in range(nt):
                eng.wait_ge(sem(dst_sem), 2 * ((before[norm] if norm else 0) + m) + kk + 1)
                copy(dst[:, 4 * kk:4 * kk + 4, m * P:(m + 1) * P],
                     ps[:, 2 * m + kk, :].rearrange("p (k t) -> p k t", k=4)).then_inc(sem(done), 1)

        def pe_project(pe):
            w_wait(pe, W_KV)
            pe.wait_ge(sem("turned"), 2 * before["n2_0"])
            w = W(W_KV, KD, 512)
            for t in range(NT + NC):
                src = HT[:, :, t * P:(t + 1) * P] if t < NT else HCT[:, :, (t - NT) * P:(t - NT + 1) * P]
                for k in range(KD):
                    mm = pe.matmul(ps[:, t, 0:256], src[:, k, :], w[:, k, 0:256], start=k == 0, stop=k == KD - 1)
                mm.then_inc(sem("kv_mm"), 1)
            used(pe, "kv_mm", NT + NC)
            t = 0
            for n, name in ((W_Q, "q_mm"), (W_G, "gu_mm"), (W_U, "gu_mm")):
                w_wait(pe, n)
                w = W(n, KD, 512)
                for m in range(NT):
                    bank = (6 + t) % 8
                    if bank < 6 and t < 8:
                        pe.wait_ge(sem("kv_act"), bank + 1)
                        pe.wait_ge(sem("kv_dve"), bank + 1)
                    if t >= 8:
                        pe.wait_ge(sem("q_dve"), t - 7)
                    for k in range(KD):
                        mm = pe.matmul(ps[:, bank, :], HT[:, k, m * P:(m + 1) * P], w[:, k, :],
                                       start=k == 0, stop=k == KD - 1)
                    mm.then_inc(sem(name), 1)
                    t += 1
                used(pe, name, NT if name == "q_mm" or n == W_G else 2 * NT)

        def act_project(act, a):
            for t in range(NT + NC):
                act.wait_ge(sem("kv_mm"), t + 1)
                dst = V[:, t, :] if t < NT else VC[:, t - NT, :]
                act.activation(dst, ps[:, t, P:2 * P], ACT.Copy).then_inc(sem("kv_act"), 1)
            for i in range(2 * NT):
                act.wait_ge(sem("gu_mm"), i + 1)
                dst = VG[:, i, :] if i < NT else UG[:, i - NT, :]
                act.activation(dst, ps[:, (6 + NT + i) % 8, :], ACT.Gelu_apprx_tanh).then_inc(sem("gu_act"), 1)

        def rotate(dve, v, src, nh, m, outs):
            cos = RP[:, R_COS + m * HD:R_COS + (m + 1) * HD]
            sin = RP[:, R_SIN + m * HD:R_SIN + (m + 1) * HD]
            t1, t2 = SGT[:, 0:nh * HD], SGT[:, 512:512 + nh * HD]
            v.sync()
            v(dve.tensor_tensor(t1.rearrange("p (h d) -> p h d", h=nh), src.rearrange("p (h d) -> p h d", h=nh),
                                cos.unsqueeze(1).to_broadcast([P, nh, HD]), ALU.mult))
            for half in range(2):
                def part(ap, hf):
                    return ap.rearrange("p (h a b f) -> p h a b f", h=nh, a=2, b=2)[:, :, :, hf, :]
                s = sin.rearrange("p (a b f) -> p a b f", a=2, b=2)[:, :, half, :].unsqueeze(1) \
                    .to_broadcast([P, nh, 2, ROPE_F])
                v(dve.tensor_tensor(part(t2, half), part(src, 1 - half), s, ALU.mult))
            v.sync()
            for dst, done in outs:
                ins = dve.tensor_tensor(dst, t1.rearrange("p (h d) -> p h d", h=nh),
                                        t2.rearrange("p (h d) -> p h d", h=nh), ALU.add)
                if done is None:
                    v(ins)
                else:
                    ins.then_inc(sem(done), 1)

        def dve_project(dve, v):
            dve.wait_ge(sem("tables_in"), 48)
            for t in range(NT):
                dve.wait_ge(sem("kv_act"), t + 1)
                if t:
                    dve.wait_ge(sem("kv_dve"), t)
                kd = KDUP[:, t, :].rearrange("p (g r d) -> p g r d", g=2, r=2)
                rotate(dve, v, ps[:, t, 0:P], 2, t, [(kd[:, :, 0, :], None), (kd[:, :, 1, :], "kv_dve")])
            for t in range(NC):
                dve.wait_ge(sem("kv_act"), NT + t + 1)
                src = ps[:, NT + t, 0:P].rearrange("p (g d) -> p g d", g=2)
                kd = KCDUP[:, t, :].rearrange("p (g r d) -> p g r d", g=2, r=2)
                v(dve.tensor_copy(kd[:, :, 0, :], src))
                dve.tensor_copy(kd[:, :, 1, :], src).then_inc(sem("kv_dve"), 1)
            for m in range(NT):
                dve.wait_ge(sem("q_mm"), m + 1)
                dve.wait_ge(sem("kv_dve"), NT + NC)
                if m:
                    dve.wait_ge(sem("q_dve"), m)
                rotate(dve, v, ps[:, (6 + m) % 8, :], N_Q, m,
                       [(Q[:, m, :].rearrange("p (h d) -> p h d", h=N_Q), "q_dve")])

        def pe_turn_qk(pe):
            pe.wait_ge(sem("q_dve"), NT)
            pe.wait_ge(sem("kv_dve"), NT + NC)
            pe.wait_ge(sem("gu_act"), 2 * NT)
            for m in range(NT):
                for j in range(4):
                    mm = pe.transpose(ps[:, m, j * P:(j + 1) * P], Q[:, m, j * P:(j + 1) * P], ident)
                mm.then_inc(sem("qk_tp"), 1)
            for g in range(2):
                for m in range(NT):
                    mm = pe.transpose(ps[:, 4 + g, m * P:(m + 1) * P], KDUP[:, m, g * P:(g + 1) * P], ident)
                mm.then_inc(sem("qk_tp"), 1)
            for g in range(2):
                for m in range(NC):
                    i = g * NC + m
                    mm = pe.transpose(ps[:, 6, i * P:(i + 1) * P], KCDUP[:, m, g * P:(g + 1) * P], ident)
            mm.then_inc(sem("qk_tp"), 1)
            pe.wait_ge(sem("tables_in"), 48)
            pe.transpose(ps[:, 7, 0:SG_G], bsr, ident[0:SG_G, 0:SG_G]).then_inc(sem("qk_tp"), 1)

        def dve_turn_qk(dve, v):
            for m in range(NT):
                dve.wait_ge(sem("qk_tp"), m + 1)
                dve.tensor_copy(QT[:, :, m * P:(m + 1) * P], ps[:, m, :].rearrange("p (j t) -> p j t", j=4)) \
                    .then_inc(sem("qk_ev"), 1)
            for g in range(2):
                dve.wait_ge(sem("qk_tp"), NT + g + 1)
                dve.tensor_copy(KT[:, g, :], ps[:, 4 + g, :]).then_inc(sem("qk_ev"), 1)
            dve.wait_ge(sem("qk_tp"), NT + 3)
            dve.tensor_copy(KCT, ps[:, 6, :].rearrange("p (g t) -> p g t", g=2)).then_inc(sem("qk_ev"), 1)
            dve.wait_ge(sem("qk_tp"), NT + 4)
            dve.tensor_copy(bsc, ps[:, 7, 0:SG_G]).then_inc(sem("qk_ev"), 1)

        def pe_spatial(pe):
            pe.wait_ge(sem("qk_ev"), NT + 4)
            pe.wait_ge(sem("ws_in"), 16)
            for b in range(2):
                for j in range(4):
                    mm = pe.transpose(ps[:, b, j * P:(j + 1) * P], WSR[:, 4 * b + j, :], ident)
                mm.then_inc(sem("ws_tp"), 1)
            pe.wait_ge(sem("ws_ev"), 2)
            pe.wait_ge(sem("sg_ln"), 1)
            for g in range(SG_G):
                pe.matmul(ps[:, g, 0:NT * SG_D], WST[:, g, :], VG[:, :, g * SG_D:(g + 1) * SG_D],
                          start=True, stop=True).then_inc(sem("sg_mm"), 1)

        def act_spatial(act, a):
            for b in range(2):
                act.wait_ge(sem("ws_tp"), b + 1)
                act.activation(WST[:, 4 * b:4 * b + 4, :], ps[:, b, :].rearrange("p (g i) -> p g i", g=4), ACT.Copy) \
                    .then_inc(sem("ws_ev"), 1)
            act.wait_ge(sem("sg_sq"), 1)
            act.activation(SGT, VG, ACT.Square).then_inc(sem("sg_ms"), 1)
            act.wait_ge(sem("sg_sq"), 2)
            act.activation(sgm, sgv, ACT.Sqrt).then_inc(sem("sg_rt"), 1)

        def dve_spatial(dve, v):
            vg = VG.rearrange("p m (g d) -> p (m g) d", g=SG_G)
            dve.wait_ge(sem("gu_act"), 2 * NT)
            v(dve.tensor_reduce(sgm, vg, AX, ALU.add))
            v.sync()
            v(dve.tensor_scalar(sgm, sgm, 1.0 / SG_D, None, ALU.mult))
            v.sync()
            dve.tensor_tensor(vg, vg, sgm.unsqueeze(2).to_broadcast([P, 32, SG_D]), ALU.subtract) \
                .then_inc(sem("sg_sq"), 1)
            dve.wait_ge(sem("sg_ms"), 1)
            v(dve.tensor_reduce(sgv, SGT.rearrange("p (g d) -> p g d", d=SG_D), AX, ALU.add))
            v.sync()
            dve.tensor_scalar(sgv, sgv, 1.0 / SG_D, EPS, ALU.mult, ALU.add).then_inc(sem("sg_sq"), 1)
            dve.wait_ge(sem("sg_rt"), 1)
            v(dve.reciprocal(sgv, sgm))
            v.sync()
            dve.wait_ge(sem("sg_sq"), 2)
            dve.tensor_tensor(vg, vg, sgv.unsqueeze(2).to_broadcast([P, 32, SG_D]), ALU.mult) \
                .then_inc(sem("sg_ln"), 1)
            for g in range(SG_G):
                dve.wait_ge(sem("sg_mm"), g + 1)
                cols = slice(g * SG_D, (g + 1) * SG_D)
                dve.scalar_tensor_tensor(MIX[:, :, ATT_W + g * SG_D:ATT_W + (g + 1) * SG_D],
                                         ps[:, g, 0:NT * SG_D].rearrange("p (m d) -> p m d", m=NT), bsc[:, g:g + 1],
                                         UG[:, :, cols], ALU.add, ALU.mult).then_inc(sem("sg_done"), 1)

        UNITS = [(m, h) for m in range(NT) for h in range(N_Q)]

        def span(m):
            lo, hi = max(m - 1, 0), min(m + 2, NT)
            return lo, hi, (hi - lo) * P

        def pe_attention(pe):
            pe.wait_ge(sem("sg_done"), SG_G)

            def scores(u):
                m, h = UNITS[u]
                lo, hi, n = span(m)
                r = slice(HD * (h % 2), HD * (h % 2) + HD)
                if u >= 2:
                    pe.wait_ge(sem("s_dve"), u - 1)
                    pe.wait_ge(sem("s_act"), u - 1)
                qT = QT[r, h // 2, m * P:(m + 1) * P]
                pe.matmul(ps[:, 2 * (u % 2), 0:n], qT, KT[r, h // 4, lo * P:hi * P], start=True, stop=True)
                pe.matmul(ps[:, 2 * (u % 2) + 1, 0:CTX], qT, KCT[r, h // 4, :], start=True, stop=True) \
                    .then_inc(sem("s_mm"), 1)

            def turn(u):
                m, h = UNITS[u]
                n = span(m)[2] // P + NC
                pe.wait_ge(sem("p_act"), u + 1)
                if u:
                    pe.wait_ge(sem("pt_out"), 2 * u)
                for b in range(n):
                    mm = pe.transpose(ps[:, 4 + b // 4, (b % 4) * P:(b % 4 + 1) * P], PB[u % 2][:, b * P:(b + 1) * P], ident)
                mm.then_inc(sem("pt_mm"), 1)

            def values(u):
                m, h = UNITS[u]
                lo, hi, n = span(m)
                g = slice(HD * (h // 4), HD * (h // 4) + HD)
                pe.wait_ge(sem("pt_out"), 2 * u + 2)
                if u:
                    pe.wait_ge(sem("o_dve"), u)
                nb = n // P + NC
                for b in range(nb):
                    vb = V[:, lo + b, g] if b < hi - lo else VC[:, b - (hi - lo), g]
                    mm = pe.matmul(ps[:, 6, 0:HD], PT[u % 2][:, b * P:(b + 1) * P], vb,
                                   start=b == 0, stop=b == nb - 1)
                mm.then_inc(sem("o_mm"), 1)

            scores(0)
            for u in range(len(UNITS)):
                if u + 1 < len(UNITS):
                    scores(u + 1)
                pe_mod_1(pe, 3 * u)
                pe_mod_1(pe, 3 * u + 1)
                turn(u)
                pe_mod_1(pe, 3 * u + 2)
                values(u)

        def act_attention(act, a):
            act.wait_ge(sem("tables_in"), 48)

            def scale_ctx(u):
                n = span(UNITS[u][0])[2]
                act.wait_ge(sem("s_mm"), u + 1)
                if u >= 2:
                    act.wait_ge(sem("p_act"), u - 1)
                act.activation(SS[u % 2][:, n:n + CTX], ps[:, 2 * (u % 2) + 1, 0:CTX], ACT.Copy, scale=HD ** -0.5) \
                    .then_inc(sem("s_act"), 1)

            def exps(u):
                m, h = UNITS[u]
                n = span(m)[2] + CTX
                act.wait_ge(sem("s_max"), u + 1)
                if u >= 2:
                    act.wait_ge(sem("pt_mm"), u - 1)
                act.activation(esc[:, u:u + 1], sinkb[:, h:h + 1], ACT.Exp, bias=nmc[:, u:u + 1]).then_inc(sem("act_chain"), 1)
                act.activation(PB[u % 2][:, 0:n], SS[u % 2][:, 0:n], ACT.Exp, bias=nmc[:, u:u + 1],
                               accum_out=rsc[:, u:u + 1]).then_inc(sem("p_act"), 1)

            def turned_p(u):
                act.wait_ge(sem("pt_mm"), u + 1)
                if u >= 2:
                    act.wait_ge(sem("o_mm"), u - 1)
                act.activation(PT[u % 2][:, 0:512], ps[:, 4, :], ACT.Copy).then_inc(sem("pt_out"), 1)

            scale_ctx(0)
            for u in range(len(UNITS)):
                if u + 1 < len(UNITS):
                    scale_ctx(u + 1)
                exps(u)
                turned_p(u)

        def dve_attention(dve, v):
            dve.wait_ge(sem("tables_in"), 48)

            def masked(u):
                m, h = UNITS[u]
                lo, hi, n = span(m)
                first = (lo - m + 1) * P
                dve.wait_ge(sem("s_mm"), u + 1)
                if u >= 2:
                    dve.wait_ge(sem("p_act"), u - 1)
                dve.scalar_tensor_tensor(SS[u % 2][:, 0:n], ps[:, 2 * (u % 2), 0:n], HD ** -0.5,
                                         RP[:, R_MASK + first:R_MASK + first + n], ALU.mult, ALU.add) \
                    .then_inc(sem("s_dve"), 1)
                dve.wait_ge(sem("s_dve"), u + 1)
                dve.wait_ge(sem("s_act"), u + 1)
                v(dve.tensor_reduce(mxc[:, u:u + 1], SS[u % 2][:, 0:n + CTX], AX, ALU.max))
                v.sync()
                dve.tensor_scalar(nmc[:, u:u + 1], mxc[:, u:u + 1], sinkb[:, h:h + 1], -1.0, ALU.max, ALU.mult) \
                    .then_inc(sem("s_max"), 1)

            def finish(u):
                m, h = UNITS[u]
                n = span(m)[2] // P + NC
                dve.wait_ge(sem("pt_mm"), u + 1)
                if u >= 2:
                    dve.wait_ge(sem("o_mm"), u - 1)
                w = max(n - 4, 0) * P
                if w:
                    dve.tensor_copy(PT[u % 2][:, 512:512 + w], ps[:, 5, 0:w]).then_inc(sem("pt_out"), 1)
                else:
                    dve.sem_inc(sem("pt_out"), 1)
                dve.wait_ge(sem("act_chain"), u + 1)
                v(dve.tensor_tensor(dnc[:, u:u + 1], rsc[:, u:u + 1], esc[:, u:u + 1], ALU.add))
                v.sync()
                v(dve.reciprocal(rcc[:, u:u + 1], dnc[:, u:u + 1]))
                v.sync()
                dve.wait_ge(sem("o_mm"), u + 1)
                dve.tensor_scalar(MIX[:, m, h * HD:(h + 1) * HD], ps[:, 6, 0:HD], rcc[:, u:u + 1], None, ALU.mult) \
                    .then_inc(sem("o_dve"), 1)

            masked(0)
            for u in range(len(UNITS)):
                if u + 1 < len(UNITS):
                    masked(u + 1)
                for n in range(3 * u // KD, (3 * u + 3) // KD):
                    dve_mod_1(dve, n)
                finish(u)

        def pe_out(pe, l, src):
            for n in range(2):
                w_wait(pe, W_OUT[l][n])
                w = W(W_OUT[l][n], KD, 512)
                for m in range(NT):
                    if n == 0 and m == 0 and l == 0:
                        pe.wait_ge(sem("mt_turned"), 2 * NT)
                    if n == 0 and m == 0 and l == 1:
                        pe.wait_ge(sem("yn"), 4 * HY_Q)
                    for k in range(KD):
                        mm = pe.matmul(ps[:, 4 * n + m, :], src[:, k, m * P:(m + 1) * P], w[:, k, :],
                                       start=k == 0, stop=k == KD - 1)
                    mm.then_inc(sem("yo_mm"), 1)
                used(pe, "yo_mm", l * 8 + 4 * n + 4)

        def dve_out(dve, v, l, tmp):
            for t in range(8):
                n, m = t // 4, t % 4
                cols = slice(n * 512, (n + 1) * 512)
                dve.wait_ge(sem("yo_mm"), l * 8 + t + 1)
                y = tmp[t % 2][:, 0:512]
                v(dve.tensor_tensor(y, ps[:, t, :], MODR[:, 2 * D + n * 512:2 * D + (n + 1) * 512], ALU.mult))
                v.sync()
                dve.tensor_tensor(X[:, m, cols], X[:, m, cols], y, ALU.add).then_inc(sem("yo_dve"), 1)
            dve.wait_ge(sem("yo_dve"), l * 8 + 8)

        G2T = [A(92, D), A(96, D)]
        RTR = A3(100, KD, E)
        EB = A(102, E)
        EXG = [A(48, D), A(52, D)]
        EXT = [A3(56, KD, P), A3(60, KD, P)]
        EY = [A(64, D), A(68, D)]
        ESG = [A(72, FE), A(73, FE)]
        EA = [A(74, FE), A(75, FE)]
        EAT = [A3(76, 2, P), A3(77, 2, P)]
        EOH = [A(78, 256).bitcast(BF16).rearrange("p (m s) -> p m s", m=NT), A(79, 256).bitcast(BF16).rearrange("p (m s) -> p m s", m=NT)]

        def t64(kb):
            return A3(kb, NT, E)
        SC, BI, MK, MR, SEL, WTS, POS, POSM, SLM = [t64(104 + i) for i in range(9)]
        M8 = A3(113, 32, 8)
        CMP, CMQ = A(114, 256), A(115, 256)
        GS, RK, GM, PEN = [A(116 + 0.125 * i, 32) for i in range(4)]
        T8, S8, W8 = [A3(116.5 + 0.125 * i, NT, 8) for i in range(3)]
        S8I = A3(116.875, NT, 8).bitcast(I32)
        CNT, OV, OVC, OVS, OVT = [A(117 + 0.25 * i, E) for i in range(5)]
        SW, RW = A(118.25, 4), A(118.3125, 4)
        OVE = A(118.5, 32, 1)
        OVI = A(118.75, 36, 1).bitcast(I32)
        IOR = A(119, P)
        TOKI = [A(119.5, 1).bitcast(I32), A(119.5625, 1).bitcast(I32)]
        BIGT = A(120, 2048)
        WGU = [A3(0, KD, 512), A3(24, KD, 512)]
        WD = [A3(16, 2, D), A3(40, 2, D)]
        CGB = [HT[:, 2 * i:2 * i + 2, :].rearrange("p k t -> p (k t)") for i in range(4)] + [A(80, D), A(84, D)]

        def sp_router(sp, l):
            sp.dma_start(RTR, w_router[l].rearrange("(p k) e -> p k e", k=KD)).then_inc(sem("eb_in"), 16)
            sp.dma_start(EB, e_bias[l:l + 1, :].to_broadcast([P, E])).then_inc(sem("eb_in"), 16)

        def e_view(w, l, e):
            v = w[l].rearrange("e (p k) f -> p e k f", k=KD)
            return v[:, bass.ds(e, 1), :, :].rearrange("p a k f -> p (a k) f")

        def sp_gate_up(sp, l, e, n, p):
            wait(sp, f"gu_m_{l}", n - 1)
            sp.dma_start(WGU[p][:, :, 0:FE], e_view(w_gate, l, e)).then_inc(sem(f"wgu{p}_{l}"), 16)
            sp.dma_start(WGU[p][:, :, FE:2 * FE], e_view(w_up, l, e)).then_inc(sem(f"wgu{p}_{l}"), 16)

        def sp_down(sp, l, e, n, p):
            wait(sp, f"y_mm_{l}", n * 2 - 2)
            v = w_down[l].rearrange("e (p k) n -> p e k n", k=2)[:, bass.ds(e, 1), :, :]
            sp.dma_start(WD[p], v.rearrange("p a k n -> p (a k) n")).then_inc(sem(f"wd{p}_{l}"), 16)

        def sp_experts(sp, l):
            sp.wait_ge(sem("dense_used"), W_SH[l][0] + 1)
            sp_gate_up(sp, l, 0, 0, 0)
            if l == 0:
                sp_gate_up(sp, l, 1, 1, 1)
                sp.wait_ge(sem("dense_used"), W_SH[l][1] + 1)
                sp_down(sp, l, 0, 0, 0)
            else:
                sp_down(sp, l, 0, 0, 0)
                sp.wait_ge(sem("dense_used"), W_SH[l][1] + 1)
                sp_gate_up(sp, l, 1, 1, 1)

            def pair(i):
                for p in range(2):
                    n = i * 2 + p
                    sp_gate_up(sp, l, n, n, p)
                    sp_down(sp, l, n - 1, n - 1, 1 - p)
            pair(1)
            with sp.Fori(2, E // 2) as i:
                pair(i)
            sp_down(sp, l, E - 1, E - 1, 1)
            sp.wait_ge(sem("tables"), l + 1)
            nov = sp_nov(sp, l)

            def over(i):
                for p in range(2):
                    with sp.If(nov > i * 2 + p):
                        e = sp.value_load(OVI[0:1, bass.ds(i * 2 + p, 1)], min_val=0, max_val=E - 1)
                        sp_gate_up(sp, l, e, i * 2 + p + E, p)
                        sp_down(sp, l, e, i * 2 + p + E, p)
            over_loop(sp, nov, over)

        def over_loop(eng, nov, pair):
            with eng.Fori(0, FEW // 2) as i:
                pair(i)
            with eng.If(nov > FEW):
                with eng.Fori(FEW // 2, OVER // 2) as i:
                    pair(i)

        def sp_nov(eng, l):
            return eng.value_load(OVI[0:1, 32:33], min_val=0, max_val=OVER)

        def pe_router(pe, l):
            pe.wait_ge(sem("turned"), 2 * (before[f"n2_{l}"] + NT))
            pe.wait_ge(sem("eb_in"), l * 32 + 32)
            for m in range(NT):
                for k in range(KD):
                    mm = pe.matmul(ps[:, 0, m * E:(m + 1) * E], HT[:, k, m * P:(m + 1) * P], RTR[:, k, :],
                                   start=k == 0, stop=k == KD - 1)
            mm.then_inc(sem("lg_mm"), 1)

        def act_router(act, a, l):
            act.wait_ge(sem("lg_mm"), l + 1)
            act.wait_ge(sem("mod_stored"), 16)
            act.activation(SC, ps[:, 0, 0:NT * E].rearrange("p (m e) -> p m e", m=NT), ACT.Sigmoid) \
                .then_inc(sem("score"), 1)

        def dve_select(dve, v, l):
            bc = lambda ap, n: ap.unsqueeze(2).to_broadcast([P, ap.shape[1], n])
            row = lambda ap: ap.unsqueeze(1).to_broadcast([P, NT, E])

            def do(ins):
                v(ins)
                v.sync()
            dve.wait_ge(sem("score"), l + 1)
            do(dve.tensor_tensor(BI, SC, row(EB), ALU.add))
            bg = BI.rearrange("p m (g e) -> p (m g) e", g=GROUPS)
            for i in range(32):
                v(dve.max(M8[:, i, :], bg[:, i, :]))
            v.sync()
            do(dve.tensor_tensor(GS, M8[:, :, 0], M8[:, :, 1], ALU.add))
            gs3 = GS.rearrange("p (m g) -> p m g", m=NT)
            c4 = lambda ap: ap.rearrange("p (m g h) -> p m g h", m=NT, g=GROUPS)
            other = gs3.unsqueeze(2).to_broadcast([P, NT, GROUPS, GROUPS])
            own = gs3.unsqueeze(3).to_broadcast([P, NT, GROUPS, GROUPS])
            v(dve.tensor_tensor(c4(CMP), other, own, ALU.is_gt))
            do(dve.tensor_tensor(c4(CMQ), other, own, ALU.is_equal))
            lt = K[:, C_LT:C_LT + 64].unsqueeze(1).to_broadcast([P, NT, 64])
            do(dve.tensor_tensor(CMQ.rearrange("p (m x) -> p m x", m=NT), CMQ.rearrange("p (m x) -> p m x", m=NT), lt, ALU.mult))
            do(dve.tensor_tensor(CMP, CMP, CMQ, ALU.add))
            do(dve.tensor_reduce(RK, CMP.rearrange("p (g h) -> p g h", h=GROUPS), AX, ALU.add))
            do(dve.tensor_scalar(GM, RK, TOPK_GROUPS - 0.5, None, ALU.is_lt))
            v(dve.tensor_scalar(PEN, GM, -1.0, BIG, ALU.add, ALU.mult))
            mg = MK.rearrange("p m (g e) -> p (m g) e", g=GROUPS)
            do(dve.tensor_tensor(mg, bg, bc(GM, 8), ALU.mult))
            do(dve.tensor_tensor(mg, mg, bc(PEN, 8), ALU.add))
            for m in range(NT):
                v(dve.max(T8[:, m, :], MK[:, m, :]))
            v.sync()
            for m in range(NT):
                v(dve.match_replace(MR[:, m, :], T8[:, m, :], MK[:, m, :], -3.0 * BIG))
            v.sync()
            dve.tensor_tensor(SEL, MR, MK, ALU.not_equal).then_inc(sem("sel"), 1)
            dve.wait_ge(sem("sel"), l + 1)
            do(dve.tensor_tensor(WTS, SC, SEL, ALU.mult))
            do(dve.tensor_reduce(SW, WTS, AX, ALU.add))
            do(dve.reciprocal(RW, SW))
            do(dve.tensor_scalar(RW, RW, ROUTED_SCALE, None, ALU.mult))
            do(dve.tensor_tensor(WTS, WTS, bc(RW, E), ALU.mult))
            dve.wait_ge(sem("pos_mm"), l + 1)
            v(dve.tensor_copy(POS, ps[:, 1, 0:NT * E].rearrange("p (m e) -> p m e", m=NT)))
            do(dve.tensor_copy(CNT, ps[:, 2, 0:E]))
            do(dve.scalar_tensor_tensor(POSM, POS, 1.0, SEL, ALU.add, ALU.mult))
            v(dve.tensor_scalar(POSM, POSM, -1.0, None, ALU.add))
            do(dve.tensor_scalar(OV, CNT, P + 0.5, None, ALU.is_gt))
            for j in range(2, NT):
                do(dve.scalar_tensor_tensor(OV, CNT, j * P + 0.5, OV, ALU.is_gt, ALU.add))
            do(dve.tensor_tensor_scan(OVC, ones[:, 0:E], OV, 0.0, ALU.mult, ALU.add))
            do(dve.tensor_tensor(OVS, OVC, OV, ALU.subtract))
            do(dve.tensor_scalar(OVS, OVS, E - 1.0, 128.0, ALU.add, ALU.mult))
            do(dve.tensor_tensor(OVS, OVS, K[:, C_E128:C_E128 + E], ALU.subtract))
            do(dve.tensor_scalar(SLM, POS, P - 0.5, None, ALU.is_gt))
            do(dve.tensor_tensor(SLM, SLM, row(OVS), ALU.mult))
            do(dve.tensor_tensor(SLM, SLM, POS, ALU.add))
            do(dve.tensor_tensor(SLM, SLM, row(K[:, C_E128:C_E128 + E]), ALU.add))
            do(dve.scalar_tensor_tensor(SLM, SLM, 1.0, SEL, ALU.add, ALU.mult))
            dve.tensor_scalar(SLM, SLM, -1.0, None, ALU.add).then_inc(sem("slots"), 1)

        def dve_over_table(dve, v, l):
            def do(ins):
                v(ins)
                v.sync()
            j3 = BIGT[0:1, :].rearrange("p (j e) -> p j e", j=32)
            do(dve.tensor_tensor(j3, OVC[0:1, :].unsqueeze(1).to_broadcast([1, 32, E]),
                                 K[0:1, C_IOTA:C_IOTA + 32].unsqueeze(2).to_broadcast([1, 32, E]), ALU.is_le))
            do(dve.tensor_reduce(OVE, j3, AX, ALU.add))
            do(dve.tensor_scalar(OVE, OVE, E - 1.0, None, ALU.min))
            v(dve.tensor_copy(OVI[:, 0:32], OVE))
            v(dve.tensor_copy(OVI[:, 32:33], OVC[0:1, E - 1:E]))
            dve.tensor_scalar(IOR, K[:, C_IOTA:C_IOTA + P], float(E * P), None, ALU.add).then_inc(sem(f"next_range_{l}"), 1)

        def dve_slot_table(dve, v, l, tiles):
            def do(ins):
                v(ins)
                v.sync()
            if 0 in tiles:
                for m in range(NT):
                    v(dve.max(S8[:, m, :], SLM[:, m, :]))
                v.sync()
                v(dve.tensor_copy(S8I, S8))
            hit = BIGT[:, 0:512].rearrange("p (k e) -> p k e", k=8)
            for m in tiles:
                do(dve.tensor_tensor(hit, SLM[:, m, :].unsqueeze(1).to_broadcast([P, 8, E]),
                                     S8[:, m, :].unsqueeze(2).to_broadcast([P, 8, E]), ALU.is_equal))
                do(dve.tensor_tensor(hit, hit, WTS[:, m, :].unsqueeze(1).to_broadcast([P, 8, E]), ALU.mult))
                do(dve.tensor_reduce(W8[:, m, :], hit, AX, ALU.add))
            if NT - 1 in tiles:
                dve.engine_nop().then_inc(sem("tables"), 1)

        def pe_positions(pe, l):
            pe.wait_ge(sem("sel"), l + 1)
            pe.wait_ge(sem("consts_made"), 1)
            for m in range(NT):
                for j in range(m + 1):
                    pe.matmul(ps[:, 1, m * E:(m + 1) * E], ones[:, :] if j < m else K[:, C_TRI:C_TRI + P], SEL[:, j, :],
                              start=j == 0, stop=j == m)
            for m in range(NT):
                mm = pe.matmul(ps[:, 2, 0:E], ones[:, :], SEL[:, m, :], start=m == 0, stop=m == NT - 1)
            mm.then_inc(sem("pos_mm"), 1)

        def pe_shared(pe, l, tiles):
            a, b = W_SH[l]
            if tiles is not None:
                w_wait(pe, a)
                w = W(a, KD, 512)
                for m in tiles:
                    bank = 3 + m
                    for k in range(KD):
                        mm = pe.matmul(ps[:, bank, :], HT[:, k, m * P:(m + 1) * P], w[:, k, :],
                                       start=k == 0, stop=k == KD - 1)
                    mm.then_inc(sem("shgu_mm"), 1)
                if NT - 1 in tiles:
                    used(pe, "shgu_mm", l * NT + NT)
                return
            w_wait(pe, b)
            w = W(b, 2, D)
            for m in range(NT):
                pe.wait_ge(sem("sha"), l * NT + m + 1)
                if m:
                    pe.wait_ge(sem("shat"), l * NT + m)
                for k in range(2):
                    mm = pe.transpose(ps[:, 0, k * P:(k + 1) * P], EA[m % 2][:, k * P:(k + 1) * P], ident)
                mm.then_inc(sem("shat_mm"), 1)
                pe.wait_ge(sem("shat"), l * NT + m + 1)
                for n in range(2):
                    t = 2 * m + n
                    bank = 3 + t % 4
                    if t < 4:
                        pe.wait_ge(sem("sha"), l * NT + bank - 2)
                    else:
                        pe.wait_ge(sem("shy_act"), l * NT + (t - 4) // 2 + 1)
                        pe.wait_ge(sem("shy_dve"), l * NT + (t - 4) // 2 + 1)
                    for k in range(2):
                        mm = pe.matmul(ps[:, bank, :], EAT[m % 2][:, k, :], w[:, k, n * 512:(n + 1) * 512],
                                       start=k == 0, stop=k == 1)
                    mm.then_inc(sem("shy_mm"), 1)
            used(pe, "shy_mm", l * 2 * NT + 2 * NT)

        SHG = BIGT[:, 0:1024].rearrange("p (m f) -> p m f", m=NT)
        SHA = BIGT[:, 1024:2048].rearrange("p (m f) -> p m f", m=NT)

        def act_shared(act, a, l):
            for m in range(NT):
                act.wait_ge(sem("shgu_mm"), l * NT + m + 1)
                act.activation(SHG[:, m, :], ps[:, 3 + m, 0:FE], ACT.Silu).then_inc(sem("shsilu"), 1)
            for m in range(NT):
                act.wait_ge(sem("shat_mm"), l * NT + m + 1)
                if m >= 2:
                    act.wait_ge(sem("shy_mm"), l * 2 * NT + 2 * m - 2)
                act.activation(EAT[m % 2], ps[:, 0, 0:FE].rearrange("p (k t) -> p k t", k=2), ACT.Copy) \
                    .then_inc(sem("shat"), 1)
                act.wait_ge(sem("shy_mm"), l * 2 * NT + 2 * m + 1)
                act.activation(H[:, m, 0:512], ps[:, 3 + (2 * m) % 4, :], ACT.Copy).then_inc(sem("shy_act"), 1)

        def dve_shared(dve, v, l, tiles):
            if tiles is not None:
                for m in tiles:
                    dve.wait_ge(sem("shsilu"), l * NT + m + 1)
                    if m >= 2:
                        dve.wait_ge(sem("shat_mm"), l * NT + m - 1)
                    dve.tensor_tensor(EA[m % 2].rearrange("p (k j) -> p j k", k=2),
                                      SHG[:, m, :].rearrange("p (j k) -> p j k", k=2),
                                      ps[:, 3 + m, FE:2 * FE].rearrange("p (j k) -> p j k", k=2), ALU.mult) \
                        .then_inc(sem("sha"), 1)
                return
            for m in range(NT):
                dve.wait_ge(sem("shy_mm"), l * 2 * NT + 2 * m + 2)
                dve.tensor_copy(H[:, m, 512:1024], ps[:, 3 + (2 * m + 1) % 4, :]).then_inc(sem("shy_dve"), 1)

        def pe_token_ids(pe, l, n, p):
            pe.wait_ge(sem(f"oh_{l}"), n + 1)
            pe.wait_ge(sem(f"tok_{l}"), n)
            for m in range(NT):
                mm = pe.matmul(ps[:, 7, 2 * p:2 * p + 2], EOH[p][:, m, :], tid[:, 2 * m:2 * m + 2],
                               start=m == 0, stop=m == NT - 1)
            mm.then_inc(sem(f"tok_mm_{l}"), 1)

        def pe_rows(pe, l, n, p, landed_sem, landed_count, first):
            pe.wait_ge(sem(landed_sem), landed_count)
            for kk in range(2):
                if not first:
                    pe.wait_ge(sem(f"xt_out_{l}"), n * 2)
                for j in range(4):
                    k = 4 * kk + j
                    mm = pe.transpose(ps[:, kk, j * P:(j + 1) * P], EXG[p][:, k * P:(k + 1) * P], ident)
                mm.then_inc(sem(f"xt_mm_{l}"), 1)

        def pe_gate_up(pe, l, n, p, count, between=None):
            pe.wait_ge(sem(f"xt_out_{l}"), n * 2 + 2)
            pe.wait_ge(sem(f"wgu{p}_{l}"), count)
            for k in range(KD):
                if k == KD // 2 and between is not None:
                    between()
                mm = pe.matmul(ps[:, 2 + p, :], EXT[p][:, k, :], WGU[p][:, k, :], start=k == 0, stop=k == KD - 1)
            mm.then_inc(sem(f"gu_m_{l}"), 1)

        def pe_turn_a(pe, l, n, p):
            pe.wait_ge(sem(f"a_{l}"), n + 1)
            for k in range(2):
                mm = pe.transpose(ps[:, 4, k * P:(k + 1) * P], EA[p][:, k * P:(k + 1) * P], ident)
            mm.then_inc(sem(f"at_mm_{l}"), 1)

        def pe_down(pe, l, n, p, count, first):
            pe.wait_ge(sem(f"at_{l}"), n + 1)
            pe.wait_ge(sem(f"wd{p}_{l}"), count)
            for h in range(2):
                if not first:
                    pe.wait_ge(sem(f"y_out_{l}"), n * 2)
                for k in range(2):
                    mm = pe.matmul(ps[:, 5 + h, :], EAT[p][:, k, :], WD[p][:, k, h * 512:(h + 1) * 512],
                                   start=k == 0, stop=k == 1)
                mm.then_inc(sem(f"y_mm_{l}"), 1)

        def pe_experts(pe, l):
            pe.wait_ge(sem("shy_dve"), l * NT + NT)
            pe.wait_ge(sem("shy_act"), l * NT + NT)
            pe_rows(pe, l, 0, 0, f"xg0_{l}", 16, True)

            def pair(i, last):
                for p in range(2):
                    n, q = i * 2 + p, 1 - p
                    pe_gate_up(pe, l, n, p, i * 32 + 32, None if last else lambda: pe_token_ids(pe, l, n + 2, p))
                    if not (last and p == 1):
                        pe_rows(pe, l, n + 1, q, f"xg{q}_{l}", (i + p) * 16 + 16, False)
                    if not (isinstance(n, int) and n == 0):
                        pe_down(pe, l, n - 1, q, (i + p) * 16, isinstance(n, int) and n == 1)
                    pe_turn_a(pe, l, n, p)
            pair(0, False)
            pair(1, False)
            with pe.Fori(2, E // 2 - 1) as i:
                pair(i, False)
            pair(E // 2 - 1, True)
            pe_down(pe, l, E - 1, 1, E // 2 * 16, False)
            pe.wait_ge(sem("tables"), l + 1)
            nov = sp_nov(pe, l)
            with pe.If(nov > 0):
                pe_token_ids(pe, l, E, 0)

            def over(i):
                for p in range(2):
                    n = i * 2 + p + E
                    with pe.If(nov > i * 2 + p):
                        pe_rows(pe, l, n, p, f"xg{p}_{l}", i * 16 + 16 * (E // 2 + 1), False)
                        with pe.If(nov > i * 2 + p + 1):
                            pe_token_ids(pe, l, n + 1, 1 - p)
                        pe_gate_up(pe, l, n, p, i * 32 + 32 * (E // 2 + 1))
                        pe_turn_a(pe, l, n, p)
                        pe_down(pe, l, n, p, i * 16 + 16 * (E // 2 + 1), False)
            over_loop(pe, nov, over)

        def act_rows(act, l, n, p, wait_free):
            act.wait_ge(sem(f"xt_mm_{l}"), n * 2 + 1)
            if wait_free:
                act.wait_ge(sem(f"gu_m_{l}"), n - 1)
            act.activation(EXT[p][:, 0:4, :], ps[:, 0, :].rearrange("p (k s) -> p k s", k=4), ACT.Copy) \
                .then_inc(sem(f"xt_out_{l}"), 1)

        def act_silu(act, l, n, p):
            act.wait_ge(sem(f"gu_m_{l}"), n + 1)
            act.activation(ESG[p], ps[:, 2 + p, 0:FE], ACT.Silu).then_inc(sem(f"silu_{l}"), 1)

        def act_turned_a(act, l, n, p):
            act.wait_ge(sem(f"at_mm_{l}"), n + 1)
            act.activation(EAT[p], ps[:, 4, 0:FE].rearrange("p (k s) -> p k s", k=2), ACT.Copy) \
                .then_inc(sem(f"at_{l}"), 1)

        def act_result(act, l, n, p):
            act.wait_ge(sem(f"y_mm_{l}"), n * 2 + 1)
            act.activation(EY[p][:, 0:512], ps[:, 5, :], ACT.Copy).then_inc(sem(f"y_out_{l}"), 1)

        def act_store(act, l, n, p, b, done):
            act.wait_ge(sem(f"y_out_{l}"), n * 2 + 2)
            rows = y_dram.rearrange("(b s) d -> s b d", s=P)[:, bass.ds(b, 1), :].rearrange("s a d -> s (a d)")
            act.dma_start(rows, EY[p]).then_inc(sem(done), 16)

        def act_experts(act, a, l):
            act.wait_ge(sem("zeroed"), 16)
            act_rows(act, l, 0, 0, False)

            def result(n, q, count):
                wait(act, f"yst{q}_{l}", count)
                act_result(act, l, n, q)

            def pair(i, last):
                for p in range(2):
                    n, q = i * 2 + p, 1 - p
                    act_silu(act, l, n, p)
                    if not (last and p == 1):
                        act_rows(act, l, n + 1, q, not (isinstance(n, int) and n == 0))
                    begun = not (isinstance(n, int) and n == 0)
                    if begun:
                        result(n - 1, q, (i + p) * 16 - 16)
                    act_turned_a(act, l, n, p)
                    if begun:
                        act_store(act, l, n - 1, q, n - 1, f"yst{q}_{l}")
            pair(0, False)
            pair(1, False)
            with act.Fori(2, E // 2 - 1) as i:
                pair(i, False)
            pair(E // 2 - 1, True)
            result(E - 1, 1, E // 2 * 16 - 16)
            act_store(act, l, E - 1, 1, E - 1, f"yst1_{l}")
            act.wait_ge(sem("tables"), l + 1)
            nov = sp_nov(act, l)
            act.sem_inc(sem(f"over_stored_{l}"), 1)

            def over(i):
                for p in range(2):
                    n = i * 2 + p + E
                    with act.If(nov > i * 2 + p):
                        act_rows(act, l, n, p, False)
                        act_silu(act, l, n, p)
                        act_turned_a(act, l, n, p)
                        act.wait_ge(sem(f"yst{p}_{l}"), 16 * (E // 2))
                        act.wait_ge(sem(f"over_stored_{l}"), (i * 2 + p) * 16 + 1)
                        act_result(act, l, n, p)
                        act_store(act, l, n, p, n, f"over_stored_{l}")
            over_loop(act, nov, over)
            for p in range(2):
                act.wait_ge(sem(f"yst{p}_{l}"), 16 * (E // 2))
            act.wait_ge(sem(f"over_stored_{l}"), nov * 16 + 1)
            act.sem_inc(sem("moe_done"), 1)

        def dve_one_hot(dve, l, n, p, column, against, wait_free):
            if wait_free:
                dve.wait_ge(sem(f"tok_mm_{l}"), n - 1)
            dve.tensor_tensor(EOH[p], column.to_broadcast([P, NT, P]), against.unsqueeze(1).to_broadcast([P, NT, P]),
                              ALU.is_equal).then_inc(sem(f"oh_{l}"), 1)

        def dve_token_ids(dve, l, n, p, wait_free):
            dve.wait_ge(sem(f"tok_mm_{l}"), n + 1)
            if wait_free is not None:
                dve.wait_ge(sem(f"xg{p}_{l}"), wait_free)
            dve.tensor_scalar(TOKI[p], ps[:, 7, 2 * p:2 * p + 1], ps[:, 7, 2 * p + 1:2 * p + 2], None, ALU.add).then_inc(sem(f"tok_{l}"), 1)

        def dve_rows(dve, l, n, p, wait_free):
            dve.wait_ge(sem(f"xt_mm_{l}"), n * 2 + 2)
            if wait_free:
                dve.wait_ge(sem(f"gu_m_{l}"), n - 1)
            dve.tensor_copy(EXT[p][:, 4:8, :], ps[:, 1, :].rearrange("p (k s) -> p k s", k=4)) \
                .then_inc(sem(f"xt_out_{l}"), 1)

        def dve_product(dve, l, n, p, wait_free):
            dve.wait_ge(sem(f"silu_{l}"), n + 1)
            dve.tensor_tensor(EA[p].rearrange("p (k j) -> p j k", k=2), ESG[p].rearrange("p (j k) -> p j k", k=2),
                              ps[:, 2 + p, FE:2 * FE].rearrange("p (j k) -> p j k", k=2), ALU.mult) \
                .then_inc(sem(f"a_{l}"), 1)

        def dve_result(dve, l, n, p):
            dve.wait_ge(sem(f"y_mm_{l}"), n * 2 + 2)
            dve.tensor_copy(EY[p][:, 512:1024], ps[:, 6, :]).then_inc(sem(f"y_out_{l}"), 1)

        def dve_experts(dve, v, l):
            first = K[:, C_IOTA:C_IOTA + P]
            dve_rows(dve, l, 0, 0, False)
            tables = {0: lambda: dve_over_table(dve, v, l), 1: lambda: dve_slot_table(dve, v, l, range(0, 2)),
                      2: lambda: dve_slot_table(dve, v, l, range(2, NT))}

            def result(n, q, count):
                wait(dve, f"yst{q}_{l}", count)
                dve_result(dve, l, n, q)

            def pair(i, last):
                for p in range(2):
                    n, q = i * 2 + p, 1 - p
                    begun = not (isinstance(n, int) and n == 0)
                    if not last:
                        dve_one_hot(dve, l, n + 2, p, POSM[:, :, bass.ds(n + 2, 1)], first, True)
                        dve_token_ids(dve, l, n + 2, p, i * 16 + 16)
                    dve_product(dve, l, n, p, True)
                    if not (last and p == 1):
                        dve_rows(dve, l, n + 1, q, begun)
                    if begun:
                        result(n - 1, q, (i + p) * 16 - 16)
                    if isinstance(n, int) and n in tables:
                        tables[n]()
            pair(0, False)
            pair(1, False)
            with dve.Fori(2, E // 2 - 1) as i:
                pair(i, False)
            pair(E // 2 - 1, True)
            result(E - 1, 1, E // 2 * 16 - 16)
            dve.wait_ge(sem("tables"), l + 1)
            nov = sp_nov(dve, l)

            def ids(n, p, block, count):
                e = dve.value_load(OVI[0:1, bass.ds(block, 1)], min_val=0, max_val=E - 1)
                dve.wait_ge(sem(f"tok_mm_{l}"), n)
                dve.wait_ge(sem(f"next_range_{l}"), n - E + 1)
                dve_one_hot(dve, l, n, p, SLM[:, :, bass.ds(e, 1)], IOR, False)
                dve.wait_ge(sem(f"oh_{l}"), n + 1)
                dve.tensor_scalar(IOR, IOR, float(P), None, ALU.add).then_inc(sem(f"next_range_{l}"), 1)
                dve_token_ids(dve, l, n, p, count)
            with dve.If(nov > 0):
                ids(E, 0, 0, 16 * (E // 2))

            def over(i):
                for p in range(2):
                    n = i * 2 + p + E
                    with dve.If(nov > i * 2 + p):
                        with dve.If(nov > i * 2 + p + 1):
                            ids(n + 1, 1 - p, i * 2 + p + 1, (i + p) * 16 + 16 * (E // 2))
                        dve_rows(dve, l, n, p, False)
                        dve_product(dve, l, n, p, False)
                        dve.wait_ge(sem(f"yst{p}_{l}"), 16 * (E // 2))
                        dve.wait_ge(sem(f"over_stored_{l}"), (i * 2 + p) * 16 + 1)
                        dve_result(dve, l, n, p)
            over_loop(dve, nov, over)

        def gather(pool, dst, table, index, bound):
            return pool.indirect_dma_start(
                out=dst, out_offset=None, in_=table,
                in_offset=bass.IndirectOffsetOnAxis(ap=index, axis=0), bounds_check=bound, oob_is_err=False)

        def pool_experts(pool, l):
            last_token, last_row = pool.to_reg(T - 1), pool.to_reg(NBLK * P - 1)
            pool.wait_ge(sem("h2_stored"), 16 * (l + 1))

            def rows(n, p, free):
                pool.wait_ge(sem(f"tok_{l}"), n + 1)
                if free is not None:
                    pool.wait_ge(sem(f"xt_mm_{l}"), free)
                pool.sem_inc(sem("rows_asked"), 1)
                gather(pool, EXG[p], h2_dram[l], TOKI[p], last_token).then_inc(sem(f"xg{p}_{l}"), 16)
            rows(0, 0, None)
            rows(1, 1, None)
            with pool.Fori(1, E // 2) as i:
                for p in range(2):
                    rows(i * 2 + p, p, i * 4 + 2 * p - 2)
            pool.wait_ge(sem("tables"), l + 1)
            nov = sp_nov(pool, l)

            def over(i):
                for p in range(2):
                    with pool.If(nov > i * 2 + p):
                        rows(i * 2 + p + E, p, i * 4 + 2 * (p + E) - 2)
            over_loop(pool, nov, over)
            pool.wait_ge(sem("moe_done"), l + 1)
            for n in range(NT * TOP_K):
                m, k = n // TOP_K, n % TOP_K
                g = l * NT * TOP_K + n
                if n >= CG:
                    pool.wait_ge(sem("cadd"), g - CG + 1)
                gather(pool, CGB[g % CG], y_dram, S8I[:, m, k:k + 1], last_row).then_inc(sem(f"cg{g % CG}"), 16)

        def dve_combine(dve, v, l):
            dve.wait_ge(sem("shy_act"), l * NT + NT)
            dve.wait_ge(sem("shy_dve"), l * NT + NT)
            for n in range(NT * TOP_K):
                m, k = n // TOP_K, n % TOP_K
                g = l * NT * TOP_K + n
                dve.wait_ge(sem(f"cg{g % CG}"), g // CG * 16 + 16)
                if k:
                    dve.wait_ge(sem("cadd"), g)
                dve.scalar_tensor_tensor(H[:, m, :], CGB[g % CG], W8[:, m, k:k + 1], H[:, m, :], ALU.mult, ALU.add) \
                    .then_inc(sem("cadd"), 1)
                if k == TOP_K - 1:
                    dve.wait_ge(sem("cadd"), g + 1)
                    v(dve.tensor_tensor(H[:, m, :], H[:, m, :], MODR[:, 5 * D:6 * D], ALU.mult))
                    v.sync()
                    dve.tensor_tensor(X[:, m, :], X[:, m, :], H[:, m, :], ALU.add).then_inc(sem("layer_start"), 1)

        DFT = [A3(48 + 8 * i, NT, T) for i in range(4)]
        MC, MS, IC, IS = DFT
        ZB = [A3(80 + 4 * j, 2, T) for j in range(3)]
        R1, R2 = A3(92, NT, 512), A3(100, NT, 512)
        AS, BS = A3(108, 2, 512), A3(112, 2, 512)
        A2T = A(120, T, FILT_HID)
        HF = MODR[:, 0:2048].rearrange("p (t c) -> p t c", t=NT)
        PP = HF
        WIN = [A(124, 512), A(126, 512)]
        TP = [A(8 + i, CH) for i in range(4)]
        ABX, ABT = A3(108, NT, 512), A(12, 512)
        TB = [A(24, T), A(26, T)]
        WZ = [A3(16 * j, KD, CH) for j in range(3)]
        WF = [A(40, 512, FILT_HID), A(42, 512, FILT_HID)]
        DL = [A(44, 512), A(46, 512)]
        Y2T = H[:, :, :].rearrange("p m (a t) -> p (m a) t", a=2)
        FEAT = A(100, T, FILT_EMB)
        CWR = A(102, P, 112)
        W1 = A(103, FILT_HID, FILT_EMB)
        W2 = A(103.5, FILT_HID, FILT_HID)
        FA, FN = A(104, T, FILT_HID), A(106, T, FILT_HID)
        A1T = A(108, T, FILT_HID)
        cols = sm[:, 0:112]
        fcol = sm[0:FILT_HID, 112:115]
        rl = sm[:, 120:124]
        TWO_PI = 2.0 * math.pi
        PI_HI, MAGIC = 6.28125, 12582912.0

        def sp_hyena(sp):
            for w, src in ((FEAT, c_feats), (CWR[0:72, :], conv_w[0].rearrange("j (c p) -> (j c) p", p=P)),
                           (CWR[72:96, :], conv_b.rearrange("a (c p) -> (a c) p", p=P)),
                           (CWR[96:112, :], filt_bias[0].rearrange("o (c p) -> (o c) p", p=P)),
                           (W1, filt_w1[0]), (W2, filt_w2[0]),
                           (fcol[:, 0:1], filt_b1.rearrange("a (p b) -> p (a b)", b=1)),
                           (fcol[:, 1:2], filt_b2.rearrange("a (p b) -> p (a b)", b=1)),
                           (fcol[:, 2:3], filt_freq.rearrange("a (p b) -> p (a b)", b=1))):
                sp.dma_start(w, src).then_inc(sem("hy_in"), 16)
            sp.wait_ge(sem("moe_done"), 1)
            sp.wait_ge(sem("cadd"), NT * TOP_K - 10)
            for i in range(4):
                sp.dma_start(DFT[i], c_dft[:, i, :, :]).then_inc(sem("dft_in"), 16)

            def quarter(q):
                wait(sp, "z_mm", q * 6)
                wz = w_in_c[0].rearrange("(p k) (j q c) -> p q k j c", k=KD, j=3, q=HY_Q)[:, bass.ds(q, 1), :, :, :]
                for j in range(3):
                    sp.dma_start(WZ[j], wz[:, :, :, j, :].rearrange("p a k c -> p (a k) c")).then_inc(sem("wz_in"), 16)
                wait(sp, "hf_mm", q * 8)
                wait(sp, "win", q * 8)
                w3 = filt_w3[0].rearrange("h (o b q c) -> h q o b c", o=2, b=2, q=HY_Q)[:, bass.ds(q, 1), :, :, :]
                dl = filt_delta.rearrange("a (o b q c) -> a q o b c", o=2, b=2, q=HY_Q)[:, bass.ds(q, 1), :, :, :]
                for o in range(2):
                    for b in range(2):
                        c = slice(b * CH, (b + 1) * CH)
                        sp.dma_start(WF[o][:, c], w3[:, :, o, b, :].rearrange("h a c -> h (a c)")).then_inc(sem("wf_in"), 16)
                        sp.dma_start(DL[o][:, c], dl[:, :, o, b, :].rearrange("a q c -> a (q c)").to_broadcast([P, CH])) \
                            .then_inc(sem("wf_in"), 16)

            quarter(0)
            sp.wait_ge(sem("layer_start"), NT)
            sp.dma_start(MODR[:, 5 * D:6 * D], mod_dram[:, 5 * D:6 * D].to_broadcast([P, D])).then_inc(sem("bmod_in"), 16)
            with sp.Fori(1, HY_Q) as i:
                quarter(i)

        def pe_filter_net(pe):
            wait(pe, "hy_in", 144)
            wait(pe, "moe_done", 1)
            pe.transpose(ps[:, 1, 0:112], CWR, ident[0:112, 0:112]).then_inc(sem("cols_tp"), 1)
            pe.matmul(ps[0:FILT_HID, 0, :], W1, FEAT, start=True, stop=True).then_inc(sem("f_mm"), 1)
            wait(pe, "f_sin", 1)
            pe.matmul(ps[0:FILT_HID, 0, :], W2, A1T, start=True, stop=True).then_inc(sem("f_mm"), 1)

        def act_filter_net(act):
            for i, dst in enumerate((A1T, A2T)):
                wait(act, "f_arg", i + 1)
                act.activation(dst, FA, ACT.Sin).then_inc(sem("f_sin"), 1)

        def dve_filter_net(dve, v):
            wait(dve, "hy_in", 144)
            wait(dve, "moe_done", 1)
            wait(dve, "cols_tp", 1)
            dve.tensor_copy(cols, ps[:, 1, 0:112]).then_inc(sem("cols_ev"), 1)
            for i in range(2):
                wait(dve, "f_mm", i + 1)
                if i:
                    wait(dve, "f_sin", i)
                v(dve.tensor_scalar(FA, ps[0:FILT_HID, 0, :], fcol[:, i:i + 1], fcol[:, 2:3], ALU.add, ALU.mult))
                v.sync()
                v(dve.tensor_scalar(FN, FA, 1.0 / TWO_PI, MAGIC, ALU.mult, ALU.add))
                v.sync()
                v(dve.tensor_scalar(FN, FN, -MAGIC, None, ALU.add))
                v.sync()
                for part in (PI_HI, TWO_PI - PI_HI):
                    v(dve.scalar_tensor_tensor(FA, FN, -part, FA, ALU.mult, ALU.add))
                    v.sync()
                top = float(np.nextafter(np.float32(math.pi), np.float32(0)))
                dve.tensor_scalar(FA, FA, top, -top, ALU.min, ALU.max).then_inc(sem("f_arg"), 1)

        def pe_hyena(pe):
            wait(pe, "f_sin", 2)
            wait(pe, "turned", 2 * before["n2_1"])
            wait(pe, "dft_in", 64)
            def quarter(q):
                for o in range(2):
                    u = q * 2 + o
                    wait(pe, "wf_in", q * 128 + 128)
                    wait(pe, "ky_act", u * 8)
                    for t in range(NT):
                        pe.matmul(ps[:, t, :], A2T[:, t * P:(t + 1) * P], WF[o], start=True, stop=True) \
                            .then_inc(sem("hf_mm"), 1)
                    if o == 0:
                        wait(pe, "wz_in", q * 48 + 48)
                        wait(pe, "yn", q * 4)
                        for t in range(6):
                            if t < NT:
                                wait(pe, "hfw", u * 4 + t + 1)
                            j, ct = t // 2, t % 2
                            for k in range(KD):
                                mm = pe.matmul(ps[:, t, :], WZ[j][:, k, ct * P:(ct + 1) * P], HT[:, k, :],
                                               start=k == 0, stop=k == KD - 1)
                            mm.then_inc(sem("z_mm"), 1)
                        wait(pe, "z_dve", q * 6 + 2)
                    else:
                        wait(pe, "yn", q * 4 + 2)
                    wait(pe, "yt_act", u * 2)
                    wait(pe, "rl1", u)
                    for b in range(2):
                        for t in range(2 * b, 2 * b + 2):
                            for ct in range(2):
                                at = (t % 2) * CH + ct * P
                                mm = pe.transpose(ps[:, 6 + b, at:at + P], ZB[0][:, ct, t * P:(t + 1) * P], ident)
                        mm.then_inc(sem("yt_mm"), 1)
                    wait(pe, "l1sum", u + 1)
                    wait(pe, "yt_act", u * 2 + 2)
                    for ct in range(2):
                        for b in range(2):
                            mm = pe.matmul(ps[:, 7, ct:ct + 1], ABT[:, b * CH + ct * P:b * CH + (ct + 1) * P], ones[:, 0:1],
                                           start=b == 0, stop=b == 1)
                    mm.then_inc(sem("l1_mm"), 1)
                    wait(pe, "sd", u * 2 + 2)
                    wait(pe, "yt_dup", u + 1)
                    if o == 0:
                        wait(pe, "z_dve", q * 6 + 6)
                    else:
                        wait(pe, "hfw", u * 4 + 4)
                    for f in range(NT):
                        if f >= 2:
                            wait(pe, "ky_act", u * 8 + 2 * (f - 1))
                        for i, (table, data) in enumerate(((MC, R1), (MS, R2))):
                            for t in range(NT):
                                mm = pe.matmul(ps[:, 2 * (f % 2) + i, :], table[:, t, f * P:(f + 1) * P], data[:, t, :],
                                               start=t == 0, stop=t == NT - 1)
                            mm.then_inc(sem("ky_mm"), 1)
                    wait(pe, "pp", u * 4 + 4)
                    if o == 1:
                        wait(pe, "yn", q * 4 + 2)
                    for ct in range(2):
                        for i, table in enumerate((IC, IS)):
                            for f in range(NT):
                                mm = pe.matmul(ps[:, 4 + ct, :], PP[:, f, i * CH + ct * P:i * CH + (ct + 1) * P],
                                               table[:, f, :], start=i + f == 0, stop=i + f == NT)
                        mm.then_inc(sem("iv_mm"), 1)

            quarter(0)
            with pe.Fori(1, HY_Q) as i:
                quarter(i)

        def act_hyena(act):
            wait(act, "cols_ev", 1)
            def quarter(q):
                for o in range(2):
                    u = q * 2 + o
                    wait(act, "wf_in", q * 128 + 128)
                    act.activation(DL[o], DL[o], ACT.Abs).then_inc(sem("act_chain"), 1)
                    wait(act, "act_chain", u + 33)
                    for t in range(NT):
                        wait(act, "hfw", u * 4 + max(t - 1, 0))
                        act.activation(WIN[t % 2], DL[o], ACT.Exp, scale=K[:, C_T01 + t:C_T01 + t + 1]).then_inc(sem("win"), 1)
                    if o == 0:
                        wait(act, "yn", q * 4)
                        wait(act, "iv_act", q * 4)
                        for t in range(6):
                            j, ct = t // 2, t % 2
                            wait(act, "z_mm", q * 6 + t + 1)
                            act.activation(ZB[j][:, ct, :], ps[:, t, :], ACT.Identity,
                                           bias=col(72 + j * 8 + ct, q), scale=col(24 + j * 8 + ct, q)).then_inc(sem("z_act"), 1)
                    wait(act, "ky_mm", u * 8)
                    wait(act, "yt_dup", u)
                    for b in range(2):
                        wait(act, "yt_mm", u * 2 + b + 1)
                        act.activation(R1[:, 2 * b:2 * b + 2, CH:2 * CH], ps[:, 6 + b, :].rearrange("p (t c) -> p t c", t=2), ACT.Copy) \
                            .then_inc(sem("yt_act"), 1)
                    for f in range(NT):
                        wait(act, "pp", u * 4 + max(f - 1, 0))
                        for i, dst in enumerate((AS, BS)):
                            wait(act, "ky_mm", u * 8 + 2 * f + i + 1)
                            act.activation(dst[:, f % 2, :], ps[:, 2 * (f % 2) + i, :], ACT.Copy).then_inc(sem("ky_act"), 1)
                    wait(act, "yn", u * 2)
                    for ct in range(2):
                        act.activation(TB[ct], ZB[0][:, ct, :], ACT.Copy, scale=col(96 + o * 8 + ct, q)).then_inc(sem("iv_act"), 1)

            quarter(0)
            with act.Fori(1, HY_Q) as i:
                quarter(i)

        def col(base, q):
            return cols[:, bass.ds(q * 2 + base, 1)]

        def dve_hyena(dve, v):
            wait(dve, "cols_ev", 1)
            def quarter(q):
                for o in range(2):
                    u = q * 2 + o
                    wait(dve, "iv_mm", u * 2)
                    for t in range(NT):
                        wait(dve, "hf_mm", u * 4 + t + 1)
                        wait(dve, "win", u * 4 + t + 1)
                        dve.scalar_tensor_tensor(HF[:, t, :], WIN[t % 2], DECAY_SHIFT, ps[:, t, :], ALU.add, ALU.mult) \
                            .then_inc(sem("hfw"), 1)
                    wait(dve, "hfw", u * 4 + 4)
                    wait(dve, "sd", u * 2)
                    v(dve.memset(HF[0:1, 0, CH:2 * CH], 0.0))
                    v.sync()
                    wait(dve, "l1_mm", u)
                    wait(dve, "pp", u * 4)
                    v(dve.scalar_tensor_tensor(ABX, HF, -1.0, HF, ALU.mult, ALU.max))
                    v.sync()
                    dve.tensor_reduce(ABT, ABX.rearrange("p t c -> p c t"), AX, ALU.add).then_inc(sem("l1sum"), 1)
                    if o == 0:
                        for t in range(6):
                            j, ct = t // 2, t % 2
                            z = ZB[j][:, ct, :]
                            wait(dve, "z_act", q * 6 + t + 1)
                            v(dve.scalar_tensor_tensor(z[:, 1:T], ps[:, t, 0:T - 1], col(j * 8 + ct, q), z[:, 1:T],
                                                       ALU.mult, ALU.add))
                            v.sync()
                            dve.scalar_tensor_tensor(z[:, 0:T - 1], ps[:, t, 1:T], col(48 + j * 8 + ct, q), z[:, 0:T - 1],
                                                     ALU.mult, ALU.add).then_inc(sem("z_dve"), 1)
                    wait(dve, "ky_mm", u * 8)
                    wait(dve, "yt_act", u * 2 + 2)
                    dve.tensor_copy(R2[:, :, CH:2 * CH], R1[:, :, CH:2 * CH]).then_inc(sem("yt_dup"), 1)
                    wait(dve, "l1_mm", u + 1)
                    wait(dve, "yn", u * 2)
                    dve.reciprocal(rl[:, 2 * o:2 * o + 2], ps[:, 7, 0:2]).then_inc(sem("rl1"), 1)
                    wait(dve, "sd", u * 2 + 2)
                    for f in range(NT):
                        a, b = AS[:, f % 2, :], BS[:, f % 2, :]
                        wait(dve, "ky_act", u * 8 + 2 * f + 2)
                        wait(dve, "pp", u * 4 + f)
                        for i, (x0, x1) in enumerate(((a[:, 0:CH], a[:, CH:]), (b[:, 0:CH], b[:, CH:]),
                                                      (a[:, 0:CH], b[:, CH:]), (b[:, 0:CH], a[:, CH:]))):
                            v(dve.tensor_tensor(TP[i], x0, x1, ALU.mult))
                        v.sync()
                        v(dve.tensor_tensor(PP[:, f, 0:CH], TP[0], TP[1], ALU.subtract))
                        v.sync()
                        dve.tensor_tensor(PP[:, f, CH:2 * CH], TP[2], TP[3], ALU.add).then_inc(sem("pp"), 1)
                    wait(dve, "rl1", u + 1)
                    for ct in range(2):
                        wait(dve, "iv_mm", u * 2 + ct + 1)
                        wait(dve, "iv_act", u * 2 + ct + 1)
                        v(dve.scalar_tensor_tensor(TB[ct], ps[:, 4 + ct, :], rl[:, 2 * o + ct:2 * o + ct + 1], TB[ct],
                                                   ALU.mult, ALU.add))
                        v.sync()
                        dst = ZB[0][:, ct, :] if o == 0 else Y2T[:, bass.ds(q * 2 + ct, 1), :].rearrange("p a t -> p (a t)")
                        dve.tensor_tensor(dst, TB[ct], ZB[1 + o][:, ct, :], ALU.mult).then_inc(sem("yn"), 1)

            quarter(0)
            with dve.Fori(1, HY_Q) as i:
                v.enter(i - 1, 6 + 2 * (1 + 1 + 20 + 2))
                quarter(i)
            v.leave(HY_Q - 1)

        def pool_hyena(pool):
            def quarter(q):
                for o in range(2):
                    u = q * 2 + o
                    wait(pool, "l1sum", u + 1)
                    wait(pool, "ky_mm", u * 8)
                    for dst, op in ((R1, ALU.add), (R2, ALU.subtract)):
                        pool.tensor_tensor(dst[:, :, 0:CH], HF[:, :, 0:CH], HF[:, :, CH:2 * CH], op).then_inc(sem("sd"), 1)

            quarter(0)
            with pool.Fori(1, HY_Q) as i:
                quarter(i)
        def sp_moe(sp, l):
            sp_dense(sp, W_SH[l][0])
            sp_dense(sp, W_SH[l][1])
            sp.wait_ge(sem("yo_mm"), l * 8 + 8)
            if l == 0:
                sp.wait_ge(sem("o_dve"), 32)
            sp.dma_start(GROW, norm_g[l, 1:2, :].to_broadcast([P, D])).then_inc(sem("norm_row_in"), 16)
            sp_router(sp, l)
            sp.wait_ge(sem("h"), before[f"n2_{l}"] + NT)
            sp.dma_start(h2_dram[l].rearrange("(m p) d -> p m d", p=P), H[:, :, :]).then_inc(sem("h2_stored"), 16)
            sp_experts(sp, l)

        def act_moe(act, a, l):
            act.wait_ge(sem("yo_dve"), l * 8 + 8)
            act_norm_sq(act, a, f"n2_{l}", X, NT, G2T)
            turned(act, lambda o, i: act.activation(o, i, ACT.Copy), HT, "tp", "turned", NT, 0, f"n2_{l}")
            act_router(act, a, l)
            act.wait_ge(sem("h2_stored"), 16 * (l + 1))
            act_shared(act, a, l)
            act_experts(act, a, l)

        def pe_moe(pe, l):
            pe.wait_ge(sem("yo_dve"), l * 8 + 8)
            pe_turn(pe, H, "tp", NT, norm=f"n2_{l}")
            pe_router(pe, l)
            pe_shared(pe, l, range(0, 2))
            pe_positions(pe, l)
            pe_shared(pe, l, range(2, NT))
            pe.wait_ge(sem("consts_made"), 2)
            pe_token_ids(pe, l, 0, 0)
            pe_token_ids(pe, l, 1, 1)
            pe_shared(pe, l, None)
            pe_experts(pe, l)

        def dve_moe(dve, v, l):
            dve.wait_ge(sem("norm_row_in"), 16 * (2 + 2 * l))
            dve_norm(dve, v, f"n2_{l}", X, NT, MODR[:, 4 * D:5 * D], MODR[:, 3 * D:4 * D], H, GROW, G2T)
            turned(dve, dve.tensor_copy, HT, "tp", "turned", NT, 1, f"n2_{l}")
            dve_select(dve, v, l)
            dve.wait_ge(sem("slots"), l + 1)
            dve_one_hot(dve, l, 0, 0, POSM[:, :, 0:1], K[:, C_IOTA:C_IOTA + P], False)
            dve_one_hot(dve, l, 1, 1, POSM[:, :, 1:2], K[:, C_IOTA:C_IOTA + P], False)
            dve_shared(dve, v, l, range(0, 2))
            dve_token_ids(dve, l, 0, 0, None)
            dve_token_ids(dve, l, 1, 1, None)
            dve_shared(dve, v, l, range(2, NT))
            dve.wait_ge(sem("sha"), l * NT + NT)
            dve.wait_ge(sem("h2_stored"), 16 * (l + 1))
            dve_shared(dve, v, l, None)
            dve_experts(dve, v, l)
            if l == 0:
                dve_filter_net(dve, v)
            dve_combine(dve, v, l)

        @block.sync
        def _(sp):
            sp_setup(sp)
            for n in range(3, W_MOD[1][0]):
                sp_dense(sp, n)
                if n == 5:
                    sp_layer0(sp)
                if n == W_U:
                    sp.wait_ge(sem("h"), before["n2_0"])
                    sp.dma_start(WSR, w_spatial[0].rearrange("g i j -> i g j")).then_inc(sem("ws_in"), 16)
            for n in W_MOD[1][:3]:
                sp_dense(sp, n)
            sp.wait_ge(sem("sg_done"), SG_G)
            sp.dma_start(BROW, b_mod[1:2, :]).then_inc(sem("bmod_in"), 16)
            sp_zero_rows(sp)
            for n in W_MOD[1][3:]:
                sp_dense(sp, n)
            sp.wait_ge(sem("mod_add"), 28)
            sp.dma_start(mod_dram, BROW).then_inc(sem("mod_stored"), 16)
            for n in W_OUT[0]:
                sp_dense(sp, n)
            sp_moe(sp, 0)
            sp.wait_ge(sem("mod_stored"), 16)
            sp.dma_start(MODR[:, 0:5 * D], mod_dram[:, 0:5 * D].to_broadcast([P, 5 * D])).then_inc(sem("bmod_in"), 16)
            sp.dma_start(GROW, norm_g[1, 0:1, :].to_broadcast([P, D])).then_inc(sem("norm_row_in"), 16)
            sp_hyena(sp)
            sp.wait_ge(sem("yn"), 16)
            for n in W_OUT[1]:
                sp_dense(sp, n)
            sp_moe(sp, 1)
            sp.wait_ge(sem("h"), before["fin"])
            sp.dma_start(GROW, final_g.rearrange("(a d) -> a d", a=1).to_broadcast([P, D])).then_inc(sem("norm_row_in"), 16)
            for m in range(NT):
                sp.wait_ge(sem("h"), before["fin"] + m + 1)
                sp.dma_start(out[0].rearrange("(m p) d -> p m d", p=P)[:, m, :], H[:, m, :]).then_inc(sem("out_stored"), 16)
            sp.wait_ge(sem("out_stored"), 16 * NT)

        @block.scalar
        def _(act):
            a = Chain(act, sem("act_chain"))
            act_setup(act, a)
            act.wait_ge(sem("x_in"), 32)
            act_norm_sq(act, a, "n1_0", X, NT, tmpn)
            turned(act, lambda o, i: act.activation(o, i, ACT.Copy), HT, "tp", "turned", NT, 0, "n1_0")
            act_norm_sq(act, a, "nc_0", CX, NC, tmpn)
            turned(act, lambda o, i: act.activation(o, i, ACT.Copy), HCT, "tp", "turned", NC, 0, "nc_0")
            act_project(act, a)
            act_spatial(act, a)
            act_attention(act, a)
            act.wait_ge(sem("zeroed"), 16)
            turned(act, lambda o, i: act.activation(o, i, ACT.Copy), HT, "mt_tp", "mt_turned", NT, 0)
            act_moe(act, a, 0)
            act_filter_net(act)
            act_norm_sq(act, a, "n1_1", X, NT, tmpn)
            turned(act, lambda o, i: act.activation(o, i, ACT.Copy), HT, "tp", "turned", NT, 0, "n1_1")
            act_hyena(act)
            act_moe(act, a, 1)
            act_norm_sq(act, a, "fin", X, NT, tmpn)

        @block.tensor
        def _(pe):
            pe.wait_ge(sem("consts_in"), 48)
            pe_mod(pe)
            pe.wait_ge(sem("mod_add"), 16)
            pe_turn(pe, H, "tp", NT, norm="n1_0")
            pe.wait_ge(sem("turned"), 2 * NT)
            pe_turn(pe, HC, "tp", NC, norm="nc_0")
            pe_project(pe)
            pe_turn_qk(pe)
            pe_spatial(pe)
            pe_attention(pe)
            pe.wait_ge(sem("o_dve"), 32)
            pe_turn(pe, MIX, "mt_tp", NT, strided=True)
            pe_out(pe, 0, HT)
            pe_moe(pe, 0)
            pe_filter_net(pe)
            pe.wait_ge(sem("cols_ev"), 1)
            pe.wait_ge(sem("f_arg"), 2)
            pe_turn(pe, H, "tp", NT, norm="n1_1")
            pe_hyena(pe)
            pe_out(pe, 1, Y2T)
            pe_moe(pe, 1)

        @block.vector
        def _(dve):
            v = Chain(dve, sem("dve_chain"))
            dve_setup(dve, v)
            dve_cond(dve, v)
            dve_mod(dve, v)
            dve.wait_ge(sem("norm_row_in"), 16)
            dve_norm(dve, v, "n1_0", X, NT, MODR[:, D:2 * D], MODR[:, 0:D], H, GROW, tmpn)
            turned(dve, dve.tensor_copy, HT, "tp", "turned", NT, 1, "n1_0")
            dve_norm(dve, v, "nc_0", CX, NC, MODC[:, D:2 * D], MODC[:, 0:D], HC, GROW, tmpn)
            turned(dve, dve.tensor_copy, HCT, "tp", "turned", NC, 1, "nc_0")
            dve_project(dve, v)
            dve_turn_qk(dve, v)
            dve_spatial(dve, v)
            dve_attention(dve, v)
            dve.wait_ge(sem("zeroed"), 16)
            turned(dve, dve.tensor_copy, HT, "mt_tp", "mt_turned", NT, 1)
            dve_out(dve, v, 0, G2T)
            dve_moe(dve, v, 0)
            dve.wait_ge(sem("bmod_in"), 64)
            dve.wait_ge(sem("norm_row_in"), 48)
            dve_norm(dve, v, "n1_1", X, NT, MODR[:, D:2 * D], MODR[:, 0:D], H, GROW, tmpn)
            turned(dve, dve.tensor_copy, HT, "tp", "turned", NT, 1, "n1_1")
            dve_hyena(dve, v)
            dve_out(dve, v, 1, G2T)
            dve_moe(dve, v, 1)
            dve.wait_ge(sem("norm_row_in"), 80)
            dve_norm(dve, v, "fin", X, NT, None, None, H, GROW, tmpn)

        @block.gpsimd
        def _(pool):
            pool.wait_ge(sem("gu_mm"), 2 * NT)
            pool.memset(ZERO, 0.0).then_inc(sem("zero_ready"), 1)
            pool_experts(pool, 0)
            pool_hyena(pool)
            pool_experts(pool, 1)


_INS = ["x", "c", "ctx", "c_ctx", "w_mod", "b_mod", "norm_g", "w_in_ab", "sink", "w_spatial", "b_spatial", "w_out_ab",
        "w_in_c", "conv_w", "conv_b", "filt_w1", "filt_b1", "filt_w2", "filt_b2", "filt_w3", "filt_freq", "filt_delta",
        "filt_bias", "w_out_c", "w_router", "e_bias", "w_gate", "w_up", "w_down", "ws_gate", "ws_up", "ws_down", "final_g"]


def kernel(**inputs):
    import concourse.bacc as _bacc
    from concourse.bass_utils import run_bass_kernel_spmd as _run

    nc = _bacc.Bacc("TRN2", target_bir_lowering=False, num_devices=1)
    arrays, args = {}, []
    for name, a in list({n: inputs[n] for n in _INS}.items()) + list(constants().items()):
        a = np.ascontiguousarray(a)
        arrays[f"in_{name}"] = a
        args.append(nc.dram_tensor(f"in_{name}", a.shape, mybir.dt.from_np(a.dtype), kind="ExternalInput").ap())
    args.append(nc.dram_tensor("out_0", (1, T, D), F32, kind="ExternalOutput").ap())
    hybrid_backbone(nc, *args)
    r = _run(nc, [arrays], core_ids=[0])
    return r.results[0]["out_0"]
```

```python
import math
from contextlib import ExitStack

import numpy as np

import concourse.bass as bass
from concourse import mybir

F32 = mybir.dt.float32
BF16 = mybir.dt.bfloat16
I32 = mybir.dt.int32
ALU = mybir.AluOpType
ACT = mybir.ActivationFunctionType
AX = mybir.AxisListType.X

P = 128
D = 1024
T = 512
CTX = 256
GRID_W = 64
KD = D // P
NT = T // P
NC = CTX // P
BANK = 512
EPS = 1e-6

N_Q, N_KV, HD = 8, 2, 64
ROPE_F = HD // 4
WINDOW = 128
ATT_W = N_Q * HD
SG_G, SG_D = 8, 64
BIG = 1.0e30

HY_Q = 4
CH = D // HY_Q
FILT_EMB, FILT_HID, BANDS = 33, 64, 16
DECAY_SHIFT = 0.05

E = 64
TOP_K = 8
GROUPS = 8
TOPK_GROUPS = 4
FE = 256
ROUTED_SCALE = 2.5
OVER = T * TOP_K // P
NBLK = E + OVER
FEW = 8
ZPARTS = 8
CG = 6

C_ID, C_IOTA, C_TRI, C_LT, C_E128, C_T01, C_TID, C_END = 0, 128, 256, 384, 448, 512, 516, 524
R_MASK, R_COS, R_SIN, R_END = 0, 384, 640, 896


def constants():
    small = np.zeros((P, C_END), np.float32)
    p = np.arange(P)
    small[:, C_ID:C_ID + P] = np.eye(P)
    small[:, C_IOTA:C_IOTA + P] = p[None, :]
    small[:, C_TRI:C_TRI + P] = p[:, None] < p[None, :]
    g = np.arange(GROUPS)
    small[:, C_LT:C_LT + 64] = (g[None, :] < g[:, None]).reshape(1, 64)
    small[:, C_E128:C_E128 + E] = 128.0 * np.arange(E)[None, :]
    order = np.concatenate([np.arange(0, T, 2), np.arange(1, T, 2)])
    t = order.astype(np.float32).reshape(NT, P).T
    small[:, C_T01:C_T01 + NT] = -(t / np.float32(T - 1))
    small[:, C_TID:C_TID + 8:2] = p[:, None]
    small[:, C_TID + 1:C_TID + 8:2] = 128.0 * np.arange(NT)[None, :]

    rope = np.zeros((P, R_END), np.float32)
    q, j = np.arange(P)[:, None], np.arange(3 * P)[None, :] - P
    rope[:, R_MASK:R_MASK + 3 * P] = np.where(np.abs(q - j) <= WINDOW, 0.0, -BIG)
    inv = np.power(10000.0, -np.arange(ROPE_F, dtype=np.float32) / ROPE_F).astype(np.float32)
    tok = np.arange(T)
    for axis, pos in enumerate((tok // GRID_W, tok % GRID_W)):
        ang = (pos.astype(np.float32)[:, None] * inv).astype(np.float32)
        cos, sin = np.cos(ang).astype(np.float32), np.sin(ang).astype(np.float32)
        for m in range(NT):
            rows = slice(m * P, (m + 1) * P)
            c0, s0 = R_COS + m * HD + axis * 32, R_SIN + m * HD + axis * 32
            rope[:, c0:c0 + 16], rope[:, c0 + 16:c0 + 32] = cos[rows], cos[rows]
            rope[:, s0:s0 + 16], rope[:, s0 + 16:s0 + 32] = -sin[rows], sin[rows]

    n = np.arange(T, dtype=np.float32)
    bands = np.linspace(1e-4, BANDS - 1, BANDS, dtype=np.float32)
    ang = np.float32(2.0 * math.pi / T) * n[:, None] * bands[None, :]
    feats = np.concatenate([(n / np.float32(T - 1))[:, None], np.cos(ang), np.sin(ang)], 1)[order].T
    th = np.outer(order, np.arange(T // 2) + 0.5) * (math.pi / T)
    c, s = np.cos(th), np.sin(th)
    fwd = np.stack([c, s]).reshape(2, NT, P, T // 2).transpose(2, 0, 1, 3).reshape(P, 2, 2 * T)
    inv = (np.stack([c.T, s.T]) / T).reshape(2, NT // 2, P, T).transpose(2, 0, 1, 3).reshape(P, 2, 2 * T)
    dft = np.concatenate([fwd, inv], 1).astype(np.float32)
    return {"c_small": small, "c_rope": rope, "c_feats": np.ascontiguousarray(feats, np.float32),
            "c_dft": np.ascontiguousarray(dft)}


class Chain:

    def __init__(self, eng, sem):
        self.eng, self.sem, self.n, self.off = eng, sem, 0, 0

    def __call__(self, ins):
        ins.then_inc(self.sem, 1)
        self.n += 1

    def sync(self):
        self.eng.wait_ge(self.sem, self.off + self.n)

    def enter(self, i, stride):
        self.start, self.off, self.stride = self.n, i * stride, stride

    def leave(self, count):
        assert self.n - self.start == self.stride, self.n - self.start
        self.n, self.off = self.start + count * self.stride, 0


def hybrid_backbone(nc, x, c, ctx, c_ctx, w_mod, b_mod, norm_g, w_in_ab, sink, w_spatial, b_spatial,
                    w_out_ab, w_in_c, conv_w, conv_b, filt_w1, filt_b1, filt_w2, filt_b2, filt_w3,
                    filt_freq, filt_delta, filt_bias, w_out_c, w_router, e_bias, w_gate, w_up, w_down,
                    ws_gate, ws_up, ws_down, final_g, c_small, c_rope, c_feats, c_dft, out):
    h2_dram = [nc.dram_tensor(f"h2_rows_{l}", [T, D], F32, kind="Internal").ap() for l in range(2)]
    mod_dram = nc.dram_tensor("modulation_1", [1, 6 * D], F32, kind="Internal").ap()
    y_dram = nc.dram_tensor("expert_rows", [NBLK * P, D], F32, kind="Internal").ap()

    ctxs = ExitStack()
    with ctxs:
        def sb(name, shape, dt=F32):
            return ctxs.enter_context(nc.sbuf_tensor(name, shape, dt))

        sems = {}

        def sem(name):
            return sems[name]

        def wait(eng, name, value):
            if not (isinstance(value, int) and value <= 0):
                eng.wait_ge(sem(name), value)

        def make(*names):
            for n in names:
                sems[n] = ctxs.enter_context(nc.semaphore(n))

        X = sb("residual", [P, NT, D])
        MODR = sb("modulation_rows", [P, 6 * D])
        HT = sb("features_major", [P, KD, T])
        H = sb("token_major", [P, NT, D])
        arena = sb("arena", [P, 128 * 256])
        K = sb("constants", [P, C_END])
        ones = sb("ones", [P, P])
        tid = sb("token_ids", [P, 8], BF16)
        ss = sb("square_sums", [P, 32])
        sm = sb("small_columns", [P, 640])
        ps = ctxs.enter_context(nc.psum_tensor("ps", [P, 8, BANK], F32))

        def A(kb, n, parts=P):
            return arena[0:parts, int(kb * 256):int(kb * 256) + n]

        def A3(kb, a, b, parts=P):
            return A(kb, a * b, parts).rearrange("p (a b) -> p a b", a=a)

        ident = K[:, C_ID:C_ID + P]

        SLOTS = 3
        dense = []

        def rows8(w, lo, n):
            return w.rearrange("(p k) n -> p k n", k=KD)[:, :, lo:lo + n]

        def add(*parts):
            dense.append(parts)
            return len(dense) - 1

        def slot(n, k, w, at=0):
            base = (n % SLOTS) * 16
            return A3(base, k, w) if at == 0 else None

        W_MOD = [[], []]
        for n in range(12):
            W_MOD[0].append(add((0, KD, 512, rows8(w_mod[0], n * 512, 512), 0, 512)))
        W_KV = add((0, KD, 512, rows8(w_in_ab[0], 512, 256), 0, 256))
        W_Q = add((0, KD, 512, rows8(w_in_ab[0], 0, 512), 0, 512))
        W_G = add((0, KD, 512, rows8(w_in_ab[0], 1280, 512), 0, 512))
        W_U = add((0, KD, 512, rows8(w_in_ab[0], 768, 512), 0, 512))
        W_OUT = [[], []]
        W_SH = [None, None]
        for n in range(12):
            W_MOD[1].append(add((0, KD, 512, rows8(w_mod[1], n * 512, 512), 0, 512)))
        for n in range(2):
            W_OUT[0].append(add((0, KD, 512, rows8(w_out_ab[0], n * 512, 512), 0, 512)))

        def add_shared(l):
            a = add((0, KD, 512, rows8(ws_gate[l], 0, FE), 0, FE), (0, KD, 512, rows8(ws_up[l], 0, FE), FE, 2 * FE))
            b = add((0, 2, D, ws_down[l].rearrange("(p k) n -> p k n", k=2), 0, D))
            W_SH[l] = (a, b)

        add_shared(0)
        for n in range(2):
            W_OUT[1].append(add((0, KD, 512, w_out_c[0].rearrange("(k p) n -> p k n", p=P)[:, :, n * 512:(n + 1) * 512], 0, 512)))
        add_shared(1)
        landed = []
        total = [0] * SLOTS
        for n, parts in enumerate(dense):
            total[n % SLOTS] += 16 * len(parts)
            landed.append(total[n % SLOTS])

        make("x_in", "consts_in", "bmod_in", "norm_row_in", "consts_made", "dense_used",
             "silu_c", "cond_cols", "dve_chain", "act_chain", "h2_stored", "layer_start")
        for s in range(SLOTS):
            make(f"dense_landed_{s}")
        make("mod_mm", "mod_add", "mod_stored")
        NORMS = ["n1_0", "nc_0", "n2_0", "n1_1", "n2_1", "fin"]
        FM = [HT, H[:, :, :].rearrange("p m (a t) -> p (m a) t", a=2)]
        TM = [H, HT[:, :, :].rearrange("p (m a) t -> p m (a t)", a=2)]
        make("sq", "ms", "rt", "h", "tp", "turned")
        tiles_of = dict(zip(NORMS, (NT, NC, NT, NT, NT, NT)))
        before = {n: sum(tiles_of[m] for m in NORMS[:i]) for i, n in enumerate(NORMS)}
        stat_steps = {n: NT if n.startswith("n2") else 1 for n in NORMS}
        stats = {n: sum(stat_steps[m] for m in NORMS[:i]) for i, n in enumerate(NORMS)}
        make("row_used", "tables_in", "ws_in", "kv_mm", "kv_act", "kv_dve", "q_mm", "q_dve",
             "gu_mm", "gu_act", "qk_tp", "qk_ev", "ws_tp", "ws_ev", "sg_ln", "sg_sq", "sg_ms", "sg_rt", "sg_mm", "sg_done",
             "s_mm", "s_dve", "s_act", "s_max", "p_act", "pt_mm", "pt_out", "o_mm", "o_dve",
             "mt_tp", "mt_turned", "yo_mm", "yo_dve")
        for l in range(2):
            make(*[f"{n}_{l}" for n in (
                "wgu0", "wgu1", "wd0", "wd1", "oh", "tok_mm", "tok", "xg0", "xg1", "xt_mm", "xt_out", "gu_m",
                "silu", "a", "at_mm", "at", "y_mm", "y_out", "yst0", "yst1", "next_range")])
        make("lg_mm", "score", "eb_in", "sel", "pos_mm", "slots", "tables", "shgu_mm", "shsilu", "sha", "shat_mm", "shat",
             "shy_mm", "shy_act", "shy_dve", "cadd", "moe_done")
        make(*[f"cg{b}" for b in range(CG)])
        make("out_stored", "rows_asked", "over_stored_0", "over_stored_1", "zero_ready", "zeroed")
        for n in ("hy_in", "f_mm", "f_arg", "f_sin", "wz_in_0", "wz_in_1", "wz_in_2", "wf_in", "dft_in",
                  "z_mm", "z_act", "z_dve", "yt_mm", "yt_act", "yt_dup", "win", "hf_mm", "hfw", "l1sum", "l1_mm", "rl1", "sd",
                  "ky_mm", "ky_act", "ky_dve", "pp", "iv_mm", "iv_act", "yn"):
            make(n)

        block = ctxs.enter_context(nc.Block())

        cbc = A3(48, KD, P)
        ccbc = A3(52, KD, P)
        MODC = A(56, 2 * D)
        CX = A3(64, NC, D)
        HC = A3(72, NC, D)
        HCT = A3(80, KD, CTX)
        GROW = A(88, D)
        tmpn = [A(92, D), A(96, D)]
        RP = A(100, R_END)
        Q = A3(104, NT, ATT_W)
        VG = A3(112, NT, 512)
        UG = A3(120, NT, 512)
        V = A3(48, NT, P)
        VC = A3(50, NC, P)
        KDUP = A3(52, NT, 2 * P)
        KCDUP = A3(62, NC, 2 * P)
        QT = A3(64, 4, T)
        KT = A3(72, 2, T)
        KCT = A3(76, 2, CTX)
        SS = [A(80, 640), A(82.5, 640)]
        PB = [A(85, 640), A(87.5, 640)]
        PT = [A(56, 640), A(58.5, 640)]
        WST = A3(92, SG_G, P)
        WSR = A3(96, SG_G, P)
        SGT = MODR[:, 0:2048]
        MIX = H
        ZERO = HT[:, 0:2, :].rearrange("p k t -> p (k t)")
        BROW = A(104, 6 * D, 1)
        ccol = sm[:, 0:16]
        sinkb = sm[:, 16:24]
        bsr = sm[0:SG_G, 24:152]
        bsc = sm[:, 152:160]
        acol = sm[:, 160:192]
        mxc = sm[:, 192:224]
        nmc = sm[:, 224:256]
        rsc = sm[:, 256:288]
        esc = sm[:, 288:320]
        dnc = sm[:, 320:352]
        rcc = sm[:, 352:384]
        sgm = sm[:, 384:416]
        sgv = sm[:, 416:448]

        def sp_setup(sp):
            sp.dma_start(ccol[:, 0:8], c.rearrange("a (p k) -> p (a k)", k=KD)).then_inc(sem("consts_in"), 16)
            sp.dma_start(ccol[:, 8:16], c_ctx.rearrange("(p k) -> p k", k=KD)).then_inc(sem("consts_in"), 16)
            sp.dma_start(K[:, :], c_small).then_inc(sem("consts_in"), 16)
            for n in range(3):
                sp_dense(sp, n)
            sp.dma_start(MODR[:, :], b_mod[0:1, :].to_broadcast([P, 6 * D])).then_inc(sem("bmod_in"), 16)
            sp.dma_start(MODC, b_mod[0:1, 0:2 * D].to_broadcast([P, 2 * D])).then_inc(sem("bmod_in"), 16)

        def sp_layer0(sp):
            sp.dma_start(X[:, :, :], x[0].rearrange("(m p) d -> p m d", p=P)).then_inc(sem("x_in"), 16)
            sp.dma_start(CX, ctx[0].rearrange("(m p) d -> p m d", p=P)).then_inc(sem("x_in"), 16)
            sp.dma_start(GROW, norm_g[0, 0:1, :].to_broadcast([P, D])).then_inc(sem("norm_row_in"), 16)
            sp.dma_start(RP, c_rope).then_inc(sem("tables_in"), 16)
            sp.dma_start(sinkb, sink.to_broadcast([P, N_Q])).then_inc(sem("tables_in"), 16)
            sp.dma_start(bsr, b_spatial[0]).then_inc(sem("tables_in"), 16)

        def sp_zero_rows(sp, part):
            sp.wait_ge(sem("zero_ready"), 1)
            n = OVER // ZPARTS
            rows = y_dram[(E + part * n) * P:(E + part * n + n) * P, :].rearrange("(b s) d -> s b d", s=P)
            sp.dma_start(rows, ZERO.unsqueeze(1).to_broadcast([P, n, D])).then_inc(sem("zeroed"), 16)

        def sp_dense(sp, n):
            if n >= SLOTS:
                sp.wait_ge(sem("dense_used"), n - SLOTS + 1)
            for (_, k, w, src, lo, hi) in dense[n]:
                base = (n % SLOTS) * 16
                if hi <= 1:
                    dst = A3(base, k, w, FILT_HID)[:, lo, :]
                else:
                    dst = A3(base, k, w)[:, :, lo:hi]
                sp.dma_start(dst, src).then_inc(sem(f"dense_landed_{n % SLOTS}"), 16)

        def W(n, k, w, parts=P):
            return A3((n % SLOTS) * 16, k, w, parts)

        def w_wait(pe, n):
            pe.wait_ge(sem(f"dense_landed_{n % SLOTS}"), landed[n])

        def act_setup(act, a):
            act.wait_ge(sem("consts_in"), 48)
            act.activation(sm[:, 0:16], sm[:, 0:16], ACT.Silu).then_inc(sem("silu_c"), 1)

        def dve_setup(dve, v):
            dve.memset(ones[:, :], 1.0).then_inc(sem("consts_made"), 1)
            dve.wait_ge(sem("consts_in"), 48)
            dve.tensor_copy(tid[:, :], K[:, C_TID:C_TID + 8]).then_inc(sem("consts_made"), 1)

        def dve_cond(dve, v):
            dve.wait_ge(sem("silu_c"), 1)
            for i, dst in enumerate((cbc, ccbc)):
                dve.tensor_copy(dst, ccol[:, 8 * i:8 * i + 8].unsqueeze(2).to_broadcast([P, KD, P])) \
                    .then_inc(sem("cond_cols"), 1)

        def pe_mod(pe):
            pe.wait_ge(sem("cond_cols"), 2)
            t = 0
            for n in range(12):
                w_wait(pe, W_MOD[0][n])
                w = W(W_MOD[0][n], KD, 512)
                for s in [cbc, ccbc] if n < 4 else [cbc]:
                    if t >= 8:
                        pe.wait_ge(sem("mod_add"), t - 7)
                    for k in range(KD):
                        mm = pe.matmul(ps[:, t % 8, :], s[:, k, :], w[:, k, :], start=k == 0, stop=k == KD - 1)
                    mm.then_inc(sem("mod_mm"), 1)
                    t += 1
                used(pe, "mod_mm", t)

        def pe_mod_1(pe, step):
            n, k = step // KD, step % KD
            if k == 0:
                w_wait(pe, W_MOD[1][n])
                pe.wait_ge(sem("mod_add"), 16 + n)
            mm = pe.matmul(ps[0:1, 7, :], ccol[:, k:k + 1], W(W_MOD[1][n], KD, 512)[:, k, :],
                           start=k == 0, stop=k == KD - 1)
            if k == KD - 1:
                mm.then_inc(sem("mod_mm"), 1)
                used(pe, "mod_mm", 16 + n + 1)

        def dve_mod_1(dve, n):
            if n == 0:
                dve.wait_ge(sem("bmod_in"), 48)
            dve.wait_ge(sem("mod_mm"), 16 + n + 1)
            d = BROW[:, n * 512:(n + 1) * 512]
            dve.tensor_tensor(d, ps[0:1, 7, :], d, ALU.add).then_inc(sem("mod_add"), 1)

        def used(pe, name, value):
            pe.wait_ge(sem(name), value)
            pe.sem_inc(sem("dense_used"), 1)

        MOD_0 = [(n, dst) for n in range(12) for dst in ([MODR, MODC] if n < 4 else [MODR])]

        def dve_mod(dve, steps):
            dve.wait_ge(sem("bmod_in"), 32)
            for t in steps:
                n, dst = MOD_0[t]
                dve.wait_ge(sem("mod_mm"), t + 1)
                d = dst[:, n * 512:(n + 1) * 512]
                dve.tensor_tensor(d, ps[:, t % 8, :], d, ALU.add).then_inc(sem("mod_add"), 1)
            dve.wait_ge(sem("mod_add"), t + 1)

        def stat_columns(n):
            return ss[:, 16:32] if n == "nc_0" else ss[:, 0:16]

        def act_norm_sq(act, a, n, src, nt, junk):
            s = stat_columns(n)
            for m in range(nt):
                if m >= 2:
                    act.wait_ge(sem("sq"), before[n] + m - 1)
                if n in ("n1_1", "fin"):
                    act.wait_ge(sem("layer_start"), NT * (1 + (n == "fin")) - NT + m + 1)
                act.activation(junk[m % 2], src[:, m, :], ACT.Square, accum_out=s[:, m:m + 1]) \
                    .then_inc(sem("sq"), 1)
            act.wait_ge(sem("ms"), stats[n] + 1)
            act.activation(s[:, 8:8 + nt], s[:, 4:4 + nt], ACT.Sqrt).then_inc(sem("rt"), 1)

        def dve_norm(dve, v, n, src, nt, rowA, rowB, dst, grow, tmp):
            s = stat_columns(n)
            dve.wait_ge(sem("sq"), before[n] + nt)
            dve.tensor_scalar(s[:, 4:4 + nt], s[:, 0:nt], 1.0 / D, EPS, ALU.mult, ALU.add).then_inc(sem("ms"), 1)
            if rowA is not None:
                dve.scalar_tensor_tensor(rowA, rowA, 1.0, grow, ALU.add, ALU.mult).then_inc(sem("row_used"), 1)
            dve.wait_ge(sem("rt"), stats[n] + 1)
            v(dve.reciprocal(s[:, 12:12 + nt], s[:, 8:8 + nt]))
            v.sync()
            if rowA is not None:
                dve.wait_ge(sem("row_used"), NORMS.index(n) + 1)
            for m in range(nt):
                r = s[:, 12 + m:13 + m]
                if rowA is None:
                    dve.scalar_tensor_tensor(dst[:, m, :], src[:, m, :], r, grow, ALU.mult, ALU.mult) \
                        .then_inc(sem("h"), 1)
                    continue
                v(dve.scalar_tensor_tensor(tmp[m % 2], src[:, m, :], r, rowA, ALU.mult, ALU.mult))
                v.sync()
                dve.tensor_tensor(dst[:, m, :].rearrange("p (k j) -> p j k", k=KD),
                                  tmp[m % 2].rearrange("p (j k) -> p j k", k=KD),
                                  rowB.rearrange("p (j k) -> p j k", k=KD), ALU.add).then_inc(sem("h"), 1)

        def pe_turn(pe, src, dst_sem, nt, strided=False, norm=None):
            for m in range(nt) if isinstance(nt, int) else nt:
                if norm is not None:
                    pe.wait_ge(sem("h"), before[norm] + m + 1)
                for kk in range(2):
                    for j in range(4):
                        k = 4 * kk + j
                        s = src[:, m, k:k + 8 * (P - 1) + 1:8] if strided else src[:, m, k * P:(k + 1) * P]
                        mm = pe.transpose(ps[:, 2 * m + kk, j * P:(j + 1) * P], s, ident)
                    mm.then_inc(sem(dst_sem), 1)

        def turned(eng, copy, dst, dst_sem, done, nt, kk, norm=None):
            for m in range(nt) if isinstance(nt, int) else nt:
                eng.wait_ge(sem(dst_sem), 2 * ((before[norm] if norm else 0) + m) + kk + 1)
                copy(dst[:, 4 * kk:4 * kk + 4, m * P:(m + 1) * P],
                     ps[:, 2 * m + kk, :].rearrange("p (k t) -> p k t", k=4)).then_inc(sem(done), 1)

        def pe_project(pe):
            w_wait(pe, W_KV)
            pe.wait_ge(sem("turned"), 2 * before["n2_0"])
            w = W(W_KV, KD, 512)
            for t in range(NT + NC):
                src = HT[:, :, t * P:(t + 1) * P] if t < NT else HCT[:, :, (t - NT) * P:(t - NT + 1) * P]
                for k in range(KD):
                    mm = pe.matmul(ps[:, t, 0:256], src[:, k, :], w[:, k, 0:256], start=k == 0, stop=k == KD - 1)
                mm.then_inc(sem("kv_mm"), 1)
            used(pe, "kv_mm", NT + NC)
            t = 0
            for n, name in ((W_Q, "q_mm"), (W_G, "gu_mm"), (W_U, "gu_mm")):
                w_wait(pe, n)
                w = W(n, KD, 512)
                for m in range(NT):
                    bank = (6 + t) % 8
                    if bank < 6 and t < 8:
                        pe.wait_ge(sem("kv_act"), bank + 1)
                        pe.wait_ge(sem("kv_dve"), bank + 1)
                    if t >= 8:
                        pe.wait_ge(sem("q_dve"), t - 7)
                    for k in range(KD):
                        mm = pe.matmul(ps[:, bank, :], HT[:, k, m * P:(m + 1) * P], w[:, k, :],
                                       start=k == 0, stop=k == KD - 1)
                    mm.then_inc(sem(name), 1)
                    t += 1
                used(pe, name, NT if name == "q_mm" or n == W_G else 2 * NT)

        def act_project(act, a):
            for t in range(NT + NC):
                act.wait_ge(sem("kv_mm"), t + 1)
                dst = V[:, t, :] if t < NT else VC[:, t - NT, :]
                act.activation(dst, ps[:, t, P:2 * P], ACT.Copy).then_inc(sem("kv_act"), 1)
            for i in range(2 * NT):
                if i == NT:
                    act.wait_ge(sem("sg_sq"), 1)
                    act.activation(SGT, VG, ACT.Square).then_inc(sem("sg_ms"), 1)
                    act.wait_ge(sem("sg_sq"), 2)
                    act.activation(sgm, sgv, ACT.Sqrt).then_inc(sem("sg_rt"), 1)
                act.wait_ge(sem("gu_mm"), i + 1)
                dst = VG[:, i, :] if i < NT else UG[:, i - NT, :]
                act.activation(dst, ps[:, (6 + NT + i) % 8, :], ACT.Gelu_apprx_tanh).then_inc(sem("gu_act"), 1)

        def rotate(dve, v, src, nh, m, outs):
            cos = RP[:, R_COS + m * HD:R_COS + (m + 1) * HD]
            sin = RP[:, R_SIN + m * HD:R_SIN + (m + 1) * HD]
            t1, t2 = SGT[:, 0:nh * HD], SGT[:, 512:512 + nh * HD]
            v.sync()
            v(dve.tensor_tensor(t1.rearrange("p (h d) -> p h d", h=nh), src.rearrange("p (h d) -> p h d", h=nh),
                                cos.unsqueeze(1).to_broadcast([P, nh, HD]), ALU.mult))
            for half in range(2):
                def part(ap, hf):
                    return ap.rearrange("p (h a b f) -> p h a b f", h=nh, a=2, b=2)[:, :, :, hf, :]
                s = sin.rearrange("p (a b f) -> p a b f", a=2, b=2)[:, :, half, :].unsqueeze(1) \
                    .to_broadcast([P, nh, 2, ROPE_F])
                v(dve.tensor_tensor(part(t2, half), part(src, 1 - half), s, ALU.mult))
            v.sync()
            for dst, done in outs:
                ins = dve.tensor_tensor(dst, t1.rearrange("p (h d) -> p h d", h=nh),
                                        t2.rearrange("p (h d) -> p h d", h=nh), ALU.add)
                if done is None:
                    v(ins)
                else:
                    ins.then_inc(sem(done), 1)

        def dve_project(dve, v):
            dve.wait_ge(sem("tables_in"), 48)
            for t in range(NT):
                dve.wait_ge(sem("kv_act"), t + 1)
                if t:
                    dve.wait_ge(sem("kv_dve"), t)
                kd = KDUP[:, t, :].rearrange("p (g r d) -> p g r d", g=2, r=2)
                rotate(dve, v, ps[:, t, 0:P], 2, t, [(kd[:, :, 0, :], None), (kd[:, :, 1, :], "kv_dve")])
            for t in range(NC):
                dve.wait_ge(sem("kv_act"), NT + t + 1)
                src = ps[:, NT + t, 0:P].rearrange("p (g d) -> p g d", g=2)
                kd = KCDUP[:, t, :].rearrange("p (g r d) -> p g r d", g=2, r=2)
                v(dve.tensor_copy(kd[:, :, 0, :], src))
                dve.tensor_copy(kd[:, :, 1, :], src).then_inc(sem("kv_dve"), 1)
            for m in range(NT):
                dve.wait_ge(sem("q_mm"), m + 1)
                dve.wait_ge(sem("kv_dve"), NT + NC)
                if m:
                    dve.wait_ge(sem("q_dve"), m)
                rotate(dve, v, ps[:, (6 + m) % 8, :], N_Q, m,
                       [(Q[:, m, :].rearrange("p (h d) -> p h d", h=N_Q), "q_dve")])

        def pe_turn_qk(pe):
            pe.wait_ge(sem("q_dve"), NT)
            pe.wait_ge(sem("kv_dve"), NT + NC)
            pe.wait_ge(sem("gu_act"), 2 * NT)
            for m in range(NT):
                for j in range(4):
                    mm = pe.transpose(ps[:, m, j * P:(j + 1) * P], Q[:, m, j * P:(j + 1) * P], ident)
                mm.then_inc(sem("qk_tp"), 1)
            for g in range(2):
                for m in range(NT):
                    mm = pe.transpose(ps[:, 4 + g, m * P:(m + 1) * P], KDUP[:, m, g * P:(g + 1) * P], ident)
                mm.then_inc(sem("qk_tp"), 1)
            for g in range(2):
                for m in range(NC):
                    i = g * NC + m
                    mm = pe.transpose(ps[:, 6, i * P:(i + 1) * P], KCDUP[:, m, g * P:(g + 1) * P], ident)
            mm.then_inc(sem("qk_tp"), 1)
            pe.wait_ge(sem("tables_in"), 48)
            pe.transpose(ps[:, 7, 0:SG_G], bsr, ident[0:SG_G, 0:SG_G]).then_inc(sem("qk_tp"), 1)

        def dve_turn_qk(dve, v):
            for m in range(NT):
                dve.wait_ge(sem("qk_tp"), m + 1)
                dve.tensor_copy(QT[:, :, m * P:(m + 1) * P], ps[:, m, :].rearrange("p (j t) -> p j t", j=4)) \
                    .then_inc(sem("qk_ev"), 1)
            for g in range(2):
                dve.wait_ge(sem("qk_tp"), NT + g + 1)
                dve.tensor_copy(KT[:, g, :], ps[:, 4 + g, :]).then_inc(sem("qk_ev"), 1)
            dve.wait_ge(sem("qk_tp"), NT + 3)
            dve.tensor_copy(KCT, ps[:, 6, :].rearrange("p (g t) -> p g t", g=2)).then_inc(sem("qk_ev"), 1)
            dve.wait_ge(sem("qk_tp"), NT + 4)
            dve.tensor_copy(bsc, ps[:, 7, 0:SG_G]).then_inc(sem("qk_ev"), 1)

        def pe_spatial(pe):
            pe.wait_ge(sem("qk_ev"), NT + 4)
            pe.wait_ge(sem("ws_in"), 16)
            for b in range(2):
                for j in range(4):
                    mm = pe.transpose(ps[:, b, j * P:(j + 1) * P], WSR[:, 4 * b + j, :], ident)
                mm.then_inc(sem("ws_tp"), 1)
            pe.wait_ge(sem("ws_ev"), 2)
            pe.wait_ge(sem("sg_ln"), 1)
            for g in range(SG_G):
                pe.matmul(ps[:, g, 0:NT * SG_D], WST[:, g, :], VG[:, :, g * SG_D:(g + 1) * SG_D],
                          start=True, stop=True).then_inc(sem("sg_mm"), 1)

        def act_spatial(act, a):
            for b in range(2):
                act.wait_ge(sem("ws_tp"), b + 1)
                act.activation(WST[:, 4 * b:4 * b + 4, :], ps[:, b, :].rearrange("p (g i) -> p g i", g=4), ACT.Copy) \
                    .then_inc(sem("ws_ev"), 1)

        def dve_gate_norm(dve, v):
            vg = VG.rearrange("p m (g d) -> p (m g) d", g=SG_G)
            dve.wait_ge(sem("gu_act"), NT)
            dve.wait_ge(sem("q_dve"), NT)
            v(dve.tensor_reduce(sgm, vg, AX, ALU.add))
            v.sync()
            v(dve.tensor_scalar(sgm, sgm, 1.0 / SG_D, None, ALU.mult))
            v.sync()
            dve.tensor_tensor(vg, vg, sgm.unsqueeze(2).to_broadcast([P, 32, SG_D]), ALU.subtract) \
                .then_inc(sem("sg_sq"), 1)
            dve.wait_ge(sem("sg_ms"), 1)
            v(dve.tensor_reduce(sgv, SGT.rearrange("p (g d) -> p g d", d=SG_D), AX, ALU.add))
            v.sync()
            dve.tensor_scalar(sgv, sgv, 1.0 / SG_D, EPS, ALU.mult, ALU.add).then_inc(sem("sg_sq"), 1)
            dve.wait_ge(sem("sg_rt"), 1)
            v(dve.reciprocal(sgv, sgm))
            v.sync()
            dve.wait_ge(sem("sg_sq"), 2)
            dve.tensor_tensor(vg, vg, sgv.unsqueeze(2).to_broadcast([P, 32, SG_D]), ALU.mult) \
                .then_inc(sem("sg_ln"), 1)

        def dve_spatial(dve, v):
            for g in range(SG_G):
                dve.wait_ge(sem("sg_mm"), g + 1)
                dve.wait_ge(sem("gu_act"), 2 * NT)
                cols = slice(g * SG_D, (g + 1) * SG_D)
                dve.scalar_tensor_tensor(MIX[:, :, ATT_W + g * SG_D:ATT_W + (g + 1) * SG_D],
                                         ps[:, g, 0:NT * SG_D].rearrange("p (m d) -> p m d", m=NT), bsc[:, g:g + 1],
                                         UG[:, :, cols], ALU.add, ALU.mult).then_inc(sem("sg_done"), 1)

        UNITS = [(m, h) for m in range(NT) for h in range(N_Q)]

        def span(m):
            lo, hi = max(m - 1, 0), min(m + 2, NT)
            return lo, hi, (hi - lo) * P

        def pe_attention(pe):
            pe.wait_ge(sem("sg_done"), SG_G)

            def scores(u):
                m, h = UNITS[u]
                lo, hi, n = span(m)
                r = slice(HD * (h % 2), HD * (h % 2) + HD)
                if u >= 2:
                    pe.wait_ge(sem("s_dve"), u - 1)
                    pe.wait_ge(sem("s_act"), u - 1)
                qT = QT[r, h // 2, m * P:(m + 1) * P]
                pe.matmul(ps[:, 2 * (u % 2), 0:n], qT, KT[r, h // 4, lo * P:hi * P], start=True, stop=True)
                pe.matmul(ps[:, 2 * (u % 2) + 1, 0:CTX], qT, KCT[r, h // 4, :], start=True, stop=True) \
                    .then_inc(sem("s_mm"), 1)

            def turn(u):
                m, h = UNITS[u]
                n = span(m)[2] // P + NC
                pe.wait_ge(sem("p_act"), u + 1)
                if u:
                    pe.wait_ge(sem("pt_out"), 2 * u)
                for b in range(n):
                    mm = pe.transpose(ps[:, 4 + b // 4, (b % 4) * P:(b % 4 + 1) * P], PB[u % 2][:, b * P:(b + 1) * P], ident)
                mm.then_inc(sem("pt_mm"), 1)

            def values(u):
                m, h = UNITS[u]
                lo, hi, n = span(m)
                g = slice(HD * (h // 4), HD * (h // 4) + HD)
                pe.wait_ge(sem("pt_out"), 2 * u + 2)
                if u:
                    pe.wait_ge(sem("o_dve"), u)
                nb = n // P + NC
                for b in range(nb):
                    vb = V[:, lo + b, g] if b < hi - lo else VC[:, b - (hi - lo), g]
                    mm = pe.matmul(ps[:, 6, 0:HD], PT[u % 2][:, b * P:(b + 1) * P], vb,
                                   start=b == 0, stop=b == nb - 1)
                mm.then_inc(sem("o_mm"), 1)

            scores(0)
            for u in range(len(UNITS)):
                if u + 1 < len(UNITS):
                    scores(u + 1)
                pe_mod_1(pe, 3 * u)
                pe_mod_1(pe, 3 * u + 1)
                turn(u)
                pe_mod_1(pe, 3 * u + 2)
                values(u)

        def act_attention(act, a):
            act.wait_ge(sem("tables_in"), 48)

            def scale_ctx(u):
                n = span(UNITS[u][0])[2]
                act.wait_ge(sem("s_mm"), u + 1)
                if u >= 2:
                    act.wait_ge(sem("p_act"), u - 1)
                act.activation(SS[u % 2][:, n:n + CTX], ps[:, 2 * (u % 2) + 1, 0:CTX], ACT.Copy, scale=HD ** -0.5) \
                    .then_inc(sem("s_act"), 1)

            def exps(u):
                m, h = UNITS[u]
                n = span(m)[2] + CTX
                act.wait_ge(sem("s_max"), u + 1)
                if u >= 2:
                    act.wait_ge(sem("pt_mm"), u - 1)
                act.activation(esc[:, u:u + 1], sinkb[:, h:h + 1], ACT.Exp, bias=nmc[:, u:u + 1]).then_inc(sem("act_chain"), 1)
                act.activation(PB[u % 2][:, 0:n], SS[u % 2][:, 0:n], ACT.Exp, bias=nmc[:, u:u + 1],
                               accum_out=rsc[:, u:u + 1]).then_inc(sem("p_act"), 1)

            def turned_p(u):
                act.wait_ge(sem("pt_mm"), u + 1)
                if u >= 2:
                    act.wait_ge(sem("o_mm"), u - 1)
                act.activation(PT[u % 2][:, 0:512], ps[:, 4, :], ACT.Copy).then_inc(sem("pt_out"), 1)

            scale_ctx(0)
            for u in range(len(UNITS)):
                if u + 1 < len(UNITS):
                    scale_ctx(u + 1)
                exps(u)
                turned_p(u)

        def dve_attention(dve, v):
            dve.wait_ge(sem("tables_in"), 48)

            def masked(u):
                m, h = UNITS[u]
                lo, hi, n = span(m)
                first = (lo - m + 1) * P
                dve.wait_ge(sem("s_mm"), u + 1)
                if u >= 2:
                    dve.wait_ge(sem("p_act"), u - 1)
                dve.scalar_tensor_tensor(SS[u % 2][:, 0:n], ps[:, 2 * (u % 2), 0:n], HD ** -0.5,
                                         RP[:, R_MASK + first:R_MASK + first + n], ALU.mult, ALU.add) \
                    .then_inc(sem("s_dve"), 1)
                dve.wait_ge(sem("s_dve"), u + 1)
                dve.wait_ge(sem("s_act"), u + 1)
                v(dve.tensor_reduce(mxc[:, u:u + 1], SS[u % 2][:, 0:n + CTX], AX, ALU.max))
                v.sync()
                dve.tensor_scalar(nmc[:, u:u + 1], mxc[:, u:u + 1], sinkb[:, h:h + 1], -1.0, ALU.max, ALU.mult) \
                    .then_inc(sem("s_max"), 1)

            def finish(u):
                m, h = UNITS[u]
                n = span(m)[2] // P + NC
                dve.wait_ge(sem("pt_mm"), u + 1)
                if u >= 2:
                    dve.wait_ge(sem("o_mm"), u - 1)
                w = max(n - 4, 0) * P
                if w:
                    dve.tensor_copy(PT[u % 2][:, 512:512 + w], ps[:, 5, 0:w]).then_inc(sem("pt_out"), 1)
                else:
                    dve.sem_inc(sem("pt_out"), 1)
                dve.wait_ge(sem("act_chain"), u + 1)
                v(dve.tensor_tensor(dnc[:, u:u + 1], rsc[:, u:u + 1], esc[:, u:u + 1], ALU.add))
                v.sync()
                v(dve.reciprocal(rcc[:, u:u + 1], dnc[:, u:u + 1]))
                v.sync()
                dve.wait_ge(sem("o_mm"), u + 1)
                dve.tensor_scalar(MIX[:, m, h * HD:(h + 1) * HD], ps[:, 6, 0:HD], rcc[:, u:u + 1], None, ALU.mult) \
                    .then_inc(sem("o_dve"), 1)

            masked(0)
            for u in range(len(UNITS)):
                if u + 1 < len(UNITS):
                    masked(u + 1)
                for n in range(3 * u // KD, (3 * u + 3) // KD):
                    dve_mod_1(dve, n)
                finish(u)

        def pe_out(pe, l, src):
            if l == 0:
                pe.wait_ge(sem("mt_turned"), 2 * NT)
            else:
                pe.wait_ge(sem("yn"), 4 * HY_Q)
            norm = f"n2_{l}"
            for m in range(NT):
                for n in range(2):
                    w_wait(pe, W_OUT[l][n])
                    w = W(W_OUT[l][n], KD, 512)
                    for k in range(KD):
                        mm = pe.matmul(ps[:, 2 * m + n, :], src[:, k, m * P:(m + 1) * P], w[:, k, :],
                                       start=k == 0, stop=k == KD - 1)
                    mm.then_inc(sem("yo_mm"), 1)
                    if m == NT - 1:
                        used(pe, "yo_mm", l * 2 * NT + 2 * m + n + 1)
                if m >= 2:
                    pe_router(pe, l, m - 2)
                if m:
                    pe_turn(pe, TM[l], "tp", [m - 1], norm=norm)
            pe_router(pe, l, NT - 2)
            pe_turn(pe, TM[l], "tp", [NT - 1], norm=norm)
            pe_router(pe, l, NT - 1)

        def act_out(act, l):
            norm = f"n2_{l}"

            def turn(m):
                turned(act, lambda o, i: act.activation(o, i, ACT.Copy), FM[l], "tp", "turned", [m], 0, norm)
            for m in range(NT):
                act.wait_ge(sem("yo_dve"), l * 2 * NT + 2 * m + 2)
                if m >= 2:
                    act.wait_ge(sem("sq"), before[norm] + m - 1)
                act.activation([A(80, D), A(84, D)][m % 2], X[:, m, :], ACT.Square, accum_out=ss[:, m:m + 1]) \
                    .then_inc(sem("sq"), 1)
                act.wait_ge(sem("ms"), stats[norm] + m + 1)
                act.activation(ss[:, 8 + m:9 + m], ss[:, 4 + m:5 + m], ACT.Sqrt).then_inc(sem("rt"), 1)
                if m:
                    turn(m - 1)
            turn(NT - 1)

        def dve_out(dve, v, l, tmp):
            norm = f"n2_{l}"
            rowA, rowB = MODR[:, 4 * D:5 * D], MODR[:, 3 * D:4 * D]
            dve.wait_ge(sem("norm_row_in"), 16 * (2 + 2 * l))
            dve.scalar_tensor_tensor(rowA, rowA, 1.0, GROW, ALU.add, ALU.mult).then_inc(sem("row_used"), 1)
            for m in range(NT):
                if m:
                    dve.wait_ge(sem("h"), before[norm] + m)
                for n in range(2):
                    cols = slice(n * 512, (n + 1) * 512)
                    dve.wait_ge(sem("yo_mm"), l * 2 * NT + 2 * m + n + 1)
                    y = tmp[n][:, 0:512]
                    v.sync()
                    v(dve.tensor_tensor(y, ps[:, 2 * m + n, :], MODR[:, 2 * D + n * 512:2 * D + (n + 1) * 512], ALU.mult))
                    v.sync()
                    dve.tensor_tensor(X[:, m, cols], X[:, m, cols], y, ALU.add).then_inc(sem("yo_dve"), 1)
                dve.wait_ge(sem("sq"), before[norm] + m + 1)
                dve.tensor_scalar(ss[:, 4 + m:5 + m], ss[:, m:m + 1], 1.0 / D, EPS, ALU.mult, ALU.add).then_inc(sem("ms"), 1)
                if m:
                    turned(dve, dve.tensor_copy, FM[l], "tp", "turned", [m - 1], 1, norm)
                dve.wait_ge(sem("rt"), stats[norm] + m + 1)
                v(dve.reciprocal(ss[:, 12 + m:13 + m], ss[:, 8 + m:9 + m]))
                v.sync()
                dve.wait_ge(sem("row_used"), NORMS.index(norm) + 1)
                dve.wait_ge(sem("yo_dve"), l * 2 * NT + 2 * m + 2)
                v(dve.scalar_tensor_tensor(tmp[m % 2], X[:, m, :], ss[:, 12 + m:13 + m], rowA, ALU.mult, ALU.mult))
                v.sync()
                dve.tensor_tensor(TM[l][:, m, :].rearrange("p (k j) -> p j k", k=KD),
                                  tmp[m % 2].rearrange("p (j k) -> p j k", k=KD),
                                  rowB.rearrange("p (j k) -> p j k", k=KD), ALU.add).then_inc(sem("h"), 1)
            turned(dve, dve.tensor_copy, FM[l], "tp", "turned", [NT - 1], 1, norm)

        G2T = [A(92, D), A(96, D)]
        RTR = A3(100, KD, E)
        EB = A(102, E)
        EXG = [A(48, D), A(52, D)]
        EXT = [A3(56, KD, P), A3(60, KD, P)]
        EY = [A(64, D), A(68, D)]
        ESG = [A(72, FE), A(73, FE)]
        EA = [A(74, FE), A(75, FE)]
        EAT = [A3(76, 2, P), A3(77, 2, P)]
        EOH = [A(78, 256).bitcast(BF16).rearrange("p (m s) -> p m s", m=NT), A(79, 256).bitcast(BF16).rearrange("p (m s) -> p m s", m=NT)]

        def t64(kb):
            return A3(kb, NT, E)
        SC, BI, MK, MR, SEL, WTS, POS, POSM, SLM = [t64(104 + i) for i in range(9)]
        M8 = A3(113, 32, 8)
        CMP, CMQ = A(114, 256), A(115, 256)
        GS, RK, GM, PEN = [A(116 + 0.125 * i, 32) for i in range(4)]
        T8, S8, W8 = [A3(116.5 + 0.125 * i, NT, 8) for i in range(3)]
        S8I = A3(116.875, NT, 8).bitcast(I32)
        CNT, OV, OVC, OVS, OVT = [A(117 + 0.25 * i, E) for i in range(5)]
        SW, RW = A(118.25, 4), A(118.3125, 4)
        OVE = A(118.5, 32, 1)
        OVI = A(118.75, 36, 1).bitcast(I32)
        IOR = A(119, P)
        TOKI = [A(119.5, 1).bitcast(I32), A(119.5625, 1).bitcast(I32)]
        BIGT = A(120, 2048)
        WGU = [A3(0, KD, 512), A3(24, KD, 512)]
        WD = [A3(16, 2, D), A3(40, 2, D)]
        CGB = [HT[:, 2 * i:2 * i + 2, :].rearrange("p k t -> p (k t)") for i in range(4)] + [A(80, D), A(84, D)]

        def sp_router(sp, l):
            sp.dma_start(RTR, w_router[l].rearrange("(p k) e -> p k e", k=KD)).then_inc(sem("eb_in"), 16)
            sp.dma_start(EB, e_bias[l:l + 1, :].to_broadcast([P, E])).then_inc(sem("eb_in"), 16)

        def e_view(w, l, e):
            v = w[l].rearrange("e (p k) f -> p e k f", k=KD)
            return v[:, bass.ds(e, 1), :, :].rearrange("p a k f -> p (a k) f")

        def sp_gate_up(sp, l, e, n, p):
            wait(sp, f"gu_m_{l}", n - 1)
            sp.dma_start(WGU[p][:, :, 0:FE], e_view(w_gate, l, e)).then_inc(sem(f"wgu{p}_{l}"), 16)
            sp.dma_start(WGU[p][:, :, FE:2 * FE], e_view(w_up, l, e)).then_inc(sem(f"wgu{p}_{l}"), 16)

        def sp_down(sp, l, e, n, p):
            wait(sp, f"y_mm_{l}", n * 2 - 2)
            v = w_down[l].rearrange("e (p k) n -> p e k n", k=2)[:, bass.ds(e, 1), :, :]
            sp.dma_start(WD[p], v.rearrange("p a k n -> p (a k) n")).then_inc(sem(f"wd{p}_{l}"), 16)

        def sp_experts(sp, l):
            sp.wait_ge(sem("dense_used"), W_SH[l][0] + 1)
            sp_gate_up(sp, l, 0, 0, 0)
            if l == 0:
                sp_gate_up(sp, l, 1, 1, 1)
                sp.wait_ge(sem("dense_used"), W_SH[l][1] + 1)
                sp_down(sp, l, 0, 0, 0)
            else:
                sp_down(sp, l, 0, 0, 0)
                sp.wait_ge(sem("dense_used"), W_SH[l][1] + 1)
                sp_gate_up(sp, l, 1, 1, 1)

            def pair(i):
                for p in range(2):
                    n = i * 2 + p
                    sp_gate_up(sp, l, n, n, p)
                    sp_down(sp, l, n - 1, n - 1, 1 - p)
            pair(1)
            with sp.Fori(2, E // 2) as i:
                pair(i)
            sp_down(sp, l, E - 1, E - 1, 1)
            sp.wait_ge(sem("tables"), l + 1)
            nov = sp_nov(sp, l)

            def over(i):
                for p in range(2):
                    with sp.If(nov > i * 2 + p):
                        e = sp.value_load(OVI[0:1, bass.ds(i * 2 + p, 1)], min_val=0, max_val=E - 1)
                        sp_gate_up(sp, l, e, i * 2 + p + E, p)
                        sp_down(sp, l, e, i * 2 + p + E, p)
            over_loop(sp, nov, over)

        def over_loop(eng, nov, pair):
            with eng.Fori(0, FEW // 2) as i:
                pair(i)
            with eng.If(nov > FEW):
                with eng.Fori(FEW // 2, OVER // 2) as i:
                    pair(i)

        def sp_nov(eng, l):
            return eng.value_load(OVI[0:1, 32:33], min_val=0, max_val=OVER)

        def pe_router(pe, l, m):
            pe.wait_ge(sem("turned"), 2 * (before[f"n2_{l}"] + m + 1))
            pe.wait_ge(sem("eb_in"), l * 32 + 32)
            for k in range(KD):
                mm = pe.matmul(ps[:, 0, m * E:(m + 1) * E], FM[l][:, k, m * P:(m + 1) * P], RTR[:, k, :],
                               start=k == 0, stop=k == KD - 1)
            if m == NT - 1:
                mm.then_inc(sem("lg_mm"), 1)

        def act_router(act, a, l):
            act.wait_ge(sem("lg_mm"), l + 1)
            act.wait_ge(sem("mod_stored"), 16)
            act.activation(SC, ps[:, 0, 0:NT * E].rearrange("p (m e) -> p m e", m=NT), ACT.Sigmoid) \
                .then_inc(sem("score"), 1)

        def dve_select(dve, v, l):
            bc = lambda ap, n: ap.unsqueeze(2).to_broadcast([P, ap.shape[1], n])
            row = lambda ap: ap.unsqueeze(1).to_broadcast([P, NT, E])

            def do(ins):
                v(ins)
                v.sync()
            dve.wait_ge(sem("score"), l + 1)
            do(dve.tensor_tensor(BI, SC, row(EB), ALU.add))
            bg = BI.rearrange("p m (g e) -> p (m g) e", g=GROUPS)
            for i in range(32):
                v(dve.max(M8[:, i, :], bg[:, i, :]))
            v.sync()
            do(dve.tensor_tensor(GS, M8[:, :, 0], M8[:, :, 1], ALU.add))
            gs3 = GS.rearrange("p (m g) -> p m g", m=NT)
            c4 = lambda ap: ap.rearrange("p (m g h) -> p m g h", m=NT, g=GROUPS)
            other = gs3.unsqueeze(2).to_broadcast([P, NT, GROUPS, GROUPS])
            own = gs3.unsqueeze(3).to_broadcast([P, NT, GROUPS, GROUPS])
            v(dve.tensor_tensor(c4(CMP), other, own, ALU.is_gt))
            do(dve.tensor_tensor(c4(CMQ), other, own, ALU.is_equal))
            lt = K[:, C_LT:C_LT + 64].unsqueeze(1).to_broadcast([P, NT, 64])
            do(dve.tensor_tensor(CMQ.rearrange("p (m x) -> p m x", m=NT), CMQ.rearrange("p (m x) -> p m x", m=NT), lt, ALU.mult))
            do(dve.tensor_tensor(CMP, CMP, CMQ, ALU.add))
            do(dve.tensor_reduce(RK, CMP.rearrange("p (g h) -> p g h", h=GROUPS), AX, ALU.add))
            do(dve.tensor_scalar(GM, RK, TOPK_GROUPS - 0.5, None, ALU.is_lt))
            v(dve.tensor_scalar(PEN, GM, -1.0, BIG, ALU.add, ALU.mult))
            mg = MK.rearrange("p m (g e) -> p (m g) e", g=GROUPS)
            do(dve.tensor_tensor(mg, bg, bc(GM, 8), ALU.mult))
            do(dve.tensor_tensor(mg, mg, bc(PEN, 8), ALU.add))
            for m in range(NT):
                v(dve.max(T8[:, m, :], MK[:, m, :]))
            v.sync()
            for m in range(NT):
                v(dve.match_replace(MR[:, m, :], T8[:, m, :], MK[:, m, :], -3.0 * BIG))
            v.sync()
            dve.tensor_tensor(SEL, MR, MK, ALU.not_equal).then_inc(sem("sel"), 1)
            dve.wait_ge(sem("sel"), l + 1)
            do(dve.tensor_tensor(WTS, SC, SEL, ALU.mult))
            do(dve.tensor_reduce(SW, WTS, AX, ALU.add))
            do(dve.reciprocal(RW, SW))
            do(dve.tensor_scalar(RW, RW, ROUTED_SCALE, None, ALU.mult))
            do(dve.tensor_tensor(WTS, WTS, bc(RW, E), ALU.mult))
            dve.wait_ge(sem("pos_mm"), l + 1)
            v(dve.tensor_copy(POS, ps[:, 1, 0:NT * E].rearrange("p (m e) -> p m e", m=NT)))
            do(dve.tensor_copy(CNT, ps[:, 2, 0:E]))
            do(dve.scalar_tensor_tensor(POSM, POS, 1.0, SEL, ALU.add, ALU.mult))
            v(dve.tensor_scalar(POSM, POSM, -1.0, None, ALU.add))
            do(dve.tensor_scalar(OV, CNT, P + 0.5, None, ALU.is_gt))
            for j in range(2, NT):
                do(dve.scalar_tensor_tensor(OV, CNT, j * P + 0.5, OV, ALU.is_gt, ALU.add))
            do(dve.tensor_tensor_scan(OVC, ones[:, 0:E], OV, 0.0, ALU.mult, ALU.add))
            do(dve.tensor_tensor(OVS, OVC, OV, ALU.subtract))
            do(dve.tensor_scalar(OVS, OVS, E - 1.0, 128.0, ALU.add, ALU.mult))
            do(dve.tensor_tensor(OVS, OVS, K[:, C_E128:C_E128 + E], ALU.subtract))
            do(dve.tensor_scalar(SLM, POS, P - 0.5, None, ALU.is_gt))
            do(dve.tensor_tensor(SLM, SLM, row(OVS), ALU.mult))
            do(dve.tensor_tensor(SLM, SLM, POS, ALU.add))
            do(dve.tensor_tensor(SLM, SLM, row(K[:, C_E128:C_E128 + E]), ALU.add))
            do(dve.scalar_tensor_tensor(SLM, SLM, 1.0, SEL, ALU.add, ALU.mult))
            dve.tensor_scalar(SLM, SLM, -1.0, None, ALU.add).then_inc(sem("slots"), 1)

        def dve_over_table(dve, v, l):
            def do(ins):
                v(ins)
                v.sync()
            j3 = BIGT[0:1, :].rearrange("p (j e) -> p j e", j=32)
            do(dve.tensor_tensor(j3, OVC[0:1, :].unsqueeze(1).to_broadcast([1, 32, E]),
                                 K[0:1, C_IOTA:C_IOTA + 32].unsqueeze(2).to_broadcast([1, 32, E]), ALU.is_le))
            do(dve.tensor_reduce(OVE, j3, AX, ALU.add))
            do(dve.tensor_scalar(OVE, OVE, E - 1.0, None, ALU.min))
            v(dve.tensor_copy(OVI[:, 0:32], OVE))
            v(dve.tensor_copy(OVI[:, 32:33], OVC[0:1, E - 1:E]))
            dve.tensor_scalar(IOR, K[:, C_IOTA:C_IOTA + P], float(E * P), None, ALU.add).then_inc(sem(f"next_range_{l}"), 1)

        def dve_slot_table(dve, v, l, tiles):
            def do(ins):
                v(ins)
                v.sync()
            if 0 in tiles:
                for m in range(NT):
                    v(dve.max(S8[:, m, :], SLM[:, m, :]))
                v.sync()
                v(dve.tensor_copy(S8I, S8))
            hit = BIGT[:, 0:512].rearrange("p (k e) -> p k e", k=8)
            for m in tiles:
                do(dve.tensor_tensor(hit, SLM[:, m, :].unsqueeze(1).to_broadcast([P, 8, E]),
                                     S8[:, m, :].unsqueeze(2).to_broadcast([P, 8, E]), ALU.is_equal))
                do(dve.tensor_tensor(hit, hit, WTS[:, m, :].unsqueeze(1).to_broadcast([P, 8, E]), ALU.mult))
                do(dve.tensor_reduce(W8[:, m, :], hit, AX, ALU.add))
            if NT - 1 in tiles:
                dve.engine_nop().then_inc(sem("tables"), 1)

        def pe_positions(pe, l):
            pe.wait_ge(sem("sel"), l + 1)
            pe.wait_ge(sem("consts_made"), 1)
            for m in range(NT):
                for j in range(m + 1):
                    pe.matmul(ps[:, 1, m * E:(m + 1) * E], ones[:, :] if j < m else K[:, C_TRI:C_TRI + P], SEL[:, j, :],
                              start=j == 0, stop=j == m)
            for m in range(NT):
                mm = pe.matmul(ps[:, 2, 0:E], ones[:, :], SEL[:, m, :], start=m == 0, stop=m == NT - 1)
            mm.then_inc(sem("pos_mm"), 1)

        def pe_shared(pe, l, tiles):
            a, b = W_SH[l]
            if tiles is not None:
                w_wait(pe, a)
                w = W(a, KD, 512)
                for m in tiles:
                    bank = 3 + m
                    for k in range(KD):
                        mm = pe.matmul(ps[:, bank, :], FM[l][:, k, m * P:(m + 1) * P], w[:, k, :],
                                       start=k == 0, stop=k == KD - 1)
                    mm.then_inc(sem("shgu_mm"), 1)
                if NT - 1 in tiles:
                    used(pe, "shgu_mm", l * NT + NT)
                return
            w_wait(pe, b)
            w = W(b, 2, D)
            for m in range(NT):
                pe.wait_ge(sem("sha"), l * NT + m + 1)
                if m:
                    pe.wait_ge(sem("shat"), l * NT + m)
                for k in range(2):
                    mm = pe.transpose(ps[:, 0, k * P:(k + 1) * P], EA[m % 2][:, k * P:(k + 1) * P], ident)
                mm.then_inc(sem("shat_mm"), 1)
                pe.wait_ge(sem("shat"), l * NT + m + 1)
                for n in range(2):
                    t = 2 * m + n
                    bank = 3 + t % 4
                    if t < 4:
                        pe.wait_ge(sem("sha"), l * NT + bank - 2)
                    else:
                        pe.wait_ge(sem("shy_act"), l * NT + (t - 4) // 2 + 1)
                        pe.wait_ge(sem("shy_dve"), l * NT + (t - 4) // 2 + 1)
                    for k in range(2):
                        mm = pe.matmul(ps[:, bank, :], EAT[m % 2][:, k, :], w[:, k, n * 512:(n + 1) * 512],
                                       start=k == 0, stop=k == 1)
                    mm.then_inc(sem("shy_mm"), 1)
            used(pe, "shy_mm", l * 2 * NT + 2 * NT)

        SHG = BIGT[:, 0:1024].rearrange("p (m f) -> p m f", m=NT)
        SHA = BIGT[:, 1024:2048].rearrange("p (m f) -> p m f", m=NT)

        def act_shared(act, a, l):
            for m in range(NT):
                act.wait_ge(sem("shgu_mm"), l * NT + m + 1)
                act.activation(SHG[:, m, :], ps[:, 3 + m, 0:FE], ACT.Silu).then_inc(sem("shsilu"), 1)
            for m in range(NT):
                act.wait_ge(sem("shat_mm"), l * NT + m + 1)
                if m >= 2:
                    act.wait_ge(sem("shy_mm"), l * 2 * NT + 2 * m - 2)
                act.activation(EAT[m % 2], ps[:, 0, 0:FE].rearrange("p (k t) -> p k t", k=2), ACT.Copy) \
                    .then_inc(sem("shat"), 1)
                act.wait_ge(sem("shy_mm"), l * 2 * NT + 2 * m + 1)
                act.activation(H[:, m, 0:512], ps[:, 3 + (2 * m) % 4, :], ACT.Copy).then_inc(sem("shy_act"), 1)

        def dve_shared(dve, v, l, tiles):
            if tiles is not None:
                for m in tiles:
                    dve.wait_ge(sem("shsilu"), l * NT + m + 1)
                    if m >= 2:
                        dve.wait_ge(sem("shat_mm"), l * NT + m - 1)
                    dve.tensor_tensor(EA[m % 2].rearrange("p (k j) -> p j k", k=2),
                                      SHG[:, m, :].rearrange("p (j k) -> p j k", k=2),
                                      ps[:, 3 + m, FE:2 * FE].rearrange("p (j k) -> p j k", k=2), ALU.mult) \
                        .then_inc(sem("sha"), 1)
                return
            for m in range(NT):
                dve.wait_ge(sem("shy_mm"), l * 2 * NT + 2 * m + 2)
                dve.tensor_copy(H[:, m, 512:1024], ps[:, 3 + (2 * m + 1) % 4, :]).then_inc(sem("shy_dve"), 1)

        def pe_token_ids(pe, l, n, p):
            pe.wait_ge(sem(f"oh_{l}"), n + 1)
            pe.wait_ge(sem(f"tok_{l}"), n)
            for m in range(NT):
                mm = pe.matmul(ps[:, 7, 2 * p:2 * p + 2], EOH[p][:, m, :], tid[:, 2 * m:2 * m + 2],
                               start=m == 0, stop=m == NT - 1)
            mm.then_inc(sem(f"tok_mm_{l}"), 1)

        def pe_rows(pe, l, n, p, landed_sem, landed_count, first):
            pe.wait_ge(sem(landed_sem), landed_count)
            for kk in range(2):
                if not first:
                    pe.wait_ge(sem(f"xt_out_{l}"), n * 2)
                for j in range(4):
                    k = 4 * kk + j
                    mm = pe.transpose(ps[:, kk, j * P:(j + 1) * P], EXG[p][:, k * P:(k + 1) * P], ident)
                mm.then_inc(sem(f"xt_mm_{l}"), 1)

        def pe_gate_up(pe, l, n, p, count, between=None):
            pe.wait_ge(sem(f"xt_out_{l}"), n * 2 + 2)
            pe.wait_ge(sem(f"wgu{p}_{l}"), count)
            for k in range(KD):
                if k == KD // 2 and between is not None:
                    between()
                mm = pe.matmul(ps[:, 2 + p, :], EXT[p][:, k, :], WGU[p][:, k, :], start=k == 0, stop=k == KD - 1)
            mm.then_inc(sem(f"gu_m_{l}"), 1)

        def pe_turn_a(pe, l, n, p):
            pe.wait_ge(sem(f"a_{l}"), n + 1)
            for k in range(2):
                mm = pe.transpose(ps[:, 4, k * P:(k + 1) * P], EA[p][:, k * P:(k + 1) * P], ident)
            mm.then_inc(sem(f"at_mm_{l}"), 1)

        def pe_down(pe, l, n, p, count, first):
            pe.wait_ge(sem(f"at_{l}"), n + 1)
            pe.wait_ge(sem(f"wd{p}_{l}"), count)
            for h in range(2):
                if not first:
                    pe.wait_ge(sem(f"y_out_{l}"), n * 2)
                for k in range(2):
                    mm = pe.matmul(ps[:, 5 + h, :], EAT[p][:, k, :], WD[p][:, k, h * 512:(h + 1) * 512],
                                   start=k == 0, stop=k == 1)
                mm.then_inc(sem(f"y_mm_{l}"), 1)

        def pe_experts(pe, l):
            pe.wait_ge(sem("shy_dve"), l * NT + NT)
            pe.wait_ge(sem("shy_act"), l * NT + NT)
            pe_rows(pe, l, 0, 0, f"xg0_{l}", 16, True)

            def pair(i, last):
                for p in range(2):
                    n, q = i * 2 + p, 1 - p
                    pe_gate_up(pe, l, n, p, i * 32 + 32, None if last else lambda: pe_token_ids(pe, l, n + 2, p))
                    if not (last and p == 1):
                        pe_rows(pe, l, n + 1, q, f"xg{q}_{l}", (i + p) * 16 + 16, False)
                    if not (isinstance(n, int) and n == 0):
                        pe_down(pe, l, n - 1, q, (i + p) * 16, isinstance(n, int) and n == 1)
                    pe_turn_a(pe, l, n, p)
            pair(0, False)
            pair(1, False)
            with pe.Fori(2, E // 2 - 1) as i:
                pair(i, False)
            pair(E // 2 - 1, True)
            pe_down(pe, l, E - 1, 1, E // 2 * 16, False)
            pe.wait_ge(sem("tables"), l + 1)
            nov = sp_nov(pe, l)
            with pe.If(nov > 0):
                pe_token_ids(pe, l, E, 0)

            def over(i):
                for p in range(2):
                    n = i * 2 + p + E
                    with pe.If(nov > i * 2 + p):
                        pe_rows(pe, l, n, p, f"xg{p}_{l}", i * 16 + 16 * (E // 2 + 1), False)
                        with pe.If(nov > i * 2 + p + 1):
                            pe_token_ids(pe, l, n + 1, 1 - p)
                        pe_gate_up(pe, l, n, p, i * 32 + 32 * (E // 2 + 1))
                        pe_turn_a(pe, l, n, p)
                        pe_down(pe, l, n, p, i * 16 + 16 * (E // 2 + 1), False)
            over_loop(pe, nov, over)

        def act_rows(act, l, n, p, wait_free):
            act.wait_ge(sem(f"xt_mm_{l}"), n * 2 + 1)
            if wait_free:
                act.wait_ge(sem(f"gu_m_{l}"), n - 1)
            act.activation(EXT[p][:, 0:4, :], ps[:, 0, :].rearrange("p (k s) -> p k s", k=4), ACT.Copy) \
                .then_inc(sem(f"xt_out_{l}"), 1)

        def act_silu(act, l, n, p):
            act.wait_ge(sem(f"gu_m_{l}"), n + 1)
            act.activation(ESG[p], ps[:, 2 + p, 0:FE], ACT.Silu).then_inc(sem(f"silu_{l}"), 1)

        def act_turned_a(act, l, n, p):
            act.wait_ge(sem(f"at_mm_{l}"), n + 1)
            act.activation(EAT[p], ps[:, 4, 0:FE].rearrange("p (k s) -> p k s", k=2), ACT.Copy) \
                .then_inc(sem(f"at_{l}"), 1)

        def act_result(act, l, n, p):
            act.wait_ge(sem(f"y_mm_{l}"), n * 2 + 1)
            act.activation(EY[p][:, 0:512], ps[:, 5, :], ACT.Copy).then_inc(sem(f"y_out_{l}"), 1)

        def act_store(act, l, n, p, b, done):
            act.wait_ge(sem(f"y_out_{l}"), n * 2 + 2)
            rows = y_dram.rearrange("(b s) d -> s b d", s=P)[:, bass.ds(b, 1), :].rearrange("s a d -> s (a d)")
            act.dma_start(rows, EY[p]).then_inc(sem(done), 16)

        def act_experts(act, a, l):
            act.wait_ge(sem("zeroed"), 16 * ZPARTS)
            act_rows(act, l, 0, 0, False)

            def result(n, q, count):
                wait(act, f"yst{q}_{l}", count)
                act_result(act, l, n, q)

            def pair(i, last):
                for p in range(2):
                    n, q = i * 2 + p, 1 - p
                    act_silu(act, l, n, p)
                    if not (last and p == 1):
                        act_rows(act, l, n + 1, q, not (isinstance(n, int) and n == 0))
                    begun = not (isinstance(n, int) and n == 0)
                    if begun:
                        result(n - 1, q, (i + p) * 16 - 16)
                    act_turned_a(act, l, n, p)
                    if begun:
                        act_store(act, l, n - 1, q, n - 1, f"yst{q}_{l}")
            pair(0, False)
            pair(1, False)
            with act.Fori(2, E // 2 - 1) as i:
                pair(i, False)
            pair(E // 2 - 1, True)
            result(E - 1, 1, E // 2 * 16 - 16)
            act_store(act, l, E - 1, 1, E - 1, f"yst1_{l}")
            act.wait_ge(sem("tables"), l + 1)
            nov = sp_nov(act, l)
            act.sem_inc(sem(f"over_stored_{l}"), 1)

            def over(i):
                for p in range(2):
                    n = i * 2 + p + E
                    with act.If(nov > i * 2 + p):
                        act_rows(act, l, n, p, False)
                        act_silu(act, l, n, p)
                        act_turned_a(act, l, n, p)
                        act.wait_ge(sem(f"yst{p}_{l}"), 16 * (E // 2))
                        act.wait_ge(sem(f"over_stored_{l}"), (i * 2 + p) * 16 + 1)
                        act_result(act, l, n, p)
                        act_store(act, l, n, p, n, f"over_stored_{l}")
            over_loop(act, nov, over)
            for p in range(2):
                act.wait_ge(sem(f"yst{p}_{l}"), 16 * (E // 2))
            act.wait_ge(sem(f"over_stored_{l}"), nov * 16 + 1)
            act.sem_inc(sem("moe_done"), 1)

        def dve_one_hot(dve, l, n, p, column, against, wait_free):
            if wait_free:
                dve.wait_ge(sem(f"tok_mm_{l}"), n - 1)
            dve.tensor_tensor(EOH[p], column.to_broadcast([P, NT, P]), against.unsqueeze(1).to_broadcast([P, NT, P]),
                              ALU.is_equal).then_inc(sem(f"oh_{l}"), 1)

        def dve_token_ids(dve, l, n, p, wait_free):
            dve.wait_ge(sem(f"tok_mm_{l}"), n + 1)
            if wait_free is not None:
                dve.wait_ge(sem(f"xg{p}_{l}"), wait_free)
            dve.tensor_scalar(TOKI[p], ps[:, 7, 2 * p:2 * p + 1], ps[:, 7, 2 * p + 1:2 * p + 2], None, ALU.add).then_inc(sem(f"tok_{l}"), 1)

        def dve_rows(dve, l, n, p, wait_free):
            dve.wait_ge(sem(f"xt_mm_{l}"), n * 2 + 2)
            if wait_free:
                dve.wait_ge(sem(f"gu_m_{l}"), n - 1)
            dve.tensor_copy(EXT[p][:, 4:8, :], ps[:, 1, :].rearrange("p (k s) -> p k s", k=4)) \
                .then_inc(sem(f"xt_out_{l}"), 1)

        def dve_product(dve, l, n, p, wait_free):
            dve.wait_ge(sem(f"silu_{l}"), n + 1)
            dve.tensor_tensor(EA[p].rearrange("p (k j) -> p j k", k=2), ESG[p].rearrange("p (j k) -> p j k", k=2),
                              ps[:, 2 + p, FE:2 * FE].rearrange("p (j k) -> p j k", k=2), ALU.mult) \
                .then_inc(sem(f"a_{l}"), 1)

        def dve_result(dve, l, n, p):
            dve.wait_ge(sem(f"y_mm_{l}"), n * 2 + 2)
            dve.tensor_copy(EY[p][:, 512:1024], ps[:, 6, :]).then_inc(sem(f"y_out_{l}"), 1)

        def dve_experts(dve, v, l):
            first = K[:, C_IOTA:C_IOTA + P]
            dve_rows(dve, l, 0, 0, False)
            tables = {0: lambda: dve_over_table(dve, v, l), 1: lambda: dve_slot_table(dve, v, l, range(0, 2)),
                      2: lambda: dve_slot_table(dve, v, l, range(2, NT))}

            def result(n, q, count):
                wait(dve, f"yst{q}_{l}", count)
                dve_result(dve, l, n, q)

            def pair(i, last):
                for p in range(2):
                    n, q = i * 2 + p, 1 - p
                    begun = not (isinstance(n, int) and n == 0)
                    if not last:
                        dve_one_hot(dve, l, n + 2, p, POSM[:, :, bass.ds(n + 2, 1)], first, True)
                        dve_token_ids(dve, l, n + 2, p, i * 16 + 16)
                    dve_product(dve, l, n, p, True)
                    if not (last and p == 1):
                        dve_rows(dve, l, n + 1, q, begun)
                    if begun:
                        result(n - 1, q, (i + p) * 16 - 16)
                    if isinstance(n, int) and n in tables:
                        tables[n]()
            pair(0, False)
            pair(1, False)
            with dve.Fori(2, E // 2 - 1) as i:
                pair(i, False)
            pair(E // 2 - 1, True)
            result(E - 1, 1, E // 2 * 16 - 16)
            dve.wait_ge(sem("tables"), l + 1)
            nov = sp_nov(dve, l)

            def ids(n, p, block, count):
                e = dve.value_load(OVI[0:1, bass.ds(block, 1)], min_val=0, max_val=E - 1)
                dve.wait_ge(sem(f"tok_mm_{l}"), n)
                dve.wait_ge(sem(f"next_range_{l}"), n - E + 1)
                dve_one_hot(dve, l, n, p, SLM[:, :, bass.ds(e, 1)], IOR, False)
                dve.wait_ge(sem(f"oh_{l}"), n + 1)
                dve.tensor_scalar(IOR, IOR, float(P), None, ALU.add).then_inc(sem(f"next_range_{l}"), 1)
                dve_token_ids(dve, l, n, p, count)
            with dve.If(nov > 0):
                ids(E, 0, 0, 16 * (E // 2))

            def over(i):
                for p in range(2):
                    n = i * 2 + p + E
                    with dve.If(nov > i * 2 + p):
                        with dve.If(nov > i * 2 + p + 1):
                            ids(n + 1, 1 - p, i * 2 + p + 1, (i + p) * 16 + 16 * (E // 2))
                        dve_rows(dve, l, n, p, False)
                        dve_product(dve, l, n, p, False)
                        dve.wait_ge(sem(f"yst{p}_{l}"), 16 * (E // 2))
                        dve.wait_ge(sem(f"over_stored_{l}"), (i * 2 + p) * 16 + 1)
                        dve_result(dve, l, n, p)
            over_loop(dve, nov, over)

        def gather(pool, dst, table, index, bound):
            return pool.indirect_dma_start(
                out=dst, out_offset=None, in_=table,
                in_offset=bass.IndirectOffsetOnAxis(ap=index, axis=0), bounds_check=bound, oob_is_err=False)

        def pool_experts(pool, l):
            last_token, last_row = pool.to_reg(T - 1), pool.to_reg(NBLK * P - 1)
            pool.wait_ge(sem("h2_stored"), 16 * (l + 1))

            def rows(n, p, free):
                pool.wait_ge(sem(f"tok_{l}"), n + 1)
                if free is not None:
                    pool.wait_ge(sem(f"xt_mm_{l}"), free)
                pool.sem_inc(sem("rows_asked"), 1)
                gather(pool, EXG[p], h2_dram[l], TOKI[p], last_token).then_inc(sem(f"xg{p}_{l}"), 16)
            rows(0, 0, None)
            rows(1, 1, None)
            with pool.Fori(1, E // 2) as i:
                for p in range(2):
                    rows(i * 2 + p, p, i * 4 + 2 * p - 2)
            pool.wait_ge(sem("tables"), l + 1)
            nov = sp_nov(pool, l)

            def over(i):
                for p in range(2):
                    with pool.If(nov > i * 2 + p):
                        rows(i * 2 + p + E, p, i * 4 + 2 * (p + E) - 2)
            over_loop(pool, nov, over)
            pool.wait_ge(sem("moe_done"), l + 1)
            for n in range(NT * TOP_K):
                m, k = n // TOP_K, n % TOP_K
                g = l * NT * TOP_K + n
                if n >= CG:
                    pool.wait_ge(sem("cadd"), g - CG + 1)
                gather(pool, CGB[g % CG], y_dram, S8I[:, m, k:k + 1], last_row).then_inc(sem(f"cg{g % CG}"), 16)

        def dve_combine(dve, v, l):
            dve.wait_ge(sem("shy_act"), l * NT + NT)
            dve.wait_ge(sem("shy_dve"), l * NT + NT)
            for n in range(NT * TOP_K):
                m, k = n // TOP_K, n % TOP_K
                g = l * NT * TOP_K + n
                dve.wait_ge(sem(f"cg{g % CG}"), g // CG * 16 + 16)
                if k:
                    dve.wait_ge(sem("cadd"), g)
                dve.scalar_tensor_tensor(H[:, m, :], CGB[g % CG], W8[:, m, k:k + 1], H[:, m, :], ALU.mult, ALU.add) \
                    .then_inc(sem("cadd"), 1)
                if k == TOP_K - 1:
                    dve.wait_ge(sem("cadd"), g + 1)
                    v(dve.tensor_tensor(H[:, m, :], H[:, m, :], MODR[:, 5 * D:6 * D], ALU.mult))
                    v.sync()
                    dve.tensor_tensor(X[:, m, :], X[:, m, :], H[:, m, :], ALU.add).then_inc(sem("layer_start"), 1)

        DFT = [A(48 + 4 * i, 2 * T) for i in range(4)]
        MC, MS = [DFT[i].rearrange("p (t f) -> p t f", t=NT) for i in range(2)]
        IC, IS = [DFT[2 + i].rearrange("p (f t) -> p f t", f=2) for i in range(2)]
        AS, BS = A3(64, 4, 512), A3(72, 4, 512)
        ZB = [A3(80 + 4 * j, 2, T) for j in range(3)]
        R1, R2 = A3(92, NT, 512), A3(100, NT, 512)
        EV = [[A(108 + 4 * f + 2 * i, 512) for i in range(2)] for f in range(2)]
        A2T = A(120, T, FILT_HID)
        HF = MODR[:, 0:2048].rearrange("p (t c) -> p t c", t=NT)
        PP = MODR[:, 0:2048].rearrange("p (a f c) -> p a f c", a=4, f=2)
        WIN = [A(124, 512), A(126, 512)]
        TP = [A3(kb, 2, CH) for kb in (8, 10, 116, 118)]
        ABX, ABT = A3(108, NT, 512), A(12, 512)
        TB = [A(24, T), A(26, T)]
        WZ = [A3(16 * j, KD, CH) for j in range(3)]
        WF = [A(40, 512, FILT_HID), A(42, 512, FILT_HID)]
        DL = [A(44, 512), A(46, 512)]
        Y2T = H[:, :, :].rearrange("p m (a t) -> p (m a) t", a=2)
        FEAT = A(100, T, FILT_EMB)
        CWR = A(102, P, 112)
        W1 = A(103, FILT_HID, FILT_EMB)
        W2 = A(103.5, FILT_HID, FILT_HID)
        FA, FN = A(104, T, FILT_HID), A(106, T, FILT_HID)
        A1T = A(108, T, FILT_HID)
        cols = sm[:, 0:112]
        fcol = sm[0:FILT_HID, 112:115]
        rl = sm[:, 120:124]
        TWO_PI = 2.0 * math.pi
        PI_HI, MAGIC = 6.28125, 12582912.0

        def sp_hyena(sp):
            for w, src in ((FEAT, c_feats), (CWR[0:72, :], conv_w[0].rearrange("j (c p) -> (j c) p", p=P)),
                           (CWR[72:96, :], conv_b.rearrange("a (c p) -> (a c) p", p=P)),
                           (CWR[96:112, :], filt_bias[0].rearrange("o (c p) -> (o c) p", p=P)),
                           (W1, filt_w1[0]), (W2, filt_w2[0]),
                           (fcol[:, 0:1], filt_b1.rearrange("a (p b) -> p (a b)", b=1)),
                           (fcol[:, 1:2], filt_b2.rearrange("a (p b) -> p (a b)", b=1)),
                           (fcol[:, 2:3], filt_freq.rearrange("a (p b) -> p (a b)", b=1))):
                sp.dma_start(w, src).then_inc(sem("hy_in"), 16)
            sp.wait_ge(sem("moe_done"), 1)
            sp.wait_ge(sem("cadd"), NT * TOP_K - 10)
            for i in range(4):
                sp.dma_start(DFT[i], c_dft[:, i, :]).then_inc(sem("dft_in"), 16)

            def quarter(q):
                wz = w_in_c[0].rearrange("(p k) (j q c) -> p q k j c", k=KD, j=3, q=HY_Q)[:, bass.ds(q, 1), :, :, :]

                def taps(j):
                    wait(sp, "z_mm", q * 6 - 4 + 2 * j)
                    sp.dma_start(WZ[j], wz[:, :, :, j, :].rearrange("p a k c -> p (a k) c")).then_inc(sem(f"wz_in_{j}"), 16)
                taps(0)
                taps(1)
                wait(sp, "hf_mm", q * 8)
                wait(sp, "win", q * 8)
                w3 = filt_w3[0].rearrange("h (o b q c) -> h q o b c", o=2, b=2, q=HY_Q)[:, bass.ds(q, 1), :, :, :]
                dl = filt_delta.rearrange("a (o b q c) -> a q o b c", o=2, b=2, q=HY_Q)[:, bass.ds(q, 1), :, :, :]
                for o in range(2):
                    for b in range(2):
                        c = slice(b * CH, (b + 1) * CH)
                        sp.dma_start(WF[o][:, c], w3[:, :, o, b, :].rearrange("h a c -> h (a c)")).then_inc(sem("wf_in"), 16)
                        sp.dma_start(DL[o][:, c], dl[:, :, o, b, :].rearrange("a q c -> a (q c)").to_broadcast([P, CH])) \
                            .then_inc(sem("wf_in"), 16)
                taps(2)

            quarter(0)
            sp.wait_ge(sem("layer_start"), NT)
            sp.dma_start(MODR[:, 5 * D:6 * D], mod_dram[:, 5 * D:6 * D].to_broadcast([P, D])).then_inc(sem("bmod_in"), 16)
            with sp.Fori(1, HY_Q) as i:
                quarter(i)

        def pe_filter_net(pe):
            wait(pe, "hy_in", 144)
            wait(pe, "moe_done", 1)
            pe.transpose(ps[:, 1, 0:112], CWR, ident[0:112, 0:112]).then_inc(sem("f_mm"), 1)
            pe.matmul(ps[0:FILT_HID, 0, :], W1, FEAT, start=True, stop=True).then_inc(sem("f_mm"), 1)
            wait(pe, "f_sin", 1)
            pe.matmul(ps[0:FILT_HID, 0, :], W2, A1T, start=True, stop=True).then_inc(sem("f_mm"), 1)

        def act_filter_net(act):
            for i, dst in enumerate((A1T, A2T)):
                wait(act, "f_arg", i + 2)
                act.activation(dst, FA, ACT.Sin).then_inc(sem("f_sin"), 1)

        def dve_filter_net(dve, v):
            wait(dve, "hy_in", 144)
            wait(dve, "moe_done", 1)
            wait(dve, "f_mm", 1)
            dve.tensor_copy(cols, ps[:, 1, 0:112]).then_inc(sem("f_arg"), 1)
            for i in range(2):
                wait(dve, "f_mm", i + 2)
                if i:
                    wait(dve, "f_sin", i)
                v(dve.tensor_scalar(FA, ps[0:FILT_HID, 0, :], fcol[:, i:i + 1], fcol[:, 2:3], ALU.add, ALU.mult))
                v.sync()
                v(dve.tensor_scalar(FN, FA, 1.0 / TWO_PI, MAGIC, ALU.mult, ALU.add))
                v.sync()
                v(dve.tensor_scalar(FN, FN, -MAGIC, None, ALU.add))
                v.sync()
                for part in (PI_HI, TWO_PI - PI_HI):
                    v(dve.scalar_tensor_tensor(FA, FN, -part, FA, ALU.mult, ALU.add))
                    v.sync()
                top = float(np.nextafter(np.float32(math.pi), np.float32(0)))
                dve.tensor_scalar(FA, FA, top, -top, ALU.min, ALU.max).then_inc(sem("f_arg"), 1)

        ZBANK = (0, 1, 2, 6, 4, 6)

        def pe_hyena(pe):
            def project(q, t):
                j, ct = t // 2, t % 2
                wait(pe, f"wz_in_{j}", q * 16 + 16)
                for k in range(KD):
                    mm = pe.matmul(ps[:, ZBANK[t], :], WZ[j][:, k, ct * P:(ct + 1) * P], HT[:, k, :],
                                   start=k == 0, stop=k == KD - 1)
                mm.then_inc(sem("z_mm"), 1)

            wait(pe, "f_sin", 2)
            wait(pe, "turned", 2 * before["n2_1"])
            wait(pe, "dft_in", 64)
            def quarter(q):
                for o in range(2):
                    u = q * 2 + o
                    wait(pe, "wf_in", q * 128 + 128)
                    wait(pe, "ky_act", u * 4)
                    wait(pe, "ky_dve", u * 4)
                    for t in range(NT):
                        pe.matmul(ps[:, t, :], A2T[:, t * P:(t + 1) * P], WF[o], start=True, stop=True) \
                            .then_inc(sem("hf_mm"), 1)
                    if o == 0:
                        for t in range(3):
                            wait(pe, "hfw", u * 5 + t + 1)
                            project(q, t)
                        wait(pe, "z_dve", q * 6 + 2)
                        wait(pe, "z_dve", q * 6)
                    else:
                        wait(pe, "z_dve", q * 6 + 4)
                        wait(pe, "yn", q * 4 + 2)
                    wait(pe, "yt_act", u * 2)
                    wait(pe, "rl1", u)
                    for b in range(2):
                        for t in range(2 * b, 2 * b + 2):
                            for ct in range(2):
                                at = (t % 2) * CH + ct * P
                                pos = (t % 2) * CH + b
                                mm = pe.transpose(ps[:, 6 + b, at:at + P], ZB[0][:, ct, pos:pos + 2 * P - 1:2], ident)
                        mm.then_inc(sem("yt_mm"), 1)
                    if o == 1:
                        project(q, 4)
                    wait(pe, "sd", u * 2 + 2)
                    wait(pe, "yt_dup", u + 1)
                    if o == 0:
                        wait(pe, "z_dve", q * 6 + 3)
                    else:
                        wait(pe, "hfw", u * 5 + 5)
                    for f in range(2):
                        seen = u * 4 + 2 * f
                        for i, (table, data) in enumerate(((MC, R1), (MS, R2))):
                            for odd in range(2):
                                wait(pe, "ky_dve" if odd else "ky_act", seen + i - 1)
                                for t in range(2 * odd, 2 * odd + 2):
                                    mm = pe.matmul(ps[:, 2 * i + odd, :], table[:, t, f * P:(f + 1) * P], data[:, t, :],
                                                   start=t % 2 == 0, stop=t % 2 == 1)
                                mm.then_inc(sem("ky_mm"), 1)
                    wait(pe, "yt_act", u * 2 + 2)
                    project(q, 3 + 2 * o)
                    wait(pe, "l1sum", u + 1)
                    for ct in range(2):
                        for b in range(2):
                            mm = pe.matmul(ps[:, 7, ct:ct + 1], ABT[:, b * CH + ct * P:b * CH + (ct + 1) * P], ones[:, 0:1],
                                           start=b == 0, stop=b == 1)
                    mm.then_inc(sem("l1_mm"), 1)
                    wait(pe, "pp", u * 2 + 2)
                    wait(pe, "yn", u * 2)
                    if o == 1:
                        wait(pe, "z_dve", q * 6 + 5)
                    for ct in range(2):
                        for odd in range(2):
                            for i, table in enumerate((IC, IS)):
                                for f in range(2):
                                    mm = pe.matmul(ps[:, 4 + ct, odd * CH:(odd + 1) * CH],
                                                   PP[:, 2 * odd + i, f, ct * P:(ct + 1) * P],
                                                   table[:, f, odd * CH:(odd + 1) * CH], start=i + f == 0, stop=i + f == 2)
                        mm.then_inc(sem("iv_mm"), 1)

            quarter(0)
            with pe.Fori(1, HY_Q) as i:
                quarter(i)

        def act_hyena(act):
            def middle(q, t):
                j, ct = t // 2, t % 2
                wait(act, "z_mm", q * 6 + t + 1)
                act.activation(ZB[j][:, ct, :], ps[:, ZBANK[t], :], ACT.Identity,
                               bias=col(72 + j * 8 + ct, q), scale=col(24 + j * 8 + ct, q)).then_inc(sem("z_act"), 1)

            wait(act, "f_arg", 1)
            def quarter(q):
                for o in range(2):
                    u = q * 2 + o
                    wait(act, "wf_in", q * 128 + 128)
                    act.activation(DL[o], DL[o], ACT.Abs).then_inc(sem("act_chain"), 1)
                    wait(act, "act_chain", u + 33)
                    for t in range(NT):
                        wait(act, "hfw", u * 5 + max(t - 1, 0))
                        act.activation(WIN[t % 2], DL[o], ACT.Exp, scale=K[:, C_T01 + t:C_T01 + t + 1]).then_inc(sem("win"), 1)
                    if o == 0:
                        wait(act, "yn", q * 4)
                        wait(act, "iv_act", q * 4)
                        for t in range(3):
                            middle(q, t)
                    wait(act, "ky_mm", u * 8)
                    wait(act, "yt_dup", u)
                    for b in range(2):
                        wait(act, "yt_mm", u * 2 + b + 1)
                        act.activation(R1[:, 2 * b:2 * b + 2, CH:2 * CH], ps[:, 6 + b, :].rearrange("p (t c) -> p t c", t=2), ACT.Copy) \
                            .then_inc(sem("yt_act"), 1)
                    if o == 1:
                        middle(q, 4)
                    wait(act, "l1sum", u + 1)
                    for f in range(2):
                        for i in range(2):
                            wait(act, "ky_dve", u * 4 + 2 * f - 3 + i)
                            wait(act, "ky_mm", u * 8 + 4 * f + 2 * i + 1)
                            act.activation(EV[f][i], ps[:, 2 * i, :], ACT.Copy).then_inc(sem("ky_act"), 1)
                    middle(q, 3 + 2 * o)
                    wait(act, "yn", u * 2)
                    for ct in range(2):
                        act.activation(TB[ct], ZB[0][:, ct, :], ACT.Copy, scale=col(96 + o * 8 + ct, q)).then_inc(sem("iv_act"), 1)

            quarter(0)
            with act.Fori(1, HY_Q) as i:
                quarter(i)

        def col(base, q):
            return cols[:, bass.ds(q * 2 + base, 1)]

        def dve_hyena(dve, v):
            def outer(q, t):
                j, ct = t // 2, t % 2
                z = ZB[j][:, ct, :]
                wait(dve, "z_act", q * 6 + t + 1)
                v(dve.scalar_tensor_tensor(z[:, 1:T], ps[:, ZBANK[t], 0:T - 1], col(j * 8 + ct, q), z[:, 1:T],
                                           ALU.mult, ALU.add))
                v.sync()
                dve.scalar_tensor_tensor(z[:, 0:T - 1], ps[:, ZBANK[t], 1:T], col(48 + j * 8 + ct, q), z[:, 0:T - 1],
                                         ALU.mult, ALU.add).then_inc(sem("z_dve"), 1)

            def double(u):
                wait(dve, "yt_act", u * 2 + 2)
                dve.tensor_copy(R2[:, :, CH:2 * CH], R1[:, :, CH:2 * CH]).then_inc(sem("yt_dup"), 1)

            wait(dve, "f_arg", 1)
            def quarter(q):
                for o in range(2):
                    u = q * 2 + o
                    wait(dve, "iv_mm", u * 2)
                    for t in range(NT):
                        wait(dve, "hf_mm", u * 4 + t + 1)
                        wait(dve, "win", u * 4 + t + 1)
                        dve.scalar_tensor_tensor(HF[:, t, :], WIN[t % 2], DECAY_SHIFT, ps[:, t, :], ALU.add, ALU.mult) \
                            .then_inc(sem("hfw"), 1)
                    wait(dve, "hfw", u * 5 + 4)
                    wait(dve, "sd", u * 2)
                    dve.memset(HF[0:1, 0, CH:2 * CH], 0.0).then_inc(sem("hfw"), 1)
                    wait(dve, "hfw", u * 5 + 5)
                    wait(dve, "ky_mm", u * 8)
                    dve.tensor_tensor(R2[:, :, 0:CH], HF[:, :, 0:CH], HF[:, :, CH:2 * CH], ALU.subtract).then_inc(sem("sd"), 1)
                    if o == 1:
                        double(u)
                    wait(dve, "l1_mm", u)
                    wait(dve, "pp", u * 2)
                    v(dve.scalar_tensor_tensor(ABX, HF, -1.0, HF, ALU.mult, ALU.max))
                    v.sync()
                    dve.tensor_reduce(ABT, ABX.rearrange("p t c -> p c t"), AX, ALU.add).then_inc(sem("l1sum"), 1)
                    if o == 0:
                        for t in range(3):
                            outer(q, t)
                        double(u)
                    else:
                        outer(q, 4)
                    wait(dve, "sd", u * 2 + 2)
                    for f in range(2):
                        for i, sums in enumerate((AS, BS)):
                            wait(dve, "ky_act", u * 4 + 2 * f + i + 1)
                            wait(dve, "ky_mm", u * 8 + 4 * f + 2 * i + 2)
                            even, odd = EV[f][i], ps[:, 2 * i + 1, :]
                            v.sync()
                            v(dve.tensor_tensor(sums[:, 2 * f, :], even, odd, ALU.add))
                            first, second = (even, odd) if i == 0 else (odd, even)
                            dve.tensor_tensor(sums[:, 2 * f + 1, :], first, second, ALU.subtract).then_inc(sem("ky_dve"), 1)
                        wait(dve, "ky_dve", u * 4 + 2 * f + 2)
                        v.sync()
                        ah, ay = AS[:, 2 * f:2 * f + 2, 0:CH], AS[:, 2 * f:2 * f + 2, CH:]
                        bh, by = BS[:, 2 * f:2 * f + 2, 0:CH], BS[:, 2 * f:2 * f + 2, CH:]
                        for i, (x0, x1) in enumerate(((ah, ay), (bh, by), (ah, by), (bh, ay))):
                            v(dve.tensor_tensor(TP[i], x0, x1, ALU.mult))
                        v.sync()
                        v(dve.tensor_tensor(TP[0], TP[0], TP[1], ALU.subtract))
                        v(dve.tensor_tensor(TP[2], TP[2], TP[3], ALU.add))
                        v.sync()
                        v(dve.tensor_tensor(PP[:, 0, f, :], TP[0][:, 0, :], TP[0][:, 1, :], ALU.add))
                        v(dve.tensor_tensor(PP[:, 1, f, :], TP[2][:, 0, :], TP[2][:, 1, :], ALU.subtract))
                        v(dve.tensor_tensor(PP[:, 2, f, :], TP[0][:, 0, :], TP[0][:, 1, :], ALU.subtract))
                        dve.tensor_tensor(PP[:, 3, f, :], TP[2][:, 0, :], TP[2][:, 1, :], ALU.add).then_inc(sem("pp"), 1)
                    outer(q, 3 + 2 * o)
                    wait(dve, "l1_mm", u + 1)
                    wait(dve, "yn", u * 2)
                    dve.reciprocal(rl[:, 2 * o:2 * o + 2], ps[:, 7, 0:2]).then_inc(sem("rl1"), 1)
                    wait(dve, "rl1", u + 1)
                    for ct in range(2):
                        wait(dve, "iv_mm", u * 2 + ct + 1)
                        wait(dve, "iv_act", u * 2 + ct + 1)
                        split = TB[ct].rearrange("p (i odd) -> p odd i", odd=2)
                        v(dve.scalar_tensor_tensor(split, ps[:, 4 + ct, :].rearrange("p (odd i) -> p odd i", odd=2),
                                                   rl[:, 2 * o + ct:2 * o + ct + 1], split, ALU.mult, ALU.add))
                        v.sync()
                        dst = ZB[0][:, ct, :] if o == 0 else Y2T[:, bass.ds(q * 2 + ct, 1), :].rearrange("p a t -> p (a t)")
                        dve.tensor_tensor(dst, TB[ct], ZB[1 + o][:, ct, :], ALU.mult).then_inc(sem("yn"), 1)

            quarter(0)
            with dve.Fori(1, HY_Q) as i:
                v.enter(i - 1, 6 + 2 * (1 + 2 * 11 + 2))
                quarter(i)
            v.leave(HY_Q - 1)

        def pool_hyena(pool):
            def quarter(q):
                for o in range(2):
                    u = q * 2 + o
                    wait(pool, "hfw", u * 5 + 5)
                    wait(pool, "ky_mm", u * 8)
                    pool.tensor_tensor(R1[:, :, 0:CH], HF[:, :, 0:CH], HF[:, :, CH:2 * CH], ALU.add).then_inc(sem("sd"), 1)

            quarter(0)
            with pool.Fori(1, HY_Q) as i:
                quarter(i)
        def sp_moe(sp, l):
            if l == 0:
                sp.wait_ge(sem("o_dve"), 32)
            sp.dma_start(GROW, norm_g[l, 1:2, :].to_broadcast([P, D])).then_inc(sem("norm_row_in"), 16)
            sp_router(sp, l)
            sp_dense(sp, W_SH[l][0])
            sp_dense(sp, W_SH[l][1])
            sp.wait_ge(sem("h"), before[f"n2_{l}"] + NT)
            sp.dma_start(h2_dram[l].rearrange("(m p) d -> p m d", p=P), TM[l][:, :, :]).then_inc(sem("h2_stored"), 16)
            sp_experts(sp, l)

        def act_moe(act, a, l):
            act_out(act, l)
            act_router(act, a, l)
            act.wait_ge(sem("h2_stored"), 16 * (l + 1))
            act_shared(act, a, l)
            act_experts(act, a, l)

        def pe_moe(pe, l):
            pe_shared(pe, l, range(0, 2))
            pe_positions(pe, l)
            pe_shared(pe, l, range(2, NT))
            pe.wait_ge(sem("consts_made"), 2)
            pe_token_ids(pe, l, 0, 0)
            pe_token_ids(pe, l, 1, 1)
            pe_shared(pe, l, None)
            pe_experts(pe, l)

        def dve_moe(dve, v, l):
            dve_select(dve, v, l)
            dve.wait_ge(sem("slots"), l + 1)
            dve_one_hot(dve, l, 0, 0, POSM[:, :, 0:1], K[:, C_IOTA:C_IOTA + P], False)
            dve_one_hot(dve, l, 1, 1, POSM[:, :, 1:2], K[:, C_IOTA:C_IOTA + P], False)
            dve_shared(dve, v, l, range(0, 2))
            dve_token_ids(dve, l, 0, 0, None)
            dve_token_ids(dve, l, 1, 1, None)
            dve_shared(dve, v, l, range(2, NT))
            dve.wait_ge(sem("sha"), l * NT + NT)
            dve.wait_ge(sem("h2_stored"), 16 * (l + 1))
            dve_shared(dve, v, l, None)
            dve_experts(dve, v, l)
            if l == 0:
                dve_filter_net(dve, v)
            dve_combine(dve, v, l)

        @block.sync
        def _(sp):
            sp_setup(sp)
            for n in range(3, W_MOD[1][0]):
                sp_dense(sp, n)
                if n == 5:
                    sp_layer0(sp)
                if n == W_U:
                    sp.wait_ge(sem("h"), before["n2_0"])
                    sp.dma_start(WSR, w_spatial[0].rearrange("g i j -> i g j")).then_inc(sem("ws_in"), 16)
            for n in W_MOD[1][:3]:
                sp_dense(sp, n)
            sp.wait_ge(sem("sg_done"), SG_G)
            sp.dma_start(BROW, b_mod[1:2, :]).then_inc(sem("bmod_in"), 16)
            for i, n in enumerate(W_MOD[1][3:]):
                sp_dense(sp, n)
                if i < ZPARTS:
                    sp_zero_rows(sp, i)
            sp.wait_ge(sem("mod_add"), 28)
            sp.dma_start(mod_dram, BROW).then_inc(sem("mod_stored"), 16)
            for n in W_OUT[0]:
                sp_dense(sp, n)
            sp_moe(sp, 0)
            sp.wait_ge(sem("mod_stored"), 16)
            sp.dma_start(MODR[:, 0:5 * D], mod_dram[:, 0:5 * D].to_broadcast([P, 5 * D])).then_inc(sem("bmod_in"), 16)
            sp.dma_start(GROW, norm_g[1, 0:1, :].to_broadcast([P, D])).then_inc(sem("norm_row_in"), 16)
            sp_hyena(sp)
            sp.wait_ge(sem("yn"), 16)
            for n in W_OUT[1]:
                sp_dense(sp, n)
            sp_moe(sp, 1)
            sp.wait_ge(sem("h"), before["fin"])
            sp.dma_start(GROW, final_g.rearrange("(a d) -> a d", a=1).to_broadcast([P, D])).then_inc(sem("norm_row_in"), 16)
            for m in range(NT):
                sp.wait_ge(sem("h"), before["fin"] + m + 1)
                sp.dma_start(out[0].rearrange("(m p) d -> p m d", p=P)[:, m, :], H[:, m, :]).then_inc(sem("out_stored"), 16)
            sp.wait_ge(sem("out_stored"), 16 * NT)

        @block.scalar
        def _(act):
            a = Chain(act, sem("act_chain"))
            act_setup(act, a)
            act.wait_ge(sem("x_in"), 32)
            act_norm_sq(act, a, "n1_0", X, NT, tmpn)
            act_norm_sq(act, a, "nc_0", CX, NC, [A(104, D), A(108, D)])
            turned(act, lambda o, i: act.activation(o, i, ACT.Copy), HT, "tp", "turned", NT, 0, "n1_0")
            turned(act, lambda o, i: act.activation(o, i, ACT.Copy), HCT, "tp", "turned", NC, 0, "nc_0")
            act_project(act, a)
            act_spatial(act, a)
            act_attention(act, a)
            act.wait_ge(sem("zeroed"), 16 * ZPARTS)
            turned(act, lambda o, i: act.activation(o, i, ACT.Copy), HT, "mt_tp", "mt_turned", NT, 0)
            act_moe(act, a, 0)
            act_filter_net(act)
            act_norm_sq(act, a, "n1_1", X, NT, tmpn)
            turned(act, lambda o, i: act.activation(o, i, ACT.Copy), HT, "tp", "turned", NT, 0, "n1_1")
            act_hyena(act)
            act_moe(act, a, 1)
            act_norm_sq(act, a, "fin", X, NT, tmpn)

        @block.tensor
        def _(pe):
            pe.wait_ge(sem("consts_in"), 48)
            pe_mod(pe)
            pe.wait_ge(sem("mod_add"), 16)
            pe_turn(pe, H, "tp", NT, norm="n1_0")
            pe.wait_ge(sem("turned"), 2 * NT)
            pe_turn(pe, HC, "tp", NC, norm="nc_0")
            pe_project(pe)
            pe_turn_qk(pe)
            pe_spatial(pe)
            pe_attention(pe)
            pe.wait_ge(sem("o_dve"), 32)
            pe_turn(pe, MIX, "mt_tp", NT, strided=True)
            pe_out(pe, 0, HT)
            pe_moe(pe, 0)
            pe_filter_net(pe)
            pe.wait_ge(sem("f_arg"), 3)
            pe_turn(pe, H, "tp", NT, norm="n1_1")
            pe_hyena(pe)
            pe_out(pe, 1, Y2T)
            pe_moe(pe, 1)

        @block.vector
        def _(dve):
            v = Chain(dve, sem("dve_chain"))
            dve_setup(dve, v)
            dve_cond(dve, v)
            dve_mod(dve, range(8))
            dve.wait_ge(sem("norm_row_in"), 16)
            dve_norm(dve, v, "n1_0", X, NT, MODR[:, D:2 * D], MODR[:, 0:D], H, GROW, tmpn)
            dve_norm(dve, v, "nc_0", CX, NC, MODC[:, D:2 * D], MODC[:, 0:D], HC, GROW, tmpn)
            dve_mod(dve, range(8, len(MOD_0)))
            turned(dve, dve.tensor_copy, HT, "tp", "turned", NT, 1, "n1_0")
            turned(dve, dve.tensor_copy, HCT, "tp", "turned", NC, 1, "nc_0")
            dve_project(dve, v)
            dve_gate_norm(dve, v)
            dve_turn_qk(dve, v)
            dve_spatial(dve, v)
            dve_attention(dve, v)
            dve.wait_ge(sem("zeroed"), 16 * ZPARTS)
            turned(dve, dve.tensor_copy, HT, "mt_tp", "mt_turned", NT, 1)
            dve_out(dve, v, 0, G2T)
            dve_moe(dve, v, 0)
            dve.wait_ge(sem("bmod_in"), 64)
            dve.wait_ge(sem("norm_row_in"), 48)
            dve_norm(dve, v, "n1_1", X, NT, MODR[:, D:2 * D], MODR[:, 0:D], H, GROW, tmpn)
            turned(dve, dve.tensor_copy, HT, "tp", "turned", NT, 1, "n1_1")
            dve_hyena(dve, v)
            dve_out(dve, v, 1, G2T)
            dve_moe(dve, v, 1)
            dve.wait_ge(sem("norm_row_in"), 80)
            dve_norm(dve, v, "fin", X, NT, None, None, H, GROW, tmpn)

        @block.gpsimd
        def _(pool):
            pool.wait_ge(sem("gu_mm"), 2 * NT)
            pool.memset(ZERO, 0.0).then_inc(sem("zero_ready"), 1)
            pool_experts(pool, 0)
            pool_hyena(pool)
            pool_experts(pool, 1)


_INS = ["x", "c", "ctx", "c_ctx", "w_mod", "b_mod", "norm_g", "w_in_ab", "sink", "w_spatial", "b_spatial", "w_out_ab",
        "w_in_c", "conv_w", "conv_b", "filt_w1", "filt_b1", "filt_w2", "filt_b2", "filt_w3", "filt_freq", "filt_delta",
        "filt_bias", "w_out_c", "w_router", "e_bias", "w_gate", "w_up", "w_down", "ws_gate", "ws_up", "ws_down", "final_g"]


def kernel(**inputs):
    import concourse.bacc as _bacc
    from concourse.bass_utils import run_bass_kernel_spmd as _run

    nc = _bacc.Bacc("TRN2", target_bir_lowering=False, num_devices=1)
    arrays, args = {}, []
    for name, a in list({n: inputs[n] for n in _INS}.items()) + list(constants().items()):
        a = np.ascontiguousarray(a)
        arrays[f"in_{name}"] = a
        args.append(nc.dram_tensor(f"in_{name}", a.shape, mybir.dt.from_np(a.dtype), kind="ExternalInput").ap())
    args.append(nc.dram_tensor("out_0", (1, T, D), F32, kind="ExternalOutput").ap())
    hybrid_backbone(nc, *args)
    r = _run(nc, [arrays], core_ids=[0])
    return r.results[0]["out_0"]
```

```python
import math
from contextlib import ExitStack

import numpy as np

import concourse.bass as bass
from concourse import mybir

F32 = mybir.dt.float32
BF16 = mybir.dt.bfloat16
I32 = mybir.dt.int32
ALU = mybir.AluOpType
ACT = mybir.ActivationFunctionType
AX = mybir.AxisListType.X

P = 128
D = 1024
T = 512
CTX = 256
GRID_W = 64
KD = D // P
NT = T // P
NC = CTX // P
BANK = 512
EPS = 1e-6

N_Q, N_KV, HD = 8, 2, 64
ROPE_F = HD // 4
WINDOW = 128
ATT_W = N_Q * HD
SG_G, SG_D = 8, 64
BIG = 1.0e30

HY_Q = 4
CH = D // HY_Q
FILT_EMB, FILT_HID, BANDS = 33, 64, 16
DECAY_SHIFT = 0.05

E = 64
TOP_K = 8
GROUPS = 8
TOPK_GROUPS = 4
FE = 256
ROUTED_SCALE = 2.5
OVER = T * TOP_K // P
NBLK = E + OVER
FEW = 8
ZPARTS = 8
PK = 3
CG = 6

C_ID, C_IOTA, C_TRI, C_LT, C_E128, C_T01, C_TID, C_END = 0, 128, 256, 384, 448, 512, 516, 524
R_MASK, R_COS, R_SIN, R_END = 0, 384, 640, 896


def constants():
    small = np.zeros((P, C_END), np.float32)
    p = np.arange(P)
    small[:, C_ID:C_ID + P] = np.eye(P)
    small[:, C_IOTA:C_IOTA + P] = p[None, :]
    small[:, C_TRI:C_TRI + P] = p[:, None] < p[None, :]
    g = np.arange(GROUPS)
    small[:, C_LT:C_LT + 64] = (g[None, :] < g[:, None]).reshape(1, 64)
    small[:, C_E128:C_E128 + E] = 128.0 * np.arange(E)[None, :]
    order = np.concatenate([np.arange(0, T, 2), np.arange(1, T, 2)])
    t = order.astype(np.float32).reshape(NT, P).T
    small[:, C_T01:C_T01 + NT] = -(t / np.float32(T - 1))
    small[:, C_TID:C_TID + 8:2] = p[:, None]
    small[:, C_TID + 1:C_TID + 8:2] = 128.0 * np.arange(NT)[None, :]

    rope = np.zeros((P, R_END), np.float32)
    q, j = np.arange(P)[:, None], np.arange(3 * P)[None, :] - P
    rope[:, R_MASK:R_MASK + 3 * P] = np.where(np.abs(q - j) <= WINDOW, 0.0, -BIG)
    inv = np.power(10000.0, -np.arange(ROPE_F, dtype=np.float32) / ROPE_F).astype(np.float32)
    tok = np.arange(T)
    for axis, pos in enumerate((tok // GRID_W, tok % GRID_W)):
        ang = (pos.astype(np.float32)[:, None] * inv).astype(np.float32)
        cos, sin = np.cos(ang).astype(np.float32), np.sin(ang).astype(np.float32)
        for m in range(NT):
            rows = slice(m * P, (m + 1) * P)
            c0, s0 = R_COS + m * HD + axis * 32, R_SIN + m * HD + axis * 32
            rope[:, c0:c0 + 16], rope[:, c0 + 16:c0 + 32] = cos[rows], cos[rows]
            rope[:, s0:s0 + 16], rope[:, s0 + 16:s0 + 32] = -sin[rows], sin[rows]

    n = np.arange(T, dtype=np.float32)
    bands = np.linspace(1e-4, BANDS - 1, BANDS, dtype=np.float32)
    ang = np.float32(2.0 * math.pi / T) * n[:, None] * bands[None, :]
    feats = np.concatenate([(n / np.float32(T - 1))[:, None], np.cos(ang), np.sin(ang)], 1)[order].T
    th = np.outer(order, np.arange(T // 2) + 0.5) * (math.pi / T)
    c, s = np.cos(th), np.sin(th)
    fwd = np.stack([c, s]).reshape(2, NT, P, T // 2).transpose(2, 0, 1, 3).reshape(P, 2, 2 * T)
    inv = (np.stack([c.T, s.T]) / T).reshape(2, NT // 2, P, T).transpose(2, 0, 1, 3).reshape(P, 2, 2 * T)
    dft = np.concatenate([fwd, inv], 1).astype(np.float32)
    return {"c_small": small, "c_rope": rope, "c_feats": np.ascontiguousarray(feats, np.float32),
            "c_dft": np.ascontiguousarray(dft)}


class Chain:

    def __init__(self, eng, sem):
        self.eng, self.sem, self.n, self.off = eng, sem, 0, 0

    def __call__(self, ins):
        ins.then_inc(self.sem, 1)
        self.n += 1

    def sync(self):
        self.eng.wait_ge(self.sem, self.off + self.n)

    def enter(self, i, stride):
        self.start, self.off, self.stride = self.n, i * stride, stride

    def leave(self, count):
        assert self.n - self.start == self.stride, self.n - self.start
        self.n, self.off = self.start + count * self.stride, 0


def hybrid_backbone(nc, x, c, ctx, c_ctx, w_mod, b_mod, norm_g, w_in_ab, sink, w_spatial, b_spatial,
                    w_out_ab, w_in_c, conv_w, conv_b, filt_w1, filt_b1, filt_w2, filt_b2, filt_w3,
                    filt_freq, filt_delta, filt_bias, w_out_c, w_router, e_bias, w_gate, w_up, w_down,
                    ws_gate, ws_up, ws_down, final_g, c_small, c_rope, c_feats, c_dft, out):
    h2_dram = [nc.dram_tensor(f"h2_rows_{l}", [T, D], F32, kind="Internal").ap() for l in range(2)]
    mod_dram = nc.dram_tensor("modulation_1", [1, 6 * D], F32, kind="Internal").ap()
    y_dram = nc.dram_tensor("expert_rows", [NBLK * P, D], F32, kind="Internal").ap()

    ctxs = ExitStack()
    with ctxs:
        def sb(name, shape, dt=F32):
            return ctxs.enter_context(nc.sbuf_tensor(name, shape, dt))

        sems = {}

        def sem(name):
            return sems[name]

        def wait(eng, name, value):
            if not (isinstance(value, int) and value <= 0):
                eng.wait_ge(sem(name), value)

        def make(*names):
            for n in names:
                sems[n] = ctxs.enter_context(nc.semaphore(n))

        X = sb("residual", [P, NT, D])
        MODR = sb("modulation_rows", [P, 6 * D])
        HT = sb("features_major", [P, KD, T])
        H = sb("token_major", [P, NT, D])
        arena = sb("arena", [P, 128 * 256])
        K = sb("constants", [P, C_END])
        ones = sb("ones", [P, P])
        tid = sb("token_ids", [P, 8], BF16)
        ss = sb("square_sums", [P, 32])
        sm = sb("small_columns", [P, 640])
        ps = ctxs.enter_context(nc.psum_tensor("ps", [P, 8, BANK], F32))

        def A(kb, n, parts=P):
            return arena[0:parts, int(kb * 256):int(kb * 256) + n]

        def A3(kb, a, b, parts=P):
            return A(kb, a * b, parts).rearrange("p (a b) -> p a b", a=a)

        ident = K[:, C_ID:C_ID + P]

        SLOTS = 3
        dense = []

        def rows8(w, lo, n):
            return w.rearrange("(p k) n -> p k n", k=KD)[:, :, lo:lo + n]

        def add(*parts):
            dense.append(parts)
            return len(dense) - 1

        W_MOD = [[], []]
        for n in range(12):
            W_MOD[0].append(add((KD, 512, rows8(w_mod[0], n * 512, 512), 0, 512)))
        W_KV = add((KD, 512, rows8(w_in_ab[0], 512, 256), 0, 256))
        W_Q = add((KD, 512, rows8(w_in_ab[0], 0, 512), 0, 512))
        W_G = add((KD, 512, rows8(w_in_ab[0], 1280, 512), 0, 512))
        W_U = add((KD, 512, rows8(w_in_ab[0], 768, 512), 0, 512))
        W_OUT = [[], []]
        W_SH = [None, None]
        for n in range(12):
            W_MOD[1].append(add((KD, 512, rows8(w_mod[1], n * 512, 512), 0, 512)))
        for n in range(2):
            W_OUT[0].append(add((KD, 512, rows8(w_out_ab[0], n * 512, 512), 0, 512)))

        def add_shared(l):
            a = add((KD, 512, rows8(ws_gate[l], 0, FE), 0, FE), (KD, 512, rows8(ws_up[l], 0, FE), FE, 2 * FE))
            b = add((2, D, ws_down[l].rearrange("(p k) n -> p k n", k=2), 0, D))
            W_SH[l] = (a, b)

        add_shared(0)
        for n in range(2):
            W_OUT[1].append(add((KD, 512, w_out_c[0].rearrange("(k p) n -> p k n", p=P)[:, :, n * 512:(n + 1) * 512], 0, 512)))
        add_shared(1)
        landed = []
        total = [0] * SLOTS
        for n, parts in enumerate(dense):
            total[n % SLOTS] += 16 * len(parts)
            landed.append(total[n % SLOTS])

        make("x_in", "consts_in", "bmod_in", "norm_row_in", "consts_made", "dense_used",
             "dve_chain", "act_chain", "h2_stored", "layer_start")
        for s in range(SLOTS):
            make(f"dense_landed_{s}")
        make("mod_mm", "mod_rows_mm", "mod_rows_out", "mod_add", "mod_stored")
        NORMS = ["n1_0", "nc_0", "n2_0", "n1_1", "n2_1", "fin"]
        FM = [HT, H[:, :, :].rearrange("p m (a t) -> p (m a) t", a=2)]
        TM = [H, HT[:, :, :].rearrange("p (m a) t -> p m (a t)", a=2)]
        make("sq", "ms", "rt", "h", "tp", "turned")
        tiles_of = dict(zip(NORMS, (NT, NC, NT, NT, NT, NT)))
        before = {n: sum(tiles_of[m] for m in NORMS[:i]) for i, n in enumerate(NORMS)}
        stat_steps = {n: 1 if n in ("n1_0", "nc_0") else NT for n in NORMS}
        stats = {n: sum(stat_steps[m] for m in NORMS[:i]) for i, n in enumerate(NORMS)}
        make("row_used", "tables_in", "ws_in", "kv_mm", "kv_act", "kv_dve", "q_mm", "q_dve",
             "gu_mm", "gu_act", "qk_tp", "qk_ev", "ws_tp", "ws_ev", "sg_ln", "sg_sq", "sg_ms", "sg_mm", "sg_done",
             "s_mm", "s_dve", "s_act", "s_max", "p_act", "pt_mm", "pt_out", "o_mm", "o_dve",
             "mt_tp", "mt_turned", "yo_mm", "yo_dve")
        for l in range(2):
            make(*[f"{n}_{l}" for n in (
                "wgu0", "wgu1", "wd0", "wd1", "oh", "tok_mm", "tok", "xg0", "xg1", "xt_mm", "xt_out", "gu_m",
                "silu", "a", "at_mm", "at", "y_mm", "y_out", "yst0", "yst1", "next_range")])
        make("lg_mm", "score", "eb_in", "sel", "pos_mm", "slots", "tables", "shgu_mm", "shsilu", "sha", "shat_mm", "shat",
             "shy_mm", "shy_act", "shy_dve", "cadd", "cmm", "moe_done")
        make(*[f"cg{b}" for b in range(CG)])
        make("out_stored", "rows_asked", "over_stored_0", "over_stored_1", "zero_ready", "zeroed")
        for n in ("hy_in", "f_mm", "f_arg", "f_sin", "wz_in_0", "wz_in_1", "wz_in_2", "wf_in", "dft_in",
                  "z_mm", "z_act", "z_dve", "yt_mm", "yt_act", "yt_dup", "win", "hf_mm", "hfw", "l1sum", "l1_mm", "rl1", "sd",
                  "ky_mm", "ky_act", "ky_dve", "pp", "iv_mm", "iv_act", "yn"):
            make(n)

        block = ctxs.enter_context(nc.Block())

        cbc = A3(48, KD, P)
        PICK = A3(52, 2, P, 2)
        MROWS = [A(53, 512, 2), A(55, 512, 2)]
        MODC = A(112, 2 * D)
        CX = A3(64, NC, D)
        HC = A3(72, NC, D)
        HCT = A3(80, KD, CTX)
        GROW = A(88, D)
        tmpn = [A(92, D), A(96, D)]
        RP = A(100, R_END)
        Q = A3(104, NT, ATT_W)
        VG = A3(112, NT, 512)
        UG = A3(120, NT, 512)
        V = A3(48, NT, P)
        VC = A3(50, NC, P)
        KDUP = A3(52, NT, 2 * P)
        KCDUP = A3(62, NC, 2 * P)
        QT = A3(64, 4, T)
        KT = A3(72, 2, T)
        KCT = A3(76, 2, CTX)
        SS = [A(80, 640), A(82.5, 640)]
        PB = [A(85, 640), A(87.5, 640)]
        PT = [A(56, 640), A(58.5, 640)]
        WST = A3(92, SG_G, P)
        WSR = A3(96, SG_G, P)
        SGT = MODR[:, 0:2048]
        MIX = H
        ZERO = HT[:, 0:2, :].rearrange("p k t -> p (k t)")
        BROW = A(104, 6 * D, 1)
        ccol = sm[:, 0:16]
        sinkb = sm[:, 16:24]
        bsr = sm[0:SG_G, 24:152]
        bsc = sm[:, 152:160]
        mxc = sm[:, 192:224]
        nmc = sm[:, 224:256]
        rsc = sm[:, 256:288]
        esc = sm[:, 288:320]
        dnc = sm[:, 320:352]
        rcc = sm[:, 352:384]
        sgm = sm[:, 384:416]
        sgv = sm[:, 416:448]

        def sp_setup(sp):
            sp_dense(sp, 0)
            sp.dma_start(ccol[:, 0:8], c.rearrange("a (p k) -> p (a k)", k=KD)).then_inc(sem("consts_in"), 16)
            sp.dma_start(ccol[:, 8:16], c_ctx.rearrange("(p k) -> p k", k=KD)).then_inc(sem("consts_in"), 16)
            sp.dma_start(K[:, :], c_small).then_inc(sem("consts_in"), 16)
            for n in range(1, SLOTS):
                sp_dense(sp, n)
            sp.dma_start(MODR[:, :], b_mod[0:1, :].to_broadcast([P, 6 * D])).then_inc(sem("bmod_in"), 16)
            sp.dma_start(MODC, b_mod[0:1, 0:2 * D].to_broadcast([P, 2 * D])).then_inc(sem("bmod_in"), 16)

        def sp_layer0(sp):
            sp.dma_start(X[:, :, :], x[0].rearrange("(m p) d -> p m d", p=P)).then_inc(sem("x_in"), 16)
            sp.dma_start(CX, ctx[0].rearrange("(m p) d -> p m d", p=P)).then_inc(sem("x_in"), 16)
            sp.dma_start(GROW, norm_g[0, 0:1, :].to_broadcast([P, D])).then_inc(sem("norm_row_in"), 16)
            sp.dma_start(RP, c_rope).then_inc(sem("tables_in"), 16)
            sp.dma_start(sinkb, sink.to_broadcast([P, N_Q])).then_inc(sem("tables_in"), 16)
            sp.dma_start(bsr, b_spatial[0]).then_inc(sem("tables_in"), 16)

        def sp_zero_rows(sp, part):
            sp.wait_ge(sem("zero_ready"), 1)
            n = OVER // ZPARTS
            rows = y_dram[(E + part * n) * P:(E + part * n + n) * P, :].rearrange("(b s) d -> s b d", s=P)
            sp.dma_start(rows, ZERO.unsqueeze(1).to_broadcast([P, n, D])).then_inc(sem("zeroed"), 16)

        def sp_dense(sp, n):
            if n >= SLOTS:
                sp.wait_ge(sem("dense_used"), n - SLOTS + 1)
            for (k, w, src, lo, hi) in dense[n]:
                sp.dma_start(W(n, k, w)[:, :, lo:hi], src).then_inc(sem(f"dense_landed_{n % SLOTS}"), 16)

        def W(n, k, w):
            return A3((n % SLOTS) * 16, k, w)

        def w_wait(pe, n):
            pe.wait_ge(sem(f"dense_landed_{n % SLOTS}"), landed[n])

        def act_setup(act):
            act.wait_ge(sem("consts_in"), 48)
            act.activation(sm[:, 0:16], sm[:, 0:16], ACT.Silu).then_inc(sem("mod_rows_out"), 1)

        def dve_setup(dve):
            dve.memset(ones[:, :], 1.0).then_inc(sem("consts_made"), 1)
            dve.wait_ge(sem("consts_in"), 48)
            dve.tensor_copy(tid[:, :], K[:, C_TID:C_TID + 8]).then_inc(sem("consts_made"), 1)

        def dve_cond(dve):
            dve.wait_ge(sem("mod_rows_out"), 1)
            dve.tensor_copy(cbc, ccol[:, 0:8].unsqueeze(2).to_broadcast([P, KD, P])).then_inc(sem("consts_made"), 1)
            for i in range(2):
                dve.tensor_copy(PICK[:, i, :], ident[0:2, i:i + 1].to_broadcast([2, P])).then_inc(sem("consts_made"), 1)

        def mod_bank(t):
            return t % 6 if t < 8 else t % 8

        def pe_mod(pe):
            pe.wait_ge(sem("consts_made"), 5)

            def rows(n):
                w_wait(pe, W_MOD[0][n])
                wait(pe, "mod_rows_out", n if n >= 2 else 0)
                for k in range(KD):
                    mm = pe.matmul(ps[0:2, 6 + n % 2, :], ccol[:, k:k + 9:8], W(W_MOD[0][n], KD, 512)[:, k, :],
                                   start=k == 0, stop=k == KD - 1)
                mm.then_inc(sem("mod_rows_mm"), 1)
                used(pe, "mod_rows_mm", n + 1)

            def spread(n):
                pe.wait_ge(sem("mod_rows_out"), n + 2)
                for i in range(2):
                    t = 2 * n + i
                    wait(pe, "mod_add", t - 5)
                    pe.matmul(ps[:, mod_bank(t), :], PICK[:, i, :], MROWS[n % 2], start=True, stop=True) \
                        .then_inc(sem("mod_mm"), 1)
            rows(0)
            for n in range(4):
                if n < 3:
                    rows(n + 1)
                spread(n)
            for n in range(4, 12):
                t = n + 4
                w_wait(pe, W_MOD[0][n])
                pe.wait_ge(sem("mod_add"), 8)
                for k in range(KD):
                    mm = pe.matmul(ps[:, mod_bank(t), :], cbc[:, k, :], W(W_MOD[0][n], KD, 512)[:, k, :],
                                   start=k == 0, stop=k == KD - 1)
                mm.then_inc(sem("mod_mm"), 1)
                used(pe, "mod_mm", t + 1)

        def act_mod(act):
            for n in range(4):
                act.wait_ge(sem("mod_rows_mm"), n + 1)
                wait(act, "mod_mm", 2 * n - 2)
                act.activation(MROWS[n % 2], ps[0:2, 6 + n % 2, :], ACT.Copy).then_inc(sem("mod_rows_out"), 1)

        def pe_mod_1(pe, step):
            n, k = step // KD, step % KD
            if k == 0:
                w_wait(pe, W_MOD[1][n])
                pe.wait_ge(sem("mod_add"), 16 + n)
            mm = pe.matmul(ps[0:1, 7, :], ccol[:, k:k + 1], W(W_MOD[1][n], KD, 512)[:, k, :],
                           start=k == 0, stop=k == KD - 1)
            if k == KD - 1:
                mm.then_inc(sem("mod_mm"), 1)
                used(pe, "mod_mm", 16 + n + 1)

        def dve_mod_1(dve, n):
            if n == 0:
                dve.wait_ge(sem("bmod_in"), 48)
            dve.wait_ge(sem("mod_mm"), 16 + n + 1)
            d = BROW[:, n * 512:(n + 1) * 512]
            dve.tensor_tensor(d, ps[0:1, 7, :], d, ALU.add).then_inc(sem("mod_add"), 1)

        def used(pe, name, value):
            pe.wait_ge(sem(name), value)
            pe.sem_inc(sem("dense_used"), 1)

        MOD_0 = [(n, dst) for n in range(12) for dst in ([MODR, MODC] if n < 4 else [MODR])]

        def dve_mod(dve, steps):
            dve.wait_ge(sem("bmod_in"), 32)
            for t in steps:
                n, dst = MOD_0[t]
                dve.wait_ge(sem("mod_mm"), t + 1)
                d = dst[:, n * 512:(n + 1) * 512]
                dve.tensor_tensor(d, ps[:, mod_bank(t), :], d, ALU.add).then_inc(sem("mod_add"), 1)
            dve.wait_ge(sem("mod_add"), t + 1)

        def stat_columns(n):
            return ss[:, 16:32] if n == "nc_0" else ss[:, 0:16]

        def act_norm_sq(act, n, src, nt, junk):
            s = stat_columns(n)
            for m in range(nt):
                if m >= 2:
                    act.wait_ge(sem("sq"), before[n] + m - 1)
                act.activation(junk[m % 2], src[:, m, :], ACT.Square, accum_out=s[:, m:m + 1]) \
                    .then_inc(sem("sq"), 1)
            act.wait_ge(sem("ms"), stats[n] + 1)
            act.activation(s[:, 8:8 + nt], s[:, 4:4 + nt], ACT.Sqrt).then_inc(sem("rt"), 1)

        def dve_norm(dve, v, n, src, nt, rowA, rowB, dst, grow, tmp):
            s = stat_columns(n)
            dve.wait_ge(sem("sq"), before[n] + nt)
            dve.tensor_scalar(s[:, 4:4 + nt], s[:, 0:nt], 1.0 / D, EPS, ALU.mult, ALU.add).then_inc(sem("ms"), 1)
            dve.scalar_tensor_tensor(rowA, rowA, 1.0, grow, ALU.add, ALU.mult).then_inc(sem("row_used"), 1)
            dve.wait_ge(sem("rt"), stats[n] + 1)
            v(dve.reciprocal(s[:, 12:12 + nt], s[:, 8:8 + nt]))
            v.sync()
            dve.wait_ge(sem("row_used"), NORMS.index(n) + 1)
            for m in range(nt):
                r = s[:, 12 + m:13 + m]
                v(dve.scalar_tensor_tensor(tmp[m % 2], src[:, m, :], r, rowA, ALU.mult, ALU.mult))
                v.sync()
                dve.tensor_tensor(dst[:, m, :].rearrange("p (k j) -> p j k", k=KD),
                                  tmp[m % 2].rearrange("p (j k) -> p j k", k=KD),
                                  rowB.rearrange("p (j k) -> p j k", k=KD), ALU.add).then_inc(sem("h"), 1)

        def pe_turn(pe, src, dst_sem, nt, strided=False, norm=None):
            for m in range(nt) if isinstance(nt, int) else nt:
                if norm is not None:
                    pe.wait_ge(sem("h"), before[norm] + m + 1)
                for kk in range(2):
                    for j in range(4):
                        k = 4 * kk + j
                        s = src[:, m, k:k + 8 * (P - 1) + 1:8] if strided else src[:, m, k * P:(k + 1) * P]
                        mm = pe.transpose(ps[:, 2 * m + kk, j * P:(j + 1) * P], s, ident)
                    mm.then_inc(sem(dst_sem), 1)

        def turned(eng, copy, dst, dst_sem, done, nt, kk, norm=None):
            for m in range(nt) if isinstance(nt, int) else nt:
                eng.wait_ge(sem(dst_sem), 2 * ((before[norm] if norm else 0) + m) + kk + 1)
                copy(dst[:, 4 * kk:4 * kk + 4, m * P:(m + 1) * P],
                     ps[:, 2 * m + kk, :].rearrange("p (k t) -> p k t", k=4)).then_inc(sem(done), 1)

        def pe_project(pe):
            w_wait(pe, W_KV)
            pe.wait_ge(sem("turned"), 2 * before["n2_0"])
            w = W(W_KV, KD, 512)
            for t in range(NT + NC):
                src = HT[:, :, t * P:(t + 1) * P] if t < NT else HCT[:, :, (t - NT) * P:(t - NT + 1) * P]
                for k in range(KD):
                    mm = pe.matmul(ps[:, t, 0:256], src[:, k, :], w[:, k, 0:256], start=k == 0, stop=k == KD - 1)
                mm.then_inc(sem("kv_mm"), 1)
            used(pe, "kv_mm", NT + NC)
            t = 0
            for n, name in ((W_Q, "q_mm"), (W_G, "gu_mm"), (W_U, "gu_mm")):
                w_wait(pe, n)
                w = W(n, KD, 512)
                for m in range(NT):
                    bank = (6 + t) % 8
                    if bank < 6 and t < 8:
                        pe.wait_ge(sem("kv_act"), bank + 1)
                        pe.wait_ge(sem("kv_dve"), bank + 1)
                    if t >= 8:
                        pe.wait_ge(sem("q_dve"), t - 7)
                    for k in range(KD):
                        mm = pe.matmul(ps[:, bank, :], HT[:, k, m * P:(m + 1) * P], w[:, k, :],
                                       start=k == 0, stop=k == KD - 1)
                    mm.then_inc(sem(name), 1)
                    t += 1
                used(pe, name, NT if name == "q_mm" or n == W_G else 2 * NT)

        def act_project(act):
            for t in range(NT + NC):
                act.wait_ge(sem("kv_mm"), t + 1)
                dst = V[:, t, :] if t < NT else VC[:, t - NT, :]
                act.activation(dst, ps[:, t, P:2 * P], ACT.Copy).then_inc(sem("kv_act"), 1)
            for i in range(2 * NT):
                if i == NT:
                    act.wait_ge(sem("sg_sq"), 1)
                    act.activation(SGT, VG, ACT.Square).then_inc(sem("sg_ms"), 1)
                    act.wait_ge(sem("sg_sq"), 2)
                    act.activation(sgm, sgv, ACT.Sqrt).then_inc(sem("sg_ms"), 1)
                act.wait_ge(sem("gu_mm"), i + 1)
                dst = VG[:, i, :] if i < NT else UG[:, i - NT, :]
                act.activation(dst, ps[:, (6 + NT + i) % 8, :], ACT.Gelu_apprx_tanh).then_inc(sem("gu_act"), 1)

        def rotate(dve, v, src, nh, m, outs):
            cos = RP[:, R_COS + m * HD:R_COS + (m + 1) * HD]
            sin = RP[:, R_SIN + m * HD:R_SIN + (m + 1) * HD]
            t1, t2 = SGT[:, 0:nh * HD], SGT[:, 512:512 + nh * HD]
            v.sync()
            v(dve.tensor_tensor(t1.rearrange("p (h d) -> p h d", h=nh), src.rearrange("p (h d) -> p h d", h=nh),
                                cos.unsqueeze(1).to_broadcast([P, nh, HD]), ALU.mult))
            for half in range(2):
                def part(ap, hf):
                    return ap.rearrange("p (h a b f) -> p h a b f", h=nh, a=2, b=2)[:, :, :, hf, :]
                s = sin.rearrange("p (a b f) -> p a b f", a=2, b=2)[:, :, half, :].unsqueeze(1) \
                    .to_broadcast([P, nh, 2, ROPE_F])
                v(dve.tensor_tensor(part(t2, half), part(src, 1 - half), s, ALU.mult))
            v.sync()
            for dst, done in outs:
                ins = dve.tensor_tensor(dst, t1.rearrange("p (h d) -> p h d", h=nh),
                                        t2.rearrange("p (h d) -> p h d", h=nh), ALU.add)
                if done is None:
                    v(ins)
                else:
                    ins.then_inc(sem(done), 1)

        def dve_project(dve, v):
            dve.wait_ge(sem("tables_in"), 48)
            for t in range(NT):
                dve.wait_ge(sem("kv_act"), t + 1)
                if t:
                    dve.wait_ge(sem("kv_dve"), t)
                kd = KDUP[:, t, :].rearrange("p (g r d) -> p g r d", g=2, r=2)
                rotate(dve, v, ps[:, t, 0:P], 2, t, [(kd[:, :, 0, :], None), (kd[:, :, 1, :], "kv_dve")])
            for t in range(NC):
                dve.wait_ge(sem("kv_act"), NT + t + 1)
                src = ps[:, NT + t, 0:P].rearrange("p (g d) -> p g d", g=2)
                kd = KCDUP[:, t, :].rearrange("p (g r d) -> p g r d", g=2, r=2)
                v(dve.tensor_copy(kd[:, :, 0, :], src))
                dve.tensor_copy(kd[:, :, 1, :], src).then_inc(sem("kv_dve"), 1)
            for m in range(NT):
                dve.wait_ge(sem("q_mm"), m + 1)
                dve.wait_ge(sem("kv_dve"), NT + NC)
                if m:
                    dve.wait_ge(sem("q_dve"), m)
                rotate(dve, v, ps[:, (6 + m) % 8, :], N_Q, m,
                       [(Q[:, m, :].rearrange("p (h d) -> p h d", h=N_Q), "q_dve")])

        def pe_turn_qk(pe):
            pe.wait_ge(sem("q_dve"), NT)
            pe.wait_ge(sem("kv_dve"), NT + NC)
            pe.wait_ge(sem("gu_act"), 2 * NT)
            for m in range(NT):
                for j in range(4):
                    mm = pe.transpose(ps[:, m, j * P:(j + 1) * P], Q[:, m, j * P:(j + 1) * P], ident)
                mm.then_inc(sem("qk_tp"), 1)
            for g in range(2):
                for m in range(NT):
                    mm = pe.transpose(ps[:, 4 + g, m * P:(m + 1) * P], KDUP[:, m, g * P:(g + 1) * P], ident)
                mm.then_inc(sem("qk_tp"), 1)
            for g in range(2):
                for m in range(NC):
                    i = g * NC + m
                    mm = pe.transpose(ps[:, 6, i * P:(i + 1) * P], KCDUP[:, m, g * P:(g + 1) * P], ident)
            mm.then_inc(sem("qk_tp"), 1)
            pe.wait_ge(sem("tables_in"), 48)
            pe.transpose(ps[:, 7, 0:SG_G], bsr, ident[0:SG_G, 0:SG_G]).then_inc(sem("qk_tp"), 1)

        def dve_turn_qk(dve):
            for m in range(NT):
                dve.wait_ge(sem("qk_tp"), m + 1)
                dve.tensor_copy(QT[:, :, m * P:(m + 1) * P], ps[:, m, :].rearrange("p (j t) -> p j t", j=4)) \
                    .then_inc(sem("qk_ev"), 1)
            for g in range(2):
                dve.wait_ge(sem("qk_tp"), NT + g + 1)
                dve.tensor_copy(KT[:, g, :], ps[:, 4 + g, :]).then_inc(sem("qk_ev"), 1)
            dve.wait_ge(sem("qk_tp"), NT + 3)
            dve.tensor_copy(KCT, ps[:, 6, :].rearrange("p (g t) -> p g t", g=2)).then_inc(sem("qk_ev"), 1)
            dve.wait_ge(sem("qk_tp"), NT + 4)
            dve.tensor_copy(bsc, ps[:, 7, 0:SG_G]).then_inc(sem("qk_ev"), 1)

        def pe_spatial(pe):
            pe.wait_ge(sem("qk_ev"), NT + 4)
            pe.wait_ge(sem("ws_in"), 16)
            for b in range(2):
                for j in range(4):
                    mm = pe.transpose(ps[:, b, j * P:(j + 1) * P], WSR[:, 4 * b + j, :], ident)
                mm.then_inc(sem("ws_tp"), 1)
            pe.wait_ge(sem("ws_ev"), 2)
            pe.wait_ge(sem("sg_ln"), 1)
            for g in range(SG_G):
                pe.matmul(ps[:, g, 0:NT * SG_D], WST[:, g, :], VG[:, :, g * SG_D:(g + 1) * SG_D],
                          start=True, stop=True).then_inc(sem("sg_mm"), 1)

        def act_spatial(act):
            for b in range(2):
                act.wait_ge(sem("ws_tp"), b + 1)
                act.activation(WST[:, 4 * b:4 * b + 4, :], ps[:, b, :].rearrange("p (g i) -> p g i", g=4), ACT.Copy) \
                    .then_inc(sem("ws_ev"), 1)

        def dve_gate_norm(dve, v):
            vg = VG.rearrange("p m (g d) -> p (m g) d", g=SG_G)
            dve.wait_ge(sem("gu_act"), NT)
            dve.wait_ge(sem("q_dve"), NT)
            v(dve.tensor_reduce(sgm, vg, AX, ALU.add))
            v.sync()
            v(dve.tensor_scalar(sgm, sgm, 1.0 / SG_D, None, ALU.mult))
            v.sync()
            dve.tensor_tensor(vg, vg, sgm.unsqueeze(2).to_broadcast([P, 32, SG_D]), ALU.subtract) \
                .then_inc(sem("sg_sq"), 1)
            dve.wait_ge(sem("sg_ms"), 1)
            v(dve.tensor_reduce(sgv, SGT.rearrange("p (g d) -> p g d", d=SG_D), AX, ALU.add))
            v.sync()
            dve.tensor_scalar(sgv, sgv, 1.0 / SG_D, EPS, ALU.mult, ALU.add).then_inc(sem("sg_sq"), 1)
            dve.wait_ge(sem("sg_ms"), 2)
            v(dve.reciprocal(sgv, sgm))
            v.sync()
            dve.wait_ge(sem("sg_sq"), 2)
            dve.tensor_tensor(vg, vg, sgv.unsqueeze(2).to_broadcast([P, 32, SG_D]), ALU.mult) \
                .then_inc(sem("sg_ln"), 1)

        def dve_spatial(dve):
            for g in range(SG_G):
                dve.wait_ge(sem("sg_mm"), g + 1)
                dve.wait_ge(sem("gu_act"), 2 * NT)
                cols = slice(g * SG_D, (g + 1) * SG_D)
                dve.scalar_tensor_tensor(MIX[:, :, ATT_W + g * SG_D:ATT_W + (g + 1) * SG_D],
                                         ps[:, g, 0:NT * SG_D].rearrange("p (m d) -> p m d", m=NT), bsc[:, g:g + 1],
                                         UG[:, :, cols], ALU.add, ALU.mult).then_inc(sem("sg_done"), 1)

        UNITS = [(m, h) for m in range(NT) for h in range(N_Q)]

        def span(m):
            lo, hi = max(m - 1, 0), min(m + 2, NT)
            return lo, hi, (hi - lo) * P

        def pe_attention(pe):
            pe.wait_ge(sem("sg_done"), SG_G)

            def scores(u):
                m, h = UNITS[u]
                lo, hi, n = span(m)
                r = slice(HD * (h % 2), HD * (h % 2) + HD)
                if u >= 2:
                    pe.wait_ge(sem("s_dve"), u - 1)
                    pe.wait_ge(sem("s_act"), u - 1)
                qT = QT[r, h // 2, m * P:(m + 1) * P]
                pe.matmul(ps[:, 2 * (u % 2), 0:n], qT, KT[r, h // 4, lo * P:hi * P], start=True, stop=True)
                pe.matmul(ps[:, 2 * (u % 2) + 1, 0:CTX], qT, KCT[r, h // 4, :], start=True, stop=True) \
                    .then_inc(sem("s_mm"), 1)

            def turn(u):
                m, h = UNITS[u]
                n = span(m)[2] // P + NC
                pe.wait_ge(sem("p_act"), u + 1)
                if u:
                    pe.wait_ge(sem("pt_out"), 2 * u)
                for b in range(n):
                    mm = pe.transpose(ps[:, 4 + b // 4, (b % 4) * P:(b % 4 + 1) * P], PB[u % 2][:, b * P:(b + 1) * P], ident)
                mm.then_inc(sem("pt_mm"), 1)

            def values(u):
                m, h = UNITS[u]
                lo, hi, n = span(m)
                g = slice(HD * (h // 4), HD * (h // 4) + HD)
                pe.wait_ge(sem("pt_out"), 2 * u + 2)
                if u:
                    pe.wait_ge(sem("o_dve"), u)
                nb = n // P + NC
                for b in range(nb):
                    vb = V[:, lo + b, g] if b < hi - lo else VC[:, b - (hi - lo), g]
                    mm = pe.matmul(ps[:, 6, 0:HD], PT[u % 2][:, b * P:(b + 1) * P], vb,
                                   start=b == 0, stop=b == nb - 1)
                mm.then_inc(sem("o_mm"), 1)

            scores(0)
            for u in range(len(UNITS)):
                if u + 1 < len(UNITS):
                    scores(u + 1)
                pe_mod_1(pe, 3 * u)
                pe_mod_1(pe, 3 * u + 1)
                turn(u)
                pe_mod_1(pe, 3 * u + 2)
                values(u)

        def act_attention(act):
            act.wait_ge(sem("tables_in"), 48)

            def scale_ctx(u):
                n = span(UNITS[u][0])[2]
                act.wait_ge(sem("s_mm"), u + 1)
                if u >= 2:
                    act.wait_ge(sem("p_act"), u - 1)
                act.activation(SS[u % 2][:, n:n + CTX], ps[:, 2 * (u % 2) + 1, 0:CTX], ACT.Copy, scale=HD ** -0.5) \
                    .then_inc(sem("s_act"), 1)

            def exps(u):
                m, h = UNITS[u]
                n = span(m)[2] + CTX
                act.wait_ge(sem("s_max"), u + 1)
                if u >= 2:
                    act.wait_ge(sem("pt_mm"), u - 1)
                act.activation(esc[:, u:u + 1], sinkb[:, h:h + 1], ACT.Exp, bias=nmc[:, u:u + 1]).then_inc(sem("act_chain"), 1)
                act.activation(PB[u % 2][:, 0:n], SS[u % 2][:, 0:n], ACT.Exp, bias=nmc[:, u:u + 1],
                               accum_out=rsc[:, u:u + 1]).then_inc(sem("p_act"), 1)

            def turned_p(u):
                act.wait_ge(sem("pt_mm"), u + 1)
                if u >= 2:
                    act.wait_ge(sem("o_mm"), u - 1)
                act.activation(PT[u % 2][:, 0:512], ps[:, 4, :], ACT.Copy).then_inc(sem("pt_out"), 1)

            scale_ctx(0)
            for u in range(len(UNITS)):
                exps(u)
                if u + 1 < len(UNITS):
                    scale_ctx(u + 1)
                turned_p(u)

        def dve_attention(dve, v):
            dve.wait_ge(sem("tables_in"), 48)

            def masked(u):
                m, h = UNITS[u]
                lo, hi, n = span(m)
                first = (lo - m + 1) * P
                dve.wait_ge(sem("s_mm"), u + 1)
                if u >= 2:
                    dve.wait_ge(sem("p_act"), u - 1)
                dve.scalar_tensor_tensor(SS[u % 2][:, 0:n], ps[:, 2 * (u % 2), 0:n], HD ** -0.5,
                                         RP[:, R_MASK + first:R_MASK + first + n], ALU.mult, ALU.add) \
                    .then_inc(sem("s_dve"), 1)
                dve.wait_ge(sem("s_dve"), u + 1)
                dve.wait_ge(sem("s_act"), u + 1)
                v(dve.tensor_reduce(mxc[:, u:u + 1], SS[u % 2][:, 0:n + CTX], AX, ALU.max))
                v.sync()
                dve.tensor_scalar(nmc[:, u:u + 1], mxc[:, u:u + 1], sinkb[:, h:h + 1], -1.0, ALU.max, ALU.mult) \
                    .then_inc(sem("s_max"), 1)

            def finish(u):
                m, h = UNITS[u]
                n = span(m)[2] // P + NC
                dve.wait_ge(sem("pt_mm"), u + 1)
                if u >= 2:
                    dve.wait_ge(sem("o_mm"), u - 1)
                w = max(n - 4, 0) * P
                if w:
                    dve.tensor_copy(PT[u % 2][:, 512:512 + w], ps[:, 5, 0:w]).then_inc(sem("pt_out"), 1)
                else:
                    dve.sem_inc(sem("pt_out"), 1)
                dve.wait_ge(sem("act_chain"), u + 1)
                v(dve.tensor_tensor(dnc[:, u:u + 1], rsc[:, u:u + 1], esc[:, u:u + 1], ALU.add))
                v.sync()
                v(dve.reciprocal(rcc[:, u:u + 1], dnc[:, u:u + 1]))
                v.sync()
                dve.wait_ge(sem("o_mm"), u + 1)
                dve.tensor_scalar(MIX[:, m, h * HD:(h + 1) * HD], ps[:, 6, 0:HD], rcc[:, u:u + 1], None, ALU.mult) \
                    .then_inc(sem("o_dve"), 1)

            masked(0)
            for u in range(len(UNITS)):
                if u + 1 < len(UNITS):
                    masked(u + 1)
                for n in range(3 * u // KD, (3 * u + 3) // KD):
                    dve_mod_1(dve, n)
                finish(u)

        def pe_out(pe, l, src):
            if l == 0:
                pe.wait_ge(sem("mt_turned"), 2 * NT)
            else:
                pe.wait_ge(sem("yn"), 4 * HY_Q)
            norm = f"n2_{l}"
            for m in range(NT):
                for n in range(2):
                    w_wait(pe, W_OUT[l][n])
                    w = W(W_OUT[l][n], KD, 512)
                    for k in range(KD):
                        mm = pe.matmul(ps[:, 2 * m + n, :], src[:, k, m * P:(m + 1) * P], w[:, k, :],
                                       start=k == 0, stop=k == KD - 1)
                    mm.then_inc(sem("yo_mm"), 1)
                    if m == NT - 1:
                        used(pe, "yo_mm", l * 2 * NT + 2 * m + n + 1)
                if m >= 2:
                    pe_router(pe, l, m - 2)
                if m:
                    pe_turn(pe, TM[l], "tp", [m - 1], norm=norm)
            pe_router(pe, l, NT - 2)
            pe_turn(pe, TM[l], "tp", [NT - 1], norm=norm)
            pe_router(pe, l, NT - 1)

        def act_stats(act, norm, m, junk):
            if m >= 2:
                act.wait_ge(sem("sq"), before[norm] + m - 1)
            act.activation(junk[m % 2], X[:, m, :], ACT.Square, accum_out=ss[:, m:m + 1]).then_inc(sem("sq"), 1)
            act.wait_ge(sem("ms"), stats[norm] + m + 1)
            act.activation(ss[:, 8 + m:9 + m], ss[:, 4 + m:5 + m], ACT.Sqrt).then_inc(sem("rt"), 1)

        def act_combine(act, l):
            for m in range(NT):
                act.wait_ge(sem("layer_start"), l * NT + m + 1)
                act_stats(act, ("n1_1", "fin")[l], m, [A(108, D), A(112, D)])

        def act_out(act, l):
            norm = f"n2_{l}"

            def turn(m):
                turned(act, lambda o, i: act.activation(o, i, ACT.Copy), FM[l], "tp", "turned", [m], 0, norm)
            for m in range(NT):
                act.wait_ge(sem("yo_dve"), l * 2 * NT + 2 * m + 2)
                act_stats(act, norm, m, [A(80, D), A(84, D)])
                if m:
                    turn(m - 1)
            turn(NT - 1)

        def dve_out(dve, v, l, tmp):
            norm = f"n2_{l}"
            rowA, rowB = MODR[:, 4 * D:5 * D], MODR[:, 3 * D:4 * D]
            dve.wait_ge(sem("norm_row_in"), 16 * (2 + 2 * l))
            dve.scalar_tensor_tensor(rowA, rowA, 1.0, GROW, ALU.add, ALU.mult).then_inc(sem("row_used"), 1)
            for m in range(NT):
                if m:
                    dve.wait_ge(sem("h"), before[norm] + m)
                for n in range(2):
                    cols = slice(n * 512, (n + 1) * 512)
                    dve.wait_ge(sem("yo_mm"), l * 2 * NT + 2 * m + n + 1)
                    y = tmp[n][:, 0:512]
                    v.sync()
                    v(dve.tensor_tensor(y, ps[:, 2 * m + n, :], MODR[:, 2 * D + n * 512:2 * D + (n + 1) * 512], ALU.mult))
                    v.sync()
                    dve.tensor_tensor(X[:, m, cols], X[:, m, cols], y, ALU.add).then_inc(sem("yo_dve"), 1)
                dve.wait_ge(sem("sq"), before[norm] + m + 1)
                dve.tensor_scalar(ss[:, 4 + m:5 + m], ss[:, m:m + 1], 1.0 / D, EPS, ALU.mult, ALU.add).then_inc(sem("ms"), 1)
                if m:
                    turned(dve, dve.tensor_copy, FM[l], "tp", "turned", [m - 1], 1, norm)
                dve.wait_ge(sem("rt"), stats[norm] + m + 1)
                v(dve.reciprocal(ss[:, 12 + m:13 + m], ss[:, 8 + m:9 + m]))
                v.sync()
                dve.wait_ge(sem("row_used"), NORMS.index(norm) + 1)
                dve.wait_ge(sem("yo_dve"), l * 2 * NT + 2 * m + 2)
                v(dve.scalar_tensor_tensor(tmp[m % 2], X[:, m, :], ss[:, 12 + m:13 + m], rowA, ALU.mult, ALU.mult))
                v.sync()
                dve.tensor_tensor(TM[l][:, m, :].rearrange("p (k j) -> p j k", k=KD),
                                  tmp[m % 2].rearrange("p (j k) -> p j k", k=KD),
                                  rowB.rearrange("p (j k) -> p j k", k=KD), ALU.add).then_inc(sem("h"), 1)
            turned(dve, dve.tensor_copy, FM[l], "tp", "turned", [NT - 1], 1, norm)

        G2T = [A(92, D), A(96, D)]
        RTR = A3(100, KD, E)
        EB = A(102, E)
        EXG = [A(48, D), A(52, D)]
        EXT = [A3(56, KD, P), A3(60, KD, P)]
        EY = [A(64, D), A(68, D)]
        ESG = [A(72, FE), A(73, FE)]
        EA = [A(74, FE), A(75, FE)]
        EAT = [A3(76, 2, P), A3(77, 2, P)]
        EOH = [A(78, 256).bitcast(BF16).rearrange("p (m s) -> p m s", m=NT), A(79, 256).bitcast(BF16).rearrange("p (m s) -> p m s", m=NT)]

        def t64(kb):
            return A3(kb, NT, E)
        SC, BI, MK, MR, SEL, WTS, POS, POSM, SLM = [t64(104 + i) for i in range(9)]
        M8 = A3(113, 32, 8)
        CMP, CMQ = A(114, 256), A(115, 256)
        GS, RK, GM, PEN = [A(116 + 0.125 * i, 32) for i in range(4)]
        T8, S8, W8 = [A3(116.5 + 0.125 * i, NT, 8) for i in range(3)]
        S8I = A3(116.875, NT, 8).bitcast(I32)
        CNT, OV, OVC, OVS, OVT = [A(117 + 0.25 * i, E) for i in range(5)]
        SW, RW = A(118.25, 4), A(118.3125, 4)
        OVE = A(118.5, 32, 1)
        OVI = A(118.75, 36, 1).bitcast(I32)
        IOR = A(119, P)
        TOKI = [A(119.5, 1).bitcast(I32), A(119.5625, 1).bitcast(I32)]
        BIGT = A(120, 2048)
        WGU = [A3(0, KD, 512), A3(24, KD, 512)]
        WD = [A3(16, 2, D), A3(40, 2, D)]
        CGB = [HT[:, 2 * i:2 * i + 2, :].rearrange("p k t -> p (k t)") for i in range(4)] + [A(80, D), A(84, D)]

        def sp_router(sp, l):
            sp.dma_start(RTR, w_router[l].rearrange("(p k) e -> p k e", k=KD)).then_inc(sem("eb_in"), 16)
            sp.dma_start(EB, e_bias[l:l + 1, :].to_broadcast([P, E])).then_inc(sem("eb_in"), 16)

        def e_view(w, l, e):
            v = w[l].rearrange("e (p k) f -> p e k f", k=KD)
            return v[:, bass.ds(e, 1), :, :].rearrange("p a k f -> p (a k) f")

        def sp_gate_up(sp, l, e, n, p):
            wait(sp, f"gu_m_{l}", n - 1)
            sp.dma_start(WGU[p][:, :, 0:FE], e_view(w_gate, l, e)).then_inc(sem(f"wgu{p}_{l}"), 16)
            sp.dma_start(WGU[p][:, :, FE:2 * FE], e_view(w_up, l, e)).then_inc(sem(f"wgu{p}_{l}"), 16)

        def sp_down(sp, l, e, n, p):
            wait(sp, f"y_mm_{l}", n * 2 - 2)
            v = w_down[l].rearrange("e (p k) n -> p e k n", k=2)[:, bass.ds(e, 1), :, :]
            sp.dma_start(WD[p], v.rearrange("p a k n -> p (a k) n")).then_inc(sem(f"wd{p}_{l}"), 16)

        def sp_experts(sp, l):
            if l == 0:
                sp_filter_net(sp)
            sp.wait_ge(sem("dense_used"), W_SH[l][0] + 1)
            sp_gate_up(sp, l, 0, 0, 0)
            if l == 0:
                sp_gate_up(sp, l, 1, 1, 1)
                sp.wait_ge(sem("dense_used"), W_SH[l][1] + 1)
                sp_down(sp, l, 0, 0, 0)
            else:
                sp_down(sp, l, 0, 0, 0)
                sp.wait_ge(sem("dense_used"), W_SH[l][1] + 1)
                sp_gate_up(sp, l, 1, 1, 1)

            def pair(i):
                for p in range(2):
                    n = i * 2 + p
                    sp_gate_up(sp, l, n, n, p)
                    sp_down(sp, l, n - 1, n - 1, 1 - p)
            pair(1)
            with sp.Fori(2, E // 2) as i:
                pair(i)
            sp_down(sp, l, E - 1, E - 1, 1)
            sp.wait_ge(sem("tables"), l + 1)
            nov = sp_nov(sp, l)

            def over(i):
                for p in range(2):
                    with sp.If(nov > i * 2 + p):
                        e = sp.value_load(OVI[0:1, bass.ds(i * 2 + p, 1)], min_val=0, max_val=E - 1)
                        sp_gate_up(sp, l, e, i * 2 + p + E, p)
                        sp_down(sp, l, e, i * 2 + p + E, p)
            over_loop(sp, nov, over)

        def over_loop(eng, nov, pair):
            with eng.Fori(0, FEW // 2) as i:
                pair(i)
            with eng.If(nov > FEW):
                with eng.Fori(FEW // 2, OVER // 2) as i:
                    pair(i)

        def sp_nov(eng, l):
            return eng.value_load(OVI[0:1, 32:33], min_val=0, max_val=OVER)

        def pe_router(pe, l, m):
            pe.wait_ge(sem("turned"), 2 * (before[f"n2_{l}"] + m + 1))
            pe.wait_ge(sem("eb_in"), l * 32 + 32)
            for k in range(KD):
                mm = pe.matmul(ps[:, 0, m * E:(m + 1) * E], FM[l][:, k, m * P:(m + 1) * P], RTR[:, k, :],
                               start=k == 0, stop=k == KD - 1)
            if m == NT - 1:
                mm.then_inc(sem("lg_mm"), 1)

        def act_router(act, l):
            act.wait_ge(sem("lg_mm"), l + 1)
            act.wait_ge(sem("mod_stored"), 16)
            act.activation(SC, ps[:, 0, 0:NT * E].rearrange("p (m e) -> p m e", m=NT), ACT.Sigmoid) \
                .then_inc(sem("score"), 1)

        def dve_select(dve, v, l):
            bc = lambda ap, n: ap.unsqueeze(2).to_broadcast([P, ap.shape[1], n])
            row = lambda ap: ap.unsqueeze(1).to_broadcast([P, NT, E])

            def do(ins):
                v(ins)
                v.sync()
            dve.wait_ge(sem("score"), l * (1 + NT * PK) + 1)
            do(dve.tensor_tensor(BI, SC, row(EB), ALU.add))
            bg = BI.rearrange("p m (g e) -> p (m g) e", g=GROUPS)
            for i in range(32):
                v(dve.max(M8[:, i, :], bg[:, i, :]))
            v.sync()
            do(dve.tensor_tensor(GS, M8[:, :, 0], M8[:, :, 1], ALU.add))
            gs3 = GS.rearrange("p (m g) -> p m g", m=NT)
            c4 = lambda ap: ap.rearrange("p (m g h) -> p m g h", m=NT, g=GROUPS)
            other = gs3.unsqueeze(2).to_broadcast([P, NT, GROUPS, GROUPS])
            own = gs3.unsqueeze(3).to_broadcast([P, NT, GROUPS, GROUPS])
            v(dve.tensor_tensor(c4(CMP), other, own, ALU.is_gt))
            do(dve.tensor_tensor(c4(CMQ), other, own, ALU.is_equal))
            lt = K[:, C_LT:C_LT + 64].unsqueeze(1).to_broadcast([P, NT, 64])
            do(dve.tensor_tensor(CMQ.rearrange("p (m x) -> p m x", m=NT), CMQ.rearrange("p (m x) -> p m x", m=NT), lt, ALU.mult))
            do(dve.tensor_tensor(CMP, CMP, CMQ, ALU.add))
            do(dve.tensor_reduce(RK, CMP.rearrange("p (g h) -> p g h", h=GROUPS), AX, ALU.add))
            do(dve.tensor_scalar(GM, RK, TOPK_GROUPS - 0.5, None, ALU.is_lt))
            v(dve.tensor_scalar(PEN, GM, -1.0, BIG, ALU.add, ALU.mult))
            mg = MK.rearrange("p m (g e) -> p (m g) e", g=GROUPS)
            do(dve.tensor_tensor(mg, bg, bc(GM, 8), ALU.mult))
            do(dve.tensor_tensor(mg, mg, bc(PEN, 8), ALU.add))
            for m in range(NT):
                v(dve.max(T8[:, m, :], MK[:, m, :]))
            v.sync()
            for m in range(NT):
                v(dve.match_replace(MR[:, m, :], T8[:, m, :], MK[:, m, :], -3.0 * BIG))
            v.sync()
            dve.tensor_tensor(SEL, MR, MK, ALU.not_equal).then_inc(sem("sel"), 1)
            dve.wait_ge(sem("sel"), l + 1)
            do(dve.tensor_tensor(WTS, SC, SEL, ALU.mult))
            do(dve.tensor_reduce(SW, WTS, AX, ALU.add))
            do(dve.reciprocal(RW, SW))
            do(dve.tensor_scalar(RW, RW, ROUTED_SCALE, None, ALU.mult))
            do(dve.tensor_tensor(WTS, WTS, bc(RW, E), ALU.mult))
            dve.wait_ge(sem("pos_mm"), l + 1)
            v(dve.tensor_copy(POS, ps[:, 1, 0:NT * E].rearrange("p (m e) -> p m e", m=NT)))
            do(dve.tensor_copy(CNT, ps[:, 2, 0:E]))
            do(dve.scalar_tensor_tensor(POSM, POS, 1.0, SEL, ALU.add, ALU.mult))
            v(dve.tensor_scalar(POSM, POSM, -1.0, None, ALU.add))
            do(dve.tensor_scalar(OV, CNT, P + 0.5, None, ALU.is_gt))
            for j in range(2, NT):
                do(dve.scalar_tensor_tensor(OV, CNT, j * P + 0.5, OV, ALU.is_gt, ALU.add))
            do(dve.tensor_tensor_scan(OVC, ones[:, 0:E], OV, 0.0, ALU.mult, ALU.add))
            do(dve.tensor_tensor(OVS, OVC, OV, ALU.subtract))
            do(dve.tensor_scalar(OVS, OVS, E - 1.0, 128.0, ALU.add, ALU.mult))
            do(dve.tensor_tensor(OVS, OVS, K[:, C_E128:C_E128 + E], ALU.subtract))
            do(dve.tensor_scalar(SLM, POS, P - 0.5, None, ALU.is_gt))
            do(dve.tensor_tensor(SLM, SLM, row(OVS), ALU.mult))
            do(dve.tensor_tensor(SLM, SLM, POS, ALU.add))
            do(dve.tensor_tensor(SLM, SLM, row(K[:, C_E128:C_E128 + E]), ALU.add))
            do(dve.scalar_tensor_tensor(SLM, SLM, 1.0, SEL, ALU.add, ALU.mult))
            dve.tensor_scalar(SLM, SLM, -1.0, None, ALU.add).then_inc(sem("slots"), 1)

        def dve_over_table(dve, v, l):
            def do(ins):
                v(ins)
                v.sync()
            j3 = BIGT[0:1, :].rearrange("p (j e) -> p j e", j=32)
            do(dve.tensor_tensor(j3, OVC[0:1, :].unsqueeze(1).to_broadcast([1, 32, E]),
                                 K[0:1, C_IOTA:C_IOTA + 32].unsqueeze(2).to_broadcast([1, 32, E]), ALU.is_le))
            do(dve.tensor_reduce(OVE, j3, AX, ALU.add))
            do(dve.tensor_scalar(OVE, OVE, E - 1.0, None, ALU.min))
            v(dve.tensor_copy(OVI[:, 0:32], OVE))
            v(dve.tensor_copy(OVI[:, 32:33], OVC[0:1, E - 1:E]))
            dve.tensor_scalar(IOR, K[:, C_IOTA:C_IOTA + P], float(E * P), None, ALU.add).then_inc(sem(f"next_range_{l}"), 1)

        def dve_slot_table(dve, v, l, tiles):
            def do(ins):
                v(ins)
                v.sync()
            if 0 in tiles:
                for m in range(NT):
                    v(dve.max(S8[:, m, :], SLM[:, m, :]))
                v.sync()
                v(dve.tensor_copy(S8I, S8))
            hit = BIGT[:, 0:512].rearrange("p (k e) -> p k e", k=8)
            for m in tiles:
                do(dve.tensor_tensor(hit, SLM[:, m, :].unsqueeze(1).to_broadcast([P, 8, E]),
                                     S8[:, m, :].unsqueeze(2).to_broadcast([P, 8, E]), ALU.is_equal))
                do(dve.tensor_tensor(hit, hit, WTS[:, m, :].unsqueeze(1).to_broadcast([P, 8, E]), ALU.mult))
                do(dve.tensor_reduce(W8[:, m, :], hit, AX, ALU.add))
            if NT - 1 in tiles:
                dve.engine_nop().then_inc(sem("tables"), 1)

        def pe_positions(pe, l):
            pe.wait_ge(sem("sel"), l + 1)
            pe.wait_ge(sem("consts_made"), 1)
            for m in range(NT):
                for j in range(m + 1):
                    pe.matmul(ps[:, 1, m * E:(m + 1) * E], ones[:, :] if j < m else K[:, C_TRI:C_TRI + P], SEL[:, j, :],
                              start=j == 0, stop=j == m)
            for m in range(NT):
                mm = pe.matmul(ps[:, 2, 0:E], ones[:, :], SEL[:, m, :], start=m == 0, stop=m == NT - 1)
            mm.then_inc(sem("pos_mm"), 1)

        def pe_shared(pe, l, tiles):
            a, b = W_SH[l]
            if tiles is not None:
                w_wait(pe, a)
                w = W(a, KD, 512)
                for m in tiles:
                    bank = 3 + m
                    for k in range(KD):
                        mm = pe.matmul(ps[:, bank, :], FM[l][:, k, m * P:(m + 1) * P], w[:, k, :],
                                       start=k == 0, stop=k == KD - 1)
                    mm.then_inc(sem("shgu_mm"), 1)
                if NT - 1 in tiles:
                    used(pe, "shgu_mm", l * NT + NT)
                return
            w_wait(pe, b)
            w = W(b, 2, D)
            for m in range(NT):
                pe.wait_ge(sem("sha"), l * NT + m + 1)
                if m:
                    pe.wait_ge(sem("shat"), l * NT + m)
                for k in range(2):
                    mm = pe.transpose(ps[:, 0, k * P:(k + 1) * P], EA[m % 2][:, k * P:(k + 1) * P], ident)
                mm.then_inc(sem("shat_mm"), 1)
                pe.wait_ge(sem("shat"), l * NT + m + 1)
                for n in range(2):
                    t = 2 * m + n
                    bank = 3 + t % 4
                    if t < 4:
                        pe.wait_ge(sem("sha"), l * NT + bank - 2)
                    else:
                        pe.wait_ge(sem("shy_act"), l * NT + (t - 4) // 2 + 1)
                        pe.wait_ge(sem("shy_dve"), l * NT + (t - 4) // 2 + 1)
                    for k in range(2):
                        mm = pe.matmul(ps[:, bank, :], EAT[m % 2][:, k, :], w[:, k, n * 512:(n + 1) * 512],
                                       start=k == 0, stop=k == 1)
                    mm.then_inc(sem("shy_mm"), 1)
            used(pe, "shy_mm", l * 2 * NT + 2 * NT)

        SHG = BIGT[:, 0:1024].rearrange("p (m f) -> p m f", m=NT)

        def act_shared(act, l):
            for m in range(NT):
                act.wait_ge(sem("shgu_mm"), l * NT + m + 1)
                act.activation(SHG[:, m, :], ps[:, 3 + m, 0:FE], ACT.Silu).then_inc(sem("shsilu"), 1)
            for m in range(NT):
                act.wait_ge(sem("shat_mm"), l * NT + m + 1)
                if m >= 2:
                    act.wait_ge(sem("shy_mm"), l * 2 * NT + 2 * m - 2)
                act.activation(EAT[m % 2], ps[:, 0, 0:FE].rearrange("p (k t) -> p k t", k=2), ACT.Copy) \
                    .then_inc(sem("shat"), 1)
                act.wait_ge(sem("shy_mm"), l * 2 * NT + 2 * m + 1)
                act.activation(H[:, m, 0:512], ps[:, 3 + (2 * m) % 4, :], ACT.Copy).then_inc(sem("shy_act"), 1)

        def dve_shared(dve, l, tiles):
            if tiles is not None:
                for m in tiles:
                    dve.wait_ge(sem("shsilu"), l * NT + m + 1)
                    if m >= 2:
                        dve.wait_ge(sem("shat_mm"), l * NT + m - 1)
                    dve.tensor_tensor(EA[m % 2].rearrange("p (k j) -> p j k", k=2),
                                      SHG[:, m, :].rearrange("p (j k) -> p j k", k=2),
                                      ps[:, 3 + m, FE:2 * FE].rearrange("p (j k) -> p j k", k=2), ALU.mult) \
                        .then_inc(sem("sha"), 1)
                return
            for m in range(NT):
                dve.wait_ge(sem("shy_mm"), l * 2 * NT + 2 * m + 2)
                dve.tensor_copy(H[:, m, 512:1024], ps[:, 3 + (2 * m + 1) % 4, :]).then_inc(sem("shy_dve"), 1)

        def pe_token_ids(pe, l, n, p):
            pe.wait_ge(sem(f"oh_{l}"), n + 1)
            pe.wait_ge(sem(f"tok_{l}"), n)
            for m in range(NT):
                mm = pe.matmul(ps[:, 7, 2 * p:2 * p + 2], EOH[p][:, m, :], tid[:, 2 * m:2 * m + 2],
                               start=m == 0, stop=m == NT - 1)
            mm.then_inc(sem(f"tok_mm_{l}"), 1)

        def pe_rows(pe, l, n, p, landed_sem, landed_count, first):
            pe.wait_ge(sem(landed_sem), landed_count)
            for kk in range(2):
                if not first:
                    pe.wait_ge(sem(f"xt_out_{l}"), n * 2)
                for j in range(4):
                    k = 4 * kk + j
                    mm = pe.transpose(ps[:, kk, j * P:(j + 1) * P], EXG[p][:, k * P:(k + 1) * P], ident)
                mm.then_inc(sem(f"xt_mm_{l}"), 1)

        def pe_gate_up(pe, l, n, p, count, between=None):
            pe.wait_ge(sem(f"xt_out_{l}"), n * 2 + 2)
            pe.wait_ge(sem(f"wgu{p}_{l}"), count)
            for k in range(KD):
                if k == KD // 2 and between is not None:
                    between()
                mm = pe.matmul(ps[:, 2 + p, :], EXT[p][:, k, :], WGU[p][:, k, :], start=k == 0, stop=k == KD - 1)
            mm.then_inc(sem(f"gu_m_{l}"), 1)

        def pe_turn_a(pe, l, n, p):
            pe.wait_ge(sem(f"a_{l}"), n + 1)
            for k in range(2):
                mm = pe.transpose(ps[:, 4, k * P:(k + 1) * P], EA[p][:, k * P:(k + 1) * P], ident)
            mm.then_inc(sem(f"at_mm_{l}"), 1)

        def pe_down(pe, l, n, p, count, first):
            pe.wait_ge(sem(f"at_{l}"), n + 1)
            pe.wait_ge(sem(f"wd{p}_{l}"), count)
            for h in range(2):
                if not first:
                    pe.wait_ge(sem(f"y_out_{l}"), n * 2)
                for k in range(2):
                    mm = pe.matmul(ps[:, 5 + h, :], EAT[p][:, k, :], WD[p][:, k, h * 512:(h + 1) * 512],
                                   start=k == 0, stop=k == 1)
                mm.then_inc(sem(f"y_mm_{l}"), 1)

        def pe_experts(pe, l):
            pe.wait_ge(sem("shy_dve"), l * NT + NT)
            pe.wait_ge(sem("shy_act"), l * NT + NT)
            if l == 0:
                pe_filter_net(pe, 0)
            pe_rows(pe, l, 0, 0, f"xg0_{l}", 16, True)

            def pair(i, last):
                for p in range(2):
                    n, q = i * 2 + p, 1 - p
                    pe_gate_up(pe, l, n, p, i * 32 + 32, None if last else lambda: pe_token_ids(pe, l, n + 2, p))
                    if not (last and p == 1):
                        pe_rows(pe, l, n + 1, q, f"xg{q}_{l}", (i + p) * 16 + 16, False)
                    if l == 0 and isinstance(n, int) and n < 2:
                        pe_filter_net(pe, n + 1)
                    if not (isinstance(n, int) and n == 0):
                        pe_down(pe, l, n - 1, q, (i + p) * 16, isinstance(n, int) and n == 1)
                    pe_turn_a(pe, l, n, p)
            pair(0, False)
            pair(1, False)
            with pe.Fori(2, E // 2 - 1) as i:
                pair(i, False)
            pe.wait_ge(sem("tables"), l + 1)
            nov = sp_nov(pe, l)
            with pe.If(nov > 0):
                pe_token_ids(pe, l, E, 0)
            pair(E // 2 - 1, True)
            pe_down(pe, l, E - 1, 1, E // 2 * 16, False)
            with pe.If(nov > 0):
                pe_rows(pe, l, E, 0, f"xg0_{l}", 16 * (E // 2 + 1), False)

            def over(i):
                for p in range(2):
                    n, q = i * 2 + p + E, 1 - p
                    with pe.If(nov > i * 2 + p):
                        with pe.If(nov > i * 2 + p + 1):
                            pe_token_ids(pe, l, n + 1, q)
                        pe_gate_up(pe, l, n, p, i * 32 + 32 * (E // 2 + 1))
                        with pe.If(nov > i * 2 + p + 1):
                            pe_rows(pe, l, n + 1, q, f"xg{q}_{l}", (i + p) * 16 + 16 * (E // 2 + 1), False)
                        pe_turn_a(pe, l, n, p)
                        pe_down(pe, l, n, p, i * 16 + 16 * (E // 2 + 1), False)
            over_loop(pe, nov, over)

        def act_rows(act, l, n, p, wait_free):
            act.wait_ge(sem(f"xt_mm_{l}"), n * 2 + 1)
            if wait_free:
                act.wait_ge(sem(f"gu_m_{l}"), n - 1)
            act.activation(EXT[p][:, 0:4, :], ps[:, 0, :].rearrange("p (k s) -> p k s", k=4), ACT.Copy) \
                .then_inc(sem(f"xt_out_{l}"), 1)

        def act_silu(act, l, n, p):
            act.wait_ge(sem(f"gu_m_{l}"), n + 1)
            act.activation(ESG[p], ps[:, 2 + p, 0:FE], ACT.Silu).then_inc(sem(f"silu_{l}"), 1)

        def act_turned_a(act, l, n, p):
            act.wait_ge(sem(f"at_mm_{l}"), n + 1)
            act.activation(EAT[p], ps[:, 4, 0:FE].rearrange("p (k s) -> p k s", k=2), ACT.Copy) \
                .then_inc(sem(f"at_{l}"), 1)

        def act_result(act, l, n, p):
            act.wait_ge(sem(f"y_mm_{l}"), n * 2 + 1)
            act.activation(EY[p][:, 0:512], ps[:, 5, :], ACT.Copy).then_inc(sem(f"y_out_{l}"), 1)

        def act_store(act, l, n, p, b, done):
            act.wait_ge(sem(f"y_out_{l}"), n * 2 + 2)
            rows = y_dram.rearrange("(b s) d -> s b d", s=P)[:, bass.ds(b, 1), :].rearrange("s a d -> s (a d)")
            act.dma_start(rows, EY[p]).then_inc(sem(done), 16)

        def act_experts(act, l):
            act.wait_ge(sem("zeroed"), 16 * ZPARTS)
            act_rows(act, l, 0, 0, False)
            if l == 0:
                act_filter_net(act, 0)

            def result(n, q, count):
                wait(act, f"yst{q}_{l}", count)
                act_result(act, l, n, q)

            def pair(i, last):
                for p in range(2):
                    n, q = i * 2 + p, 1 - p
                    act_silu(act, l, n, p)
                    if not (last and p == 1):
                        act_rows(act, l, n + 1, q, not (isinstance(n, int) and n == 0))
                    begun = not (isinstance(n, int) and n == 0)
                    if begun:
                        result(n - 1, q, (i + p) * 16 - 16)
                    act_turned_a(act, l, n, p)
                    if begun:
                        act_store(act, l, n - 1, q, n - 1, f"yst{q}_{l}")
                    if l == 0 and isinstance(n, int) and n == 2:
                        act_filter_net(act, 1)
            pair(0, False)
            pair(1, False)
            with act.Fori(2, E // 2 - 1) as i:
                pair(i, False)
            pair(E // 2 - 1, True)
            result(E - 1, 1, E // 2 * 16 - 16)
            act_store(act, l, E - 1, 1, E - 1, f"yst1_{l}")
            act.wait_ge(sem("tables"), l + 1)
            nov = sp_nov(act, l)
            act.sem_inc(sem(f"over_stored_{l}"), 1)

            with act.If(nov > 0):
                act_rows(act, l, E, 0, False)

            def over(i):
                for p in range(2):
                    n = i * 2 + p + E
                    with act.If(nov > i * 2 + p):
                        act_silu(act, l, n, p)
                        with act.If(nov > i * 2 + p + 1):
                            act_rows(act, l, n + 1, 1 - p, False)
                        act_turned_a(act, l, n, p)
                        act.wait_ge(sem(f"yst{p}_{l}"), 16 * (E // 2))
                        act.wait_ge(sem(f"over_stored_{l}"), (i * 2 + p) * 16 + 1)
                        act_result(act, l, n, p)
                        act_store(act, l, n, p, n, f"over_stored_{l}")
            over_loop(act, nov, over)
            for p in range(2):
                act.wait_ge(sem(f"yst{p}_{l}"), 16 * (E // 2))
            act.wait_ge(sem(f"over_stored_{l}"), nov * 16 + 1)
            act.sem_inc(sem("moe_done"), 1)

        def dve_one_hot(dve, l, n, p, column, against, wait_free):
            if wait_free:
                dve.wait_ge(sem(f"tok_mm_{l}"), n - 1)
            dve.tensor_tensor(EOH[p], column.to_broadcast([P, NT, P]), against.unsqueeze(1).to_broadcast([P, NT, P]),
                              ALU.is_equal).then_inc(sem(f"oh_{l}"), 1)

        def dve_token_ids(dve, l, n, p, wait_free):
            dve.wait_ge(sem(f"tok_mm_{l}"), n + 1)
            if wait_free is not None:
                dve.wait_ge(sem(f"xg{p}_{l}"), wait_free)
            dve.tensor_scalar(TOKI[p], ps[:, 7, 2 * p:2 * p + 1], ps[:, 7, 2 * p + 1:2 * p + 2], None, ALU.add).then_inc(sem(f"tok_{l}"), 1)

        def dve_rows(dve, l, n, p, wait_free):
            dve.wait_ge(sem(f"xt_mm_{l}"), n * 2 + 2)
            if wait_free:
                dve.wait_ge(sem(f"gu_m_{l}"), n - 1)
            dve.tensor_copy(EXT[p][:, 4:8, :], ps[:, 1, :].rearrange("p (k s) -> p k s", k=4)) \
                .then_inc(sem(f"xt_out_{l}"), 1)

        def dve_product(dve, l, n, p):
            dve.wait_ge(sem(f"silu_{l}"), n + 1)
            dve.tensor_tensor(EA[p].rearrange("p (k j) -> p j k", k=2), ESG[p].rearrange("p (j k) -> p j k", k=2),
                              ps[:, 2 + p, FE:2 * FE].rearrange("p (j k) -> p j k", k=2), ALU.mult) \
                .then_inc(sem(f"a_{l}"), 1)

        def dve_result(dve, l, n, p):
            dve.wait_ge(sem(f"y_mm_{l}"), n * 2 + 2)
            dve.tensor_copy(EY[p][:, 512:1024], ps[:, 6, :]).then_inc(sem(f"y_out_{l}"), 1)

        def dve_experts(dve, v, l):
            first = K[:, C_IOTA:C_IOTA + P]
            dve_rows(dve, l, 0, 0, False)
            if l == 0:
                dve_filter_net(dve, v, 0)
            tables = {1: lambda: dve_over_table(dve, v, l), 2: lambda: dve_slot_table(dve, v, l, range(0, 2)),
                      3: lambda: dve_slot_table(dve, v, l, range(2, NT))}

            def result(n, q, count):
                wait(dve, f"yst{q}_{l}", count)
                dve_result(dve, l, n, q)

            def pair(i, last):
                for p in range(2):
                    n, q = i * 2 + p, 1 - p
                    begun = not (isinstance(n, int) and n == 0)
                    if not last:
                        dve_one_hot(dve, l, n + 2, p, POSM[:, :, bass.ds(n + 2, 1)], first, True)
                        dve_token_ids(dve, l, n + 2, p, i * 16 + 16)
                    if isinstance(n, int) and n in tables:
                        tables[n]()
                    dve_product(dve, l, n, p)
                    if not (last and p == 1):
                        dve_rows(dve, l, n + 1, q, begun)
                    if begun:
                        result(n - 1, q, (i + p) * 16 - 16)
                    if l == 0 and isinstance(n, int) and n == 0:
                        dve_filter_net(dve, v, 1)
            pair(0, False)
            pair(1, False)
            with dve.Fori(2, E // 2 - 1) as i:
                pair(i, False)
            dve.wait_ge(sem("tables"), l + 1)
            nov = sp_nov(dve, l)

            def ids(n, p, block, count):
                e = dve.value_load(OVI[0:1, bass.ds(block, 1)], min_val=0, max_val=E - 1)
                dve.wait_ge(sem(f"tok_mm_{l}"), n)
                dve.wait_ge(sem(f"next_range_{l}"), n - E + 1)
                dve_one_hot(dve, l, n, p, SLM[:, :, bass.ds(e, 1)], IOR, False)
                dve.wait_ge(sem(f"oh_{l}"), n + 1)
                dve.tensor_scalar(IOR, IOR, float(P), None, ALU.add).then_inc(sem(f"next_range_{l}"), 1)
                dve_token_ids(dve, l, n, p, count)
            with dve.If(nov > 0):
                ids(E, 0, 0, 16 * (E // 2))
            pair(E // 2 - 1, True)
            result(E - 1, 1, E // 2 * 16 - 16)

            with dve.If(nov > 0):
                dve_rows(dve, l, E, 0, False)

            def over(i):
                for p in range(2):
                    n = i * 2 + p + E
                    with dve.If(nov > i * 2 + p):
                        with dve.If(nov > i * 2 + p + 1):
                            ids(n + 1, 1 - p, i * 2 + p + 1, (i + p) * 16 + 16 * (E // 2))
                        dve_product(dve, l, n, p)
                        with dve.If(nov > i * 2 + p + 1):
                            dve_rows(dve, l, n + 1, 1 - p, False)
                        dve.wait_ge(sem(f"yst{p}_{l}"), 16 * (E // 2))
                        dve.wait_ge(sem(f"over_stored_{l}"), (i * 2 + p) * 16 + 1)
                        dve_result(dve, l, n, p)
            over_loop(dve, nov, over)

        def gather(pool, dst, table, index, bound):
            return pool.indirect_dma_start(
                out=dst, out_offset=None, in_=table,
                in_offset=bass.IndirectOffsetOnAxis(ap=index, axis=0), bounds_check=bound, oob_is_err=False)

        def pool_experts(pool, l):
            last_token, last_row = pool.to_reg(T - 1), pool.to_reg(NBLK * P - 1)
            pool.wait_ge(sem("h2_stored"), 16 * (l + 1))

            def rows(n, p, free):
                pool.wait_ge(sem(f"tok_{l}"), n + 1)
                if free is not None:
                    pool.wait_ge(sem(f"xt_mm_{l}"), free)
                pool.sem_inc(sem("rows_asked"), 1)
                gather(pool, EXG[p], h2_dram[l], TOKI[p], last_token).then_inc(sem(f"xg{p}_{l}"), 16)
            rows(0, 0, None)
            rows(1, 1, None)
            with pool.Fori(1, E // 2) as i:
                for p in range(2):
                    rows(i * 2 + p, p, i * 4 + 2 * p - 2)
            pool.wait_ge(sem("tables"), l + 1)
            nov = sp_nov(pool, l)

            def over(i):
                for p in range(2):
                    with pool.If(nov > i * 2 + p):
                        rows(i * 2 + p + E, p, i * 4 + 2 * (p + E) - 2)
            over_loop(pool, nov, over)
            pool.wait_ge(sem("moe_done"), l + 1)
            for n in range(NT * TOP_K):
                m, k = n // TOP_K, n % TOP_K
                g = l * NT * TOP_K + n
                if n >= CG:
                    pool.wait_ge(*row_used(g - CG))
                gather(pool, CGB[g % CG], y_dram, S8I[:, m, k:k + 1], last_row).then_inc(sem(f"cg{g % CG}"), 16)

        def row_used(g):
            tile, k = g // TOP_K, g % TOP_K
            if k < PK:
                return sem("cmm"), tile * PK + k + 1
            return sem("cadd"), tile * (TOP_K - PK) + k - PK + 1

        DIAG = A3(100, NT * PK, P)

        def act_diagonals(act, l):
            act.wait_ge(sem("tables"), l + 1)
            for m in range(NT):
                for k in range(PK):
                    act.activation(DIAG[:, m * PK + k, :], ident, ACT.Copy, scale=W8[:, m, k:k + 1]).then_inc(sem("score"), 1)

        def pe_combine(pe, l):
            pe.wait_ge(sem("score"), (l + 1) * (1 + NT * PK))
            pe.wait_ge(sem("moe_done"), l + 1)
            for m in range(NT):
                if m >= 2:
                    pe.wait_ge(sem("layer_start"), l * NT + m - 1)
                for k in range(PK):
                    g = (l * NT + m) * TOP_K + k
                    pe.wait_ge(sem(f"cg{g % CG}"), g // CG * 16 + 16)
                    for h in range(2):
                        mm = pe.matmul(ps[:, 2 * (m % 2) + h, :], DIAG[:, m * PK + k, :], CGB[g % CG][:, h * 512:(h + 1) * 512],
                                       start=k == 0, stop=k == PK - 1)
                    mm.then_inc(sem("cmm"), 1)

        def dve_combine(dve, v, l):
            dve.wait_ge(sem("shy_act"), l * NT + NT)
            dve.wait_ge(sem("shy_dve"), l * NT + NT)
            norm = ("n1_1", "fin")[l]
            rowA, rowB = MODR[:, D:2 * D], MODR[:, 0:D]
            if l == 0:
                dve.wait_ge(sem("bmod_in"), 64)
                dve.wait_ge(sem("norm_row_in"), 48)
                dve.scalar_tensor_tensor(rowA, rowA, 1.0, GROW, ALU.add, ALU.mult).then_inc(sem("row_used"), 1)

            def mean(m):
                dve.wait_ge(sem("sq"), before[norm] + m + 1)
                dve.tensor_scalar(ss[:, 4 + m:5 + m], ss[:, m:m + 1], 1.0 / D, EPS, ALU.mult, ALU.add).then_inc(sem("ms"), 1)

            def scaled(m):
                dve.wait_ge(sem("rt"), stats[norm] + m + 1)
                v(dve.reciprocal(ss[:, 12 + m:13 + m], ss[:, 8 + m:9 + m]))
                v.sync()
                dve.wait_ge(sem("layer_start"), l * NT + m + 1)
                r = ss[:, 12 + m:13 + m]
                if l == 1:
                    if m == 0:
                        dve.wait_ge(sem("norm_row_in"), 80)
                    dve.scalar_tensor_tensor(H[:, m, :], X[:, m, :], r, GROW, ALU.mult, ALU.mult).then_inc(sem("h"), 1)
                    return
                dve.wait_ge(sem("row_used"), NORMS.index(norm) + 1)
                if m >= 2:
                    dve.wait_ge(sem("h"), before[norm] + m - 1)
                v(dve.scalar_tensor_tensor(tmpn[m % 2], X[:, m, :], r, rowA, ALU.mult, ALU.mult))
                v.sync()
                dve.tensor_tensor(H[:, m, :].rearrange("p (k j) -> p j k", k=KD),
                                  tmpn[m % 2].rearrange("p (j k) -> p j k", k=KD),
                                  rowB.rearrange("p (j k) -> p j k", k=KD), ALU.add).then_inc(sem("h"), 1)

            for m in range(NT):
                for k in range(PK, TOP_K):
                    if m and k == PK + 1:
                        mean(m - 1)
                    if m and k == TOP_K - 1:
                        scaled(m - 1)
                    g = (l * NT + m) * TOP_K + k
                    dve.wait_ge(sem(f"cg{g % CG}"), g // CG * 16 + 16)
                    if k > PK:
                        dve.wait_ge(*row_used(g - 1))
                    dve.scalar_tensor_tensor(H[:, m, :], CGB[g % CG], W8[:, m, k:k + 1], H[:, m, :], ALU.mult, ALU.add) \
                        .then_inc(sem("cadd"), 1)
                dve.wait_ge(*row_used(g))
                dve.wait_ge(sem("cmm"), (l * NT + m + 1) * PK)
                b = 2 * (m % 2)
                v(dve.tensor_tensor(H[:, m, :].rearrange("p (h n) -> p h n", h=2), ps[:, b:b + 2, :],
                                    H[:, m, :].rearrange("p (h n) -> p h n", h=2), ALU.add))
                v.sync()
                v(dve.tensor_tensor(H[:, m, :], H[:, m, :], MODR[:, 5 * D:6 * D], ALU.mult))
                v.sync()
                dve.tensor_tensor(X[:, m, :], X[:, m, :], H[:, m, :], ALU.add).then_inc(sem("layer_start"), 1)
            mean(NT - 1)
            scaled(NT - 1)

        DFT = [A(48 + 4 * i, 2 * T) for i in range(4)]
        MC, MS = [DFT[i].rearrange("p (t f) -> p t f", t=NT) for i in range(2)]
        IC, IS = [DFT[2 + i].rearrange("p (f t) -> p f t", f=2) for i in range(2)]
        AS, BS = A3(64, 4, 512), A3(72, 4, 512)
        ZB = [A3(80 + 4 * j, 2, T) for j in range(3)]
        R1, R2 = A3(92, NT, 512), A3(100, NT, 512)
        EV = [[A(108 + 4 * f + 2 * i, 512) for i in range(2)] for f in range(2)]
        A2T = A(122, T, FILT_HID)
        HF = MODR[:, 0:2048].rearrange("p (t c) -> p t c", t=NT)
        PP = MODR[:, 0:2048].rearrange("p (a f c) -> p a f c", a=4, f=2)
        WIN = [A(124, 512), A(126, 512)]
        TP = [A3(kb, 2, CH) for kb in (8, 10, 116, 118)]
        ABX, ABT = A3(108, NT, 512), A(12, 512)
        TB = [A(24, T), A(26, T)]
        WZ = [A3(16 * j, KD, CH) for j in range(3)]
        WF = [A(40, 512, FILT_HID), A(42, 512, FILT_HID)]
        DL = [A(44, 512), A(46, 512)]
        Y2T = H[:, :, :].rearrange("p m (a t) -> p (m a) t", a=2)
        FEAT = A(86, T, FILT_EMB)
        CWR = A(92, P, 112)
        W1 = A(93, FILT_HID, FILT_EMB)
        W2 = A(93.5, FILT_HID, FILT_HID)
        FA, FN = A(80, T, FILT_HID), A(82, T, FILT_HID)
        A1T = A(84, T, FILT_HID)
        cols = sm[:, 0:112]
        fcol = sm[0:FILT_HID, 112:115]
        rl = sm[:, 120:124]
        TWO_PI = 2.0 * math.pi
        PI_HI, MAGIC = 6.28125, 12582912.0

        def sp_filter_net(sp):
            for w, src in ((FEAT, c_feats), (CWR[0:72, :], conv_w[0].rearrange("j (c p) -> (j c) p", p=P)),
                           (CWR[72:96, :], conv_b.rearrange("a (c p) -> (a c) p", p=P)),
                           (CWR[96:112, :], filt_bias[0].rearrange("o (c p) -> (o c) p", p=P)),
                           (W1, filt_w1[0]), (W2, filt_w2[0]),
                           (fcol[:, 0:1], filt_b1.rearrange("a (p b) -> p (a b)", b=1)),
                           (fcol[:, 1:2], filt_b2.rearrange("a (p b) -> p (a b)", b=1)),
                           (fcol[:, 2:3], filt_freq.rearrange("a (p b) -> p (a b)", b=1))):
                sp.dma_start(w, src).then_inc(sem("hy_in"), 16)

        def sp_hyena(sp):
            sp.wait_ge(sem("moe_done"), 1)
            sp.wait_ge(sem("cadd"), NT * (TOP_K - PK) - 2)
            def quarter(q):
                wz = w_in_c[0].rearrange("(p k) (j q c) -> p q k j c", k=KD, j=3, q=HY_Q)[:, bass.ds(q, 1), :, :, :]

                def taps(j):
                    wait(sp, "z_mm", q * 6 - 4 + 2 * j)
                    sp.dma_start(WZ[j], wz[:, :, :, j, :].rearrange("p a k c -> p (a k) c")).then_inc(sem(f"wz_in_{j}"), 16)
                taps(0)
                taps(1)
                wait(sp, "hf_mm", q * 8)
                wait(sp, "win", q * 8)
                w3 = filt_w3[0].rearrange("h (o b q c) -> h q o b c", o=2, b=2, q=HY_Q)[:, bass.ds(q, 1), :, :, :]
                dl = filt_delta.rearrange("a (o b q c) -> a q o b c", o=2, b=2, q=HY_Q)[:, bass.ds(q, 1), :, :, :]
                for o in range(2):
                    for b in range(2):
                        c = slice(b * CH, (b + 1) * CH)
                        sp.dma_start(WF[o][:, c], w3[:, :, o, b, :].rearrange("h a c -> h (a c)")).then_inc(sem("wf_in"), 16)
                        sp.dma_start(DL[o][:, c], dl[:, :, o, b, :].rearrange("a q c -> a (q c)").to_broadcast([P, CH])) \
                            .then_inc(sem("wf_in"), 16)
                taps(2)

            quarter(0)
            for i in range(4):
                sp.dma_start(DFT[i], c_dft[:, i, :]).then_inc(sem("dft_in"), 16)
            sp.wait_ge(sem("layer_start"), NT)
            sp.dma_start(MODR[:, 5 * D:6 * D], mod_dram[:, 5 * D:6 * D].to_broadcast([P, D])).then_inc(sem("bmod_in"), 16)
            with sp.Fori(1, HY_Q) as i:
                quarter(i)

        def pe_filter_net(pe, step):
            if step == 0:
                wait(pe, "hy_in", 144)
                pe.transpose(ps[:, 5, 0:112], CWR, ident[0:112, 0:112]).then_inc(sem("f_mm"), 1)
                pe.matmul(ps[0:FILT_HID, 6, :], W1, FEAT, start=True, stop=True).then_inc(sem("f_mm"), 1)
            elif step == 1:
                wait(pe, "f_sin", 1)
                pe.matmul(ps[0:FILT_HID, 6, :], W2, A1T, start=True, stop=True).then_inc(sem("f_mm"), 1)
            else:
                wait(pe, "f_arg", 3)

        def act_filter_net(act, i):
            wait(act, "f_arg", i + 2)
            if i:
                wait(act, "next_range_0", 1)
            act.activation((A1T, A2T)[i], FA, ACT.Sin).then_inc(sem("f_sin"), 1)

        def dve_filter_net(dve, v, i):
            if i == 0:
                wait(dve, "hy_in", 144)
                wait(dve, "f_mm", 1)
                dve.tensor_copy(cols, ps[:, 5, 0:112]).then_inc(sem("f_arg"), 1)
            wait(dve, "f_mm", i + 2)
            if i:
                wait(dve, "f_sin", i)
            v(dve.tensor_scalar(FA, ps[0:FILT_HID, 6, :], fcol[:, i:i + 1], fcol[:, 2:3], ALU.add, ALU.mult))
            v.sync()
            v(dve.tensor_scalar(FN, FA, 1.0 / TWO_PI, MAGIC, ALU.mult, ALU.add))
            v.sync()
            v(dve.tensor_scalar(FN, FN, -MAGIC, None, ALU.add))
            v.sync()
            for part in (PI_HI, TWO_PI - PI_HI):
                v(dve.scalar_tensor_tensor(FA, FN, -part, FA, ALU.mult, ALU.add))
                v.sync()
            top = float(np.nextafter(np.float32(math.pi), np.float32(0)))
            dve.tensor_scalar(FA, FA, top, -top, ALU.min, ALU.max).then_inc(sem("f_arg"), 1)

        ZBANK = (0, 1, 2, 6, 4, 6)

        def pe_hyena(pe):
            def project(q, t):
                j, ct = t // 2, t % 2
                wait(pe, f"wz_in_{j}", q * 16 + 16)
                for k in range(KD):
                    mm = pe.matmul(ps[:, ZBANK[t], :], WZ[j][:, k, ct * P:(ct + 1) * P], HT[:, k, :],
                                   start=k == 0, stop=k == KD - 1)
                mm.then_inc(sem("z_mm"), 1)

            wait(pe, "f_sin", 2)
            wait(pe, "turned", 2 * before["n2_1"])
            def quarter(q):
                for o in range(2):
                    u = q * 2 + o
                    wait(pe, "wf_in", q * 128 + 128)
                    wait(pe, "ky_act", u * 4)
                    wait(pe, "ky_dve", u * 4)
                    for t in range(NT):
                        pe.matmul(ps[:, t, :], A2T[:, t * P:(t + 1) * P], WF[o], start=True, stop=True) \
                            .then_inc(sem("hf_mm"), 1)
                    if o == 0:
                        for t in range(3):
                            wait(pe, "hfw", u * 5 + t + 1)
                            project(q, t)
                        wait(pe, "z_dve", q * 6 + 2)
                        wait(pe, "z_dve", q * 6)
                    else:
                        wait(pe, "z_dve", q * 6 + 4)
                        wait(pe, "yn", q * 4 + 2)
                    wait(pe, "yt_act", u * 2)
                    wait(pe, "rl1", u)
                    for b in range(2):
                        for t in range(2 * b, 2 * b + 2):
                            for ct in range(2):
                                at = (t % 2) * CH + ct * P
                                pos = (t % 2) * CH + b
                                mm = pe.transpose(ps[:, 6 + b, at:at + P], ZB[0][:, ct, pos:pos + 2 * P - 1:2], ident)
                        mm.then_inc(sem("yt_mm"), 1)
                    if o == 1:
                        project(q, 4)
                    wait(pe, "dft_in", 64)
                    wait(pe, "sd", u * 2 + 2)
                    wait(pe, "yt_dup", u + 1)
                    if o == 0:
                        wait(pe, "z_dve", q * 6 + 3)
                    else:
                        wait(pe, "hfw", u * 5 + 5)
                    for f in range(2):
                        seen = u * 4 + 2 * f
                        for i, (table, data) in enumerate(((MC, R1), (MS, R2))):
                            for odd in range(2):
                                wait(pe, "ky_dve" if odd else "ky_act", seen + i - 1)
                                for t in range(2 * odd, 2 * odd + 2):
                                    mm = pe.matmul(ps[:, 2 * i + odd, :], table[:, t, f * P:(f + 1) * P], data[:, t, :],
                                                   start=t % 2 == 0, stop=t % 2 == 1)
                                mm.then_inc(sem("ky_mm"), 1)
                    wait(pe, "yt_act", u * 2 + 2)
                    project(q, 3 + 2 * o)
                    wait(pe, "l1sum", u + 1)
                    for ct in range(2):
                        for b in range(2):
                            mm = pe.matmul(ps[:, 7, ct:ct + 1], ABT[:, b * CH + ct * P:b * CH + (ct + 1) * P], ones[:, 0:1],
                                           start=b == 0, stop=b == 1)
                    mm.then_inc(sem("l1_mm"), 1)
                    wait(pe, "pp", u * 2 + 2)
                    wait(pe, "yn", u * 2)
                    if o == 1:
                        wait(pe, "z_dve", q * 6 + 5)
                    for ct in range(2):
                        for odd in range(2):
                            for i, table in enumerate((IC, IS)):
                                for f in range(2):
                                    mm = pe.matmul(ps[:, 4 + ct, odd * CH:(odd + 1) * CH],
                                                   PP[:, 2 * odd + i, f, ct * P:(ct + 1) * P],
                                                   table[:, f, odd * CH:(odd + 1) * CH], start=i + f == 0, stop=i + f == 2)
                        mm.then_inc(sem("iv_mm"), 1)

            quarter(0)
            with pe.Fori(1, HY_Q) as i:
                quarter(i)

        def act_hyena(act):
            def middle(q, t):
                j, ct = t // 2, t % 2
                wait(act, "z_mm", q * 6 + t + 1)
                act.activation(ZB[j][:, ct, :], ps[:, ZBANK[t], :], ACT.Identity,
                               bias=col(72 + j * 8 + ct, q), scale=col(24 + j * 8 + ct, q)).then_inc(sem("z_act"), 1)

            wait(act, "f_arg", 1)
            def quarter(q):
                for o in range(2):
                    u = q * 2 + o
                    wait(act, "wf_in", q * 128 + 128)
                    act.activation(DL[o], DL[o], ACT.Abs).then_inc(sem("act_chain"), 1)
                    wait(act, "act_chain", u + 33)
                    for t in range(NT):
                        wait(act, "hfw", u * 5 + max(t - 1, 0))
                        act.activation(WIN[t % 2], DL[o], ACT.Exp, scale=K[:, C_T01 + t:C_T01 + t + 1]).then_inc(sem("win"), 1)
                    if o == 0:
                        wait(act, "yn", q * 4)
                        wait(act, "iv_act", q * 4)
                        for t in range(3):
                            middle(q, t)
                    wait(act, "ky_mm", u * 8)
                    wait(act, "yt_dup", u)
                    for b in range(2):
                        wait(act, "yt_mm", u * 2 + b + 1)
                        act.activation(R1[:, 2 * b:2 * b + 2, CH:2 * CH], ps[:, 6 + b, :].rearrange("p (t c) -> p t c", t=2), ACT.Copy) \
                            .then_inc(sem("yt_act"), 1)
                    if o == 1:
                        middle(q, 4)
                    wait(act, "l1sum", u + 1)
                    for f in range(2):
                        for i in range(2):
                            wait(act, "ky_dve", u * 4 + 2 * f - 3 + i)
                            wait(act, "ky_mm", u * 8 + 4 * f + 2 * i + 1)
                            act.activation(EV[f][i], ps[:, 2 * i, :], ACT.Copy).then_inc(sem("ky_act"), 1)
                    middle(q, 3 + 2 * o)
                    wait(act, "yn", u * 2)
                    for ct in range(2):
                        act.activation(TB[ct], ZB[0][:, ct, :], ACT.Copy, scale=col(96 + o * 8 + ct, q)).then_inc(sem("iv_act"), 1)

            quarter(0)
            with act.Fori(1, HY_Q) as i:
                quarter(i)

        def col(base, q):
            return cols[:, bass.ds(q * 2 + base, 1)]

        def dve_hyena(dve, v):
            def outer(q, t):
                j, ct = t // 2, t % 2
                z = ZB[j][:, ct, :]
                wait(dve, "z_act", q * 6 + t + 1)
                v(dve.scalar_tensor_tensor(z[:, 1:T], ps[:, ZBANK[t], 0:T - 1], col(j * 8 + ct, q), z[:, 1:T],
                                           ALU.mult, ALU.add))
                v.sync()
                dve.scalar_tensor_tensor(z[:, 0:T - 1], ps[:, ZBANK[t], 1:T], col(48 + j * 8 + ct, q), z[:, 0:T - 1],
                                         ALU.mult, ALU.add).then_inc(sem("z_dve"), 1)

            def double(u):
                wait(dve, "yt_act", u * 2 + 2)
                dve.tensor_copy(R2[:, :, CH:2 * CH], R1[:, :, CH:2 * CH]).then_inc(sem("yt_dup"), 1)

            wait(dve, "f_arg", 1)
            def quarter(q):
                for o in range(2):
                    u = q * 2 + o
                    wait(dve, "iv_mm", u * 2)
                    for t in range(NT):
                        wait(dve, "hf_mm", u * 4 + t + 1)
                        wait(dve, "win", u * 4 + t + 1)
                        dve.scalar_tensor_tensor(HF[:, t, :], WIN[t % 2], DECAY_SHIFT, ps[:, t, :], ALU.add, ALU.mult) \
                            .then_inc(sem("hfw"), 1)
                    wait(dve, "hfw", u * 5 + 4)
                    wait(dve, "sd", u * 2)
                    dve.memset(HF[0:1, 0, CH:2 * CH], 0.0).then_inc(sem("hfw"), 1)
                    wait(dve, "hfw", u * 5 + 5)
                    wait(dve, "ky_mm", u * 8)
                    dve.tensor_tensor(R2[:, :, 0:CH], HF[:, :, 0:CH], HF[:, :, CH:2 * CH], ALU.subtract).then_inc(sem("sd"), 1)
                    if o == 1:
                        double(u)
                    wait(dve, "l1_mm", u)
                    wait(dve, "pp", u * 2)
                    v(dve.scalar_tensor_tensor(ABX, HF, -1.0, HF, ALU.mult, ALU.max))
                    v.sync()
                    dve.tensor_reduce(ABT, ABX.rearrange("p t c -> p c t"), AX, ALU.add).then_inc(sem("l1sum"), 1)
                    if o == 0:
                        for t in range(3):
                            outer(q, t)
                        double(u)
                    else:
                        outer(q, 4)
                    wait(dve, "sd", u * 2 + 2)
                    for f in range(2):
                        for i, sums in enumerate((AS, BS)):
                            wait(dve, "ky_act", u * 4 + 2 * f + i + 1)
                            wait(dve, "ky_mm", u * 8 + 4 * f + 2 * i + 2)
                            even, odd = EV[f][i], ps[:, 2 * i + 1, :]
                            v.sync()
                            v(dve.tensor_tensor(sums[:, 2 * f, :], even, odd, ALU.add))
                            first, second = (even, odd) if i == 0 else (odd, even)
                            dve.tensor_tensor(sums[:, 2 * f + 1, :], first, second, ALU.subtract).then_inc(sem("ky_dve"), 1)
                        wait(dve, "ky_dve", u * 4 + 2 * f + 2)
                        v.sync()
                        ah, ay = AS[:, 2 * f:2 * f + 2, 0:CH], AS[:, 2 * f:2 * f + 2, CH:]
                        bh, by = BS[:, 2 * f:2 * f + 2, 0:CH], BS[:, 2 * f:2 * f + 2, CH:]
                        for i, (x0, x1) in enumerate(((ah, ay), (bh, by), (ah, by), (bh, ay))):
                            v(dve.tensor_tensor(TP[i], x0, x1, ALU.mult))
                        v.sync()
                        v(dve.tensor_tensor(TP[0], TP[0], TP[1], ALU.subtract))
                        v(dve.tensor_tensor(TP[2], TP[2], TP[3], ALU.add))
                        v.sync()
                        v(dve.tensor_tensor(PP[:, 0, f, :], TP[0][:, 0, :], TP[0][:, 1, :], ALU.add))
                        v(dve.tensor_tensor(PP[:, 1, f, :], TP[2][:, 0, :], TP[2][:, 1, :], ALU.subtract))
                        v(dve.tensor_tensor(PP[:, 2, f, :], TP[0][:, 0, :], TP[0][:, 1, :], ALU.subtract))
                        dve.tensor_tensor(PP[:, 3, f, :], TP[2][:, 0, :], TP[2][:, 1, :], ALU.add).then_inc(sem("pp"), 1)
                    outer(q, 3 + 2 * o)
                    wait(dve, "l1_mm", u + 1)
                    wait(dve, "yn", u * 2)
                    dve.reciprocal(rl[:, 2 * o:2 * o + 2], ps[:, 7, 0:2]).then_inc(sem("rl1"), 1)
                    wait(dve, "rl1", u + 1)
                    for ct in range(2):
                        wait(dve, "iv_mm", u * 2 + ct + 1)
                        wait(dve, "iv_act", u * 2 + ct + 1)
                        split = TB[ct].rearrange("p (i odd) -> p odd i", odd=2)
                        v(dve.scalar_tensor_tensor(split, ps[:, 4 + ct, :].rearrange("p (odd i) -> p odd i", odd=2),
                                                   rl[:, 2 * o + ct:2 * o + ct + 1], split, ALU.mult, ALU.add))
                        v.sync()
                        dst = ZB[0][:, ct, :] if o == 0 else Y2T[:, bass.ds(q * 2 + ct, 1), :].rearrange("p a t -> p (a t)")
                        dve.tensor_tensor(dst, TB[ct], ZB[1 + o][:, ct, :], ALU.mult).then_inc(sem("yn"), 1)

            quarter(0)
            with dve.Fori(1, HY_Q) as i:
                v.enter(i - 1, 6 + 2 * (1 + 2 * 11 + 2))
                quarter(i)
            v.leave(HY_Q - 1)

        def pool_hyena(pool):
            def quarter(q):
                for o in range(2):
                    u = q * 2 + o
                    wait(pool, "hfw", u * 5 + 5)
                    wait(pool, "ky_mm", u * 8)
                    pool.tensor_tensor(R1[:, :, 0:CH], HF[:, :, 0:CH], HF[:, :, CH:2 * CH], ALU.add).then_inc(sem("sd"), 1)

            quarter(0)
            with pool.Fori(1, HY_Q) as i:
                quarter(i)
        def sp_moe(sp, l):
            if l == 0:
                sp.wait_ge(sem("o_dve"), 32)
            sp.dma_start(GROW, norm_g[l, 1:2, :].to_broadcast([P, D])).then_inc(sem("norm_row_in"), 16)
            sp_router(sp, l)
            sp_dense(sp, W_SH[l][0])
            sp_dense(sp, W_SH[l][1])
            sp.wait_ge(sem("h"), before[f"n2_{l}"] + NT)
            sp.dma_start(h2_dram[l].rearrange("(m p) d -> p m d", p=P), TM[l][:, :, :]).then_inc(sem("h2_stored"), 16)
            if l == 0:
                sp.wait_ge(sem("mod_stored"), 16)
                sp.dma_start(MODR[:, 0:5 * D], mod_dram[:, 0:5 * D].to_broadcast([P, 5 * D])).then_inc(sem("bmod_in"), 16)
                sp.dma_start(GROW, norm_g[1, 0:1, :].to_broadcast([P, D])).then_inc(sem("norm_row_in"), 16)
            sp_experts(sp, l)

        def act_moe(act, l):
            act_out(act, l)
            act_router(act, l)
            act.wait_ge(sem("h2_stored"), 16 * (l + 1))
            act_shared(act, l)
            act_experts(act, l)
            act_diagonals(act, l)

        def pe_moe(pe, l):
            pe_shared(pe, l, range(0, 2))
            pe_positions(pe, l)
            pe_shared(pe, l, range(2, NT))
            pe.wait_ge(sem("consts_made"), 2)
            pe_token_ids(pe, l, 0, 0)
            pe_token_ids(pe, l, 1, 1)
            pe_shared(pe, l, None)
            pe_experts(pe, l)
            pe_combine(pe, l)

        def dve_moe(dve, v, l):
            dve_select(dve, v, l)
            dve.wait_ge(sem("slots"), l + 1)
            dve_one_hot(dve, l, 0, 0, POSM[:, :, 0:1], K[:, C_IOTA:C_IOTA + P], False)
            dve_one_hot(dve, l, 1, 1, POSM[:, :, 1:2], K[:, C_IOTA:C_IOTA + P], False)
            dve_shared(dve, l, range(0, 2))
            dve_token_ids(dve, l, 0, 0, None)
            dve_token_ids(dve, l, 1, 1, None)
            dve_shared(dve, l, range(2, NT))
            dve.wait_ge(sem("sha"), l * NT + NT)
            dve.wait_ge(sem("h2_stored"), 16 * (l + 1))
            dve_shared(dve, l, None)
            dve_experts(dve, v, l)
            dve_combine(dve, v, l)

        @block.sync
        def _(sp):
            sp_setup(sp)
            for n in range(3, W_MOD[1][0]):
                sp_dense(sp, n)
                if n == 5:
                    sp_layer0(sp)
                if n == W_U:
                    sp.wait_ge(sem("h"), before["n2_0"])
                    sp.dma_start(WSR, w_spatial[0].rearrange("g i j -> i g j")).then_inc(sem("ws_in"), 16)
            for n in W_MOD[1][:3]:
                sp_dense(sp, n)
            sp.wait_ge(sem("sg_done"), SG_G)
            sp.dma_start(BROW, b_mod[1:2, :]).then_inc(sem("bmod_in"), 16)
            for i, n in enumerate(W_MOD[1][3:]):
                sp_dense(sp, n)
                if i < ZPARTS:
                    sp_zero_rows(sp, i)
            for n in W_OUT[0]:
                sp_dense(sp, n)
            sp.wait_ge(sem("mod_add"), 28)
            sp.dma_start(mod_dram, BROW).then_inc(sem("mod_stored"), 16)
            sp_moe(sp, 0)
            sp_hyena(sp)
            sp.wait_ge(sem("z_mm"), 6 * HY_Q)
            sp.wait_ge(sem("hf_mm"), 8 * HY_Q)
            sp.wait_ge(sem("win"), 8 * HY_Q)
            sp_dense(sp, W_OUT[1][0])
            sp.wait_ge(sem("yn"), 4 * HY_Q)
            sp_dense(sp, W_OUT[1][1])
            sp_moe(sp, 1)
            sp.wait_ge(sem("h"), before["fin"])
            sp.dma_start(GROW, final_g.rearrange("(a d) -> a d", a=1).to_broadcast([P, D])).then_inc(sem("norm_row_in"), 16)
            for m in range(NT):
                sp.wait_ge(sem("h"), before["fin"] + m + 1)
                sp.dma_start(out[0].rearrange("(m p) d -> p m d", p=P)[:, m, :], H[:, m, :]).then_inc(sem("out_stored"), 16)
            sp.wait_ge(sem("out_stored"), 16 * NT)

        @block.scalar
        def _(act):
            act_setup(act)
            act_mod(act)
            act.wait_ge(sem("x_in"), 32)
            act_norm_sq(act, "n1_0", X, NT, tmpn)
            act_norm_sq(act, "nc_0", CX, NC, [A(104, D), A(108, D)])
            turned(act, lambda o, i: act.activation(o, i, ACT.Copy), HT, "tp", "turned", NT, 0, "n1_0")
            turned(act, lambda o, i: act.activation(o, i, ACT.Copy), HCT, "tp", "turned", NC, 0, "nc_0")
            act_project(act)
            act_spatial(act)
            act_attention(act)
            act.wait_ge(sem("zeroed"), 16 * ZPARTS)
            turned(act, lambda o, i: act.activation(o, i, ACT.Copy), HT, "mt_tp", "mt_turned", NT, 0)
            act_moe(act, 0)
            act_combine(act, 0)
            turned(act, lambda o, i: act.activation(o, i, ACT.Copy), HT, "tp", "turned", NT, 0, "n1_1")
            act_hyena(act)
            act_moe(act, 1)
            act_combine(act, 1)

        @block.tensor
        def _(pe):
            pe.wait_ge(sem("consts_in"), 48)
            pe_mod(pe)
            pe.wait_ge(sem("mod_add"), 16)
            pe_turn(pe, H, "tp", NT, norm="n1_0")
            pe.wait_ge(sem("turned"), 2 * NT)
            pe_turn(pe, HC, "tp", NC, norm="nc_0")
            pe_project(pe)
            pe_turn_qk(pe)
            pe_spatial(pe)
            pe_attention(pe)
            pe.wait_ge(sem("o_dve"), 32)
            pe_turn(pe, MIX, "mt_tp", NT, strided=True)
            pe_out(pe, 0, HT)
            pe_moe(pe, 0)
            pe.wait_ge(sem("layer_start"), NT)
            pe_turn(pe, H, "tp", NT, norm="n1_1")
            pe_hyena(pe)
            pe_out(pe, 1, Y2T)
            pe_moe(pe, 1)

        @block.vector
        def _(dve):
            v = Chain(dve, sem("dve_chain"))
            dve_setup(dve)
            dve_cond(dve)
            dve_mod(dve, range(8))
            dve.wait_ge(sem("norm_row_in"), 16)
            dve_norm(dve, v, "n1_0", X, NT, MODR[:, D:2 * D], MODR[:, 0:D], H, GROW, tmpn)
            dve_norm(dve, v, "nc_0", CX, NC, MODC[:, D:2 * D], MODC[:, 0:D], HC, GROW, tmpn)
            dve_mod(dve, range(8, len(MOD_0)))
            turned(dve, dve.tensor_copy, HT, "tp", "turned", NT, 1, "n1_0")
            turned(dve, dve.tensor_copy, HCT, "tp", "turned", NC, 1, "nc_0")
            dve_project(dve, v)
            dve_gate_norm(dve, v)
            dve_turn_qk(dve)
            dve_spatial(dve)
            dve_attention(dve, v)
            dve.wait_ge(sem("zeroed"), 16 * ZPARTS)
            turned(dve, dve.tensor_copy, HT, "mt_tp", "mt_turned", NT, 1)
            dve_out(dve, v, 0, G2T)
            dve_moe(dve, v, 0)
            turned(dve, dve.tensor_copy, HT, "tp", "turned", NT, 1, "n1_1")
            dve_hyena(dve, v)
            dve_out(dve, v, 1, G2T)
            dve_moe(dve, v, 1)

        @block.gpsimd
        def _(pool):
            pool.wait_ge(sem("gu_mm"), 2 * NT)
            pool.memset(ZERO, 0.0).then_inc(sem("zero_ready"), 1)
            pool_experts(pool, 0)
            pool_hyena(pool)
            pool_experts(pool, 1)


_INS = ["x", "c", "ctx", "c_ctx", "w_mod", "b_mod", "norm_g", "w_in_ab", "sink", "w_spatial", "b_spatial", "w_out_ab",
        "w_in_c", "conv_w", "conv_b", "filt_w1", "filt_b1", "filt_w2", "filt_b2", "filt_w3", "filt_freq", "filt_delta",
        "filt_bias", "w_out_c", "w_router", "e_bias", "w_gate", "w_up", "w_down", "ws_gate", "ws_up", "ws_down", "final_g"]


def kernel(**inputs):
    import concourse.bacc as _bacc
    from concourse.bass_utils import run_bass_kernel_spmd as _run

    nc = _bacc.Bacc("TRN2", target_bir_lowering=False, num_devices=1)
    arrays, args = {}, []
    for name, a in list({n: inputs[n] for n in _INS}.items()) + list(constants().items()):
        a = np.ascontiguousarray(a)
        arrays[f"in_{name}"] = a
        args.append(nc.dram_tensor(f"in_{name}", a.shape, mybir.dt.from_np(a.dtype), kind="ExternalInput").ap())
    args.append(nc.dram_tensor("out_0", (1, T, D), F32, kind="ExternalOutput").ap())
    hybrid_backbone(nc, *args)
    r = _run(nc, [arrays], core_ids=[0])
    return r.results[0]["out_0"]
```
